# Optimizing a Trainium2 kernel written in Bass

```python
import math
import jax, jax.numpy as jnp
from jax import lax
import numpy as np

D_MODEL = 1024
BATCH = 1
SEQ = 256
DEPTH = 2

N_A_LAYERS = DEPTH // 2
N_B_LAYERS = DEPTH - N_A_LAYERS

MLSTM_HEADS = 4
MLSTM_INNER = 2 * D_MODEL
MLSTM_HEAD_DIM = MLSTM_INNER // MLSTM_HEADS
CONV_WIDTH = 4
MLSTM_CHUNK = 128

ATTN_HEADS = 16
ATTN_HEAD_DIM = D_MODEL // ATTN_HEADS
MOBA_BLOCK = 256
MOBA_TOPK = 3
MOBA_QCHUNK = 32

N_EXPERTS = 16
N_GROUPS = 4
EXPERTS_PER_GROUP = N_EXPERTS // N_GROUPS
MOE_TOPK = 2
D_FF_EXPERT = 512
MOE_ROW_BLOCK = 256

DEEPNORM_ALPHA = (2.0 * DEPTH) ** 0.25
DEEPNORM_BETA = (8.0 * DEPTH) ** -0.25
LN_EPS = 1e-5
N_MOD_PER_LAYER = 6


def layer_norm(x, g, b):
    xf = x.astype(jnp.float32)
    mu = xf.mean(-1, keepdims=True)
    var = jnp.square(xf - mu).mean(-1, keepdims=True)
    return ((xf - mu) * lax.rsqrt(var + LN_EPS) * g + b).astype(x.dtype)

def modulate(x, shift, scale):
    return x * (1 + scale[:, None, :]) + shift[:, None, :]

def causal_conv(x, w, b):
    K, C = w.shape
    y = lax.conv_general_dilated(x, w[:, None, :], window_strides=(1,), padding=[(K - 1, 0)],
                                 dimension_numbers=('NWC', 'WIO', 'NWC'), feature_group_count=C)
    return y + b

def mlstm_chunkwise(q, k, v, log_i, log_f):
    B, H, S, Dh = q.shape
    L = MLSTM_CHUNK
    nc = S // L

    def to_chunks(t):
        return jnp.moveaxis(t.reshape(t.shape[:2] + (nc, L) + t.shape[3:]), 2, 0)

    causal = jnp.tril(jnp.ones((L, L), bool))

    def step(carry, inp):
        C, n, m = carry
        qc, kc, vc, ic, fc = inp
        b = jnp.cumsum(fc, axis=-1)
        d = jnp.where(causal, b[..., :, None] - b[..., None, :] + ic[..., None, :], -jnp.inf)
        a = b + m[..., None]
        m_t = jnp.maximum(a, d.max(-1))
        w_intra = jnp.exp(d - m_t[..., None])
        w_inter = jnp.exp(a - m_t)
        s = jnp.einsum('bhtd,bhsd->bhts', qc, kc) * w_intra
        num = jnp.einsum('bhts,bhsd->bhtd', s, vc) + w_inter[..., None] * jnp.einsum('bhvd,bhtd->bhtv', C, qc)
        den = s.sum(-1) + w_inter * jnp.einsum('bhd,bhtd->bht', n, qc)
        h = num / jnp.maximum(jnp.abs(den), jnp.exp(-m_t))[..., None]
        b_last = b[..., -1]
        w_s = b_last[..., None] - b + ic
        m_new = jnp.maximum(b_last + m, w_s.max(-1))
        decay = jnp.exp(b_last + m - m_new)
        w_s = jnp.exp(w_s - m_new[..., None])
        C_new = decay[..., None, None] * C + jnp.einsum('bhs,bhsv,bhsd->bhvd', w_s, vc, kc)
        n_new = decay[..., None] * n + jnp.einsum('bhs,bhsd->bhd', w_s, kc)
        return (C_new, n_new, m_new), h

    init = (jnp.zeros((B, H, Dh, Dh), jnp.float32), jnp.zeros((B, H, Dh), jnp.float32),
            jnp.zeros((B, H), jnp.float32))
    _, hs = lax.scan(step, init, (to_chunks(q), to_chunks(k), to_chunks(v), to_chunks(log_i), to_chunks(log_f)))
    return jnp.moveaxis(hs, 0, 2).reshape(B, H, S, Dh)

def mlstm_layer(h, w_in, conv_w, conv_b, wq, wk, wv, w_if, b_if, gn_g, skip, w_out):
    B, S, _ = h.shape
    NH, DH = MLSTM_HEADS, MLSTM_HEAD_DIM
    f32 = jnp.float32
    xm, z = jnp.split(h @ w_in, 2, axis=-1)
    xc = jax.nn.silu(causal_conv(xm, conv_w, conv_b))
    xc_h = xc.reshape(B, S, NH, DH)
    xm_h = xm.reshape(B, S, NH, DH)
    q = jnp.einsum('bshd,hde->bhse', xc_h, wq).astype(f32)
    k = (jnp.einsum('bshd,hde->bhse', xc_h, wk) * (DH ** -0.5)).astype(f32)
    v = jnp.einsum('bshd,hde->bhse', xm_h, wv).astype(f32)
    gates = jnp.transpose((xc @ w_if + b_if).astype(f32), (0, 2, 1))
    log_i = gates[:, :NH]
    log_f = jax.nn.log_sigmoid(gates[:, NH:])
    hh = mlstm_chunkwise(q, k, v, log_i, log_f)
    mu = hh.mean(-1, keepdims=True)
    var = jnp.square(hh - mu).mean(-1, keepdims=True)
    hh = (hh - mu) * lax.rsqrt(var + LN_EPS)
    hh = hh.transpose(0, 2, 1, 3).reshape(B, S, MLSTM_INNER).astype(h.dtype) * gn_g
    hh = (hh + skip * xc) * jax.nn.silu(z)
    return hh @ w_out

def shared_kv(x, shift, scale, w_kv):
    B, S, D = x.shape
    k, v = jnp.split(modulate(x, shift, scale) @ w_kv, 2, axis=-1)
    s_pad = -(-S // MOBA_BLOCK) * MOBA_BLOCK
    nblk = s_pad // MOBA_BLOCK

    def to_blocks(t):
        t = t.reshape(B, S, ATTN_HEADS, ATTN_HEAD_DIM).transpose(0, 2, 1, 3)
        t = jnp.pad(t, ((0, 0), (0, 0), (0, s_pad - S), (0, 0)))
        return t.reshape(B, ATTN_HEADS, nblk, MOBA_BLOCK, ATTN_HEAD_DIM)

    k_blocks, v_blocks = to_blocks(k), to_blocks(v)
    k_means = k_blocks.astype(jnp.float32).mean(3).astype(k.dtype)
    return k_blocks, v_blocks, k_means

def alibi_slopes(n_heads):
    return jnp.exp2(-8.0 * (jnp.arange(n_heads, dtype=jnp.float32) + 1.0) / n_heads)

def moba_attention(q, k_blocks, v_blocks, k_means, slopes):
    B, H, S, Dh = q.shape
    nblk = k_blocks.shape[2]
    topk = min(MOBA_TOPK, nblk)
    QC, BLK = MOBA_QCHUNK, MOBA_BLOCK
    nq = S // QC
    q_chunks = jnp.moveaxis(q.reshape(B, H, nq, QC, Dh), 2, 0)
    bi = jnp.arange(B)[:, None, None, None]
    hi = jnp.arange(H)[None, :, None, None]
    blk_ids = jnp.arange(nblk)
    offs = jnp.arange(BLK)
    f32 = jnp.float32

    def one_chunk(args):
        ci, qc = args
        t = ci * QC + jnp.arange(QC)
        own = (ci * QC) // BLK
        gate = jnp.einsum('bhtd,bhnd->bhtn', qc, k_means).astype(f32)
        gate = jnp.where(blk_ids < own, gate, -jnp.inf)
        _, sel = lax.top_k(gate, topk)
        valid = sel < own
        k_sel = k_blocks[bi, hi, sel]
        v_sel = v_blocks[bi, hi, sel].reshape(B, H, QC, topk * BLK, Dh)
        s_sel = jnp.einsum('bhtd,bhtjsd->bhtjs', qc, k_sel).astype(f32)
        pos_sel = sel[..., None] * BLK + offs
        dist_sel = (t[:, None, None] - pos_sel).astype(f32)
        s_sel = s_sel - slopes[:, None, None, None] * dist_sel
        s_sel = jnp.where(valid[..., None], s_sel, -jnp.inf).reshape(B, H, QC, topk * BLK)
        k_own = lax.dynamic_index_in_dim(k_blocks, own, axis=2, keepdims=False)
        v_own = lax.dynamic_index_in_dim(v_blocks, own, axis=2, keepdims=False)
        s_own = jnp.einsum('bhtd,bhsd->bhts', qc, k_own).astype(f32)
        pos_own = own * BLK + offs
        dist_own = (t[:, None] - pos_own[None, :]).astype(f32)
        s_own = jnp.where(dist_own >= 0, s_own - slopes[:, None, None] * dist_own, -jnp.inf)
        p = jax.nn.softmax(jnp.concatenate([s_sel, s_own], axis=-1), axis=-1).astype(v_blocks.dtype)
        return (jnp.einsum('bhts,bhtsd->bhtd', p[..., :topk * BLK], v_sel)
                + jnp.einsum('bhts,bhsd->bhtd', p[..., topk * BLK:], v_own))

    outs = lax.map(one_chunk, (jnp.arange(nq), q_chunks))
    return jnp.moveaxis(outs, 0, 2).reshape(B, H, S, Dh)

def moba_layer(h, wq, wo, k_blocks, v_blocks, k_means, slopes):
    B, S, D = h.shape
    q = (h @ wq).reshape(B, S, ATTN_HEADS, ATTN_HEAD_DIM).transpose(0, 2, 1, 3) * (ATTN_HEAD_DIM ** -0.5)
    o = moba_attention(q, k_blocks, v_blocks, k_means, slopes)
    return o.transpose(0, 2, 1, 3).reshape(B, S, D) @ wo

def route(x2, w_router, b_router):
    T = x2.shape[0]
    probs = jax.nn.softmax((x2 @ w_router).astype(jnp.float32), axis=-1)
    sel_scores = (probs + b_router).reshape(T, N_GROUPS, EXPERTS_PER_GROUP)
    grp_score = lax.top_k(sel_scores, MOE_TOPK)[0].sum(-1)
    g = jnp.argmax(grp_score, axis=-1)
    masked = jnp.where(jnp.arange(N_GROUPS)[None, :, None] == g[:, None, None], sel_scores, -jnp.inf)
    _, idx = lax.top_k(masked.reshape(T, N_EXPERTS), MOE_TOPK)
    w = jnp.take_along_axis(probs, idx, axis=-1)
    return idx, w / w.sum(-1, keepdims=True)

def moe_ffn(h, w_router, b_router, w_gate, w_up, w_down):
    B, S, D = h.shape
    T = B * S
    x2 = h.reshape(T, D)
    idx, wts = route(x2, w_router, b_router)
    n_assign = T * MOE_TOPK
    e_flat = idx.reshape(-1)
    tok_flat = jnp.repeat(jnp.arange(T, dtype=jnp.int32), MOE_TOPK)
    w_flat = wts.reshape(-1)
    order = jnp.argsort(e_flat)
    e_sorted = e_flat[order]
    counts = jnp.zeros((N_EXPERTS,), jnp.int32).at[e_flat].add(1)
    starts = jnp.cumsum(counts) - counts
    padded = (counts + MOE_ROW_BLOCK - 1) // MOE_ROW_BLOCK * MOE_ROW_BLOCK
    pends = jnp.cumsum(padded)
    pstarts = pends - padded
    dest = pstarts[e_sorted] + (jnp.arange(n_assign, dtype=jnp.int32) - starts[e_sorted])
    n_blocks = -(-n_assign // MOE_ROW_BLOCK) + N_EXPERTS
    cap = n_blocks * MOE_ROW_BLOCK
    buf_tok = jnp.zeros((cap,), jnp.int32).at[dest].set(tok_flat[order])
    buf_w = jnp.zeros((cap,), jnp.float32).at[dest].set(w_flat[order])
    block_start = jnp.arange(n_blocks, dtype=jnp.int32) * MOE_ROW_BLOCK
    block_expert = jnp.minimum(jnp.searchsorted(pends, block_start, side='right'), N_EXPERTS - 1)
    xs = x2[buf_tok].reshape(n_blocks, MOE_ROW_BLOCK, D)

    def expert_block(args):
        xb, e = args
        return (jax.nn.silu(xb @ w_gate[e]) * (xb @ w_up[e])) @ w_down[e]

    ys = lax.map(expert_block, (xs, block_expert)).reshape(cap, D)
    y = jnp.zeros((T, D), h.dtype).at[buf_tok].add(ys * buf_w[:, None].astype(ys.dtype))
    return y.reshape(B, S, D)

def first_inputs(seed: int = 0) -> dict:
    key = jax.random.key(seed)
    ks = jax.random.split(key, 27)
    D, DI, NH, DH = D_MODEL, MLSTM_INNER, MLSTM_HEADS, MLSTM_HEAD_DIM
    nA, nB = N_A_LAYERS, N_B_LAYERS

    def nrm(k, shape, s):
        return jax.random.normal(k, shape, jnp.float32) * s

    n_mod = DEPTH * N_MOD_PER_LAYER * D + 2 * D
    x = nrm(ks[0], (BATCH, SEQ, D), 1.0)
    c = nrm(ks[1], (BATCH, D), 1.0)
    w_ada = nrm(ks[2], (D, n_mod), 0.1 * D ** -0.5)
    b_ada = nrm(ks[3], (n_mod,), 0.01)
    ln_g = 1.0 + nrm(ks[4], (DEPTH, 2, D), 0.02)
    ln_b = nrm(ks[5], (DEPTH, 2, D), 0.02)
    a_w_in = nrm(ks[6], (nA, D, 2 * DI), D ** -0.5)
    a_conv_w = nrm(ks[7], (nA, CONV_WIDTH, DI), CONV_WIDTH ** -0.5)
    a_conv_b = nrm(ks[8], (nA, DI), 0.01)
    a_wq = nrm(ks[9], (nA, NH, DH, DH), DH ** -0.5)
    a_wk = nrm(ks[10], (nA, NH, DH, DH), DH ** -0.5)
    a_wv = nrm(ks[11], (nA, NH, DH, DH), DEEPNORM_BETA * DH ** -0.5)
    a_w_if = nrm(ks[12], (nA, DI, 2 * NH), 0.1 * DI ** -0.5)
    a_b_if = jnp.concatenate([nrm(ks[13], (nA, NH), 0.1),
                              jnp.linspace(3.0, 6.0, NH) + nrm(ks[14], (nA, NH), 0.1)], axis=-1)
    a_gn_g = 1.0 + nrm(ks[15], (nA, DI), 0.02)
    a_skip = 1.0 + nrm(ks[16], (nA, DI), 0.02)
    a_w_out = nrm(ks[17], (nA, DI, D), DEEPNORM_BETA * DI ** -0.5)
    b_w_kv = jnp.concatenate([nrm(ks[18], (D, D), D ** -0.5),
                              nrm(ks[19], (D, D), DEEPNORM_BETA * D ** -0.5)], axis=-1)
    b_wq = nrm(ks[20], (nB, D, D), D ** -0.5)
    b_wo = nrm(ks[21], (nB, D, D), DEEPNORM_BETA * D ** -0.5)
    moe_w_router = nrm(ks[22], (D, N_EXPERTS), D ** -0.5)
    moe_b_router = nrm(ks[23], (N_EXPERTS,), 0.01)
    moe_w_gate = nrm(ks[24], (DEPTH, N_EXPERTS, D, D_FF_EXPERT), D ** -0.5)
    moe_w_up = nrm(ks[25], (DEPTH, N_EXPERTS, D, D_FF_EXPERT), D ** -0.5)
    moe_w_down = nrm(ks[26], (DEPTH, N_EXPERTS, D_FF_EXPERT, D), DEEPNORM_BETA * D_FF_EXPERT ** -0.5)
    return {'x': x, 'c': c, 'w_ada': w_ada, 'b_ada': b_ada, 'ln_g': ln_g, 'ln_b': ln_b,
            'a_w_in': a_w_in, 'a_conv_w': a_conv_w, 'a_conv_b': a_conv_b, 'a_wq': a_wq, 'a_wk': a_wk,
            'a_wv': a_wv, 'a_w_if': a_w_if, 'a_b_if': a_b_if, 'a_gn_g': a_gn_g, 'a_skip': a_skip,
            'a_w_out': a_w_out, 'b_w_kv': b_w_kv, 'b_wq': b_wq, 'b_wo': b_wo,
            'moe_w_router': moe_w_router, 'moe_b_router': moe_b_router, 'moe_w_gate': moe_w_gate,
            'moe_w_up': moe_w_up, 'moe_w_down': moe_w_down}

def first_block(x, c, w_ada, b_ada, ln_g, ln_b, a_w_in, a_conv_w, a_conv_b, a_wq, a_wk, a_wv, a_w_if,
              a_b_if, a_gn_g, a_skip, a_w_out, b_w_kv, b_wq, b_wo, moe_w_router, moe_b_router,
              moe_w_gate, moe_w_up, moe_w_down):
    B, S, D = x.shape
    n_layer_mod = DEPTH * N_MOD_PER_LAYER * D
    cond = jax.nn.silu(c) @ w_ada + b_ada
    mods = cond[:, :n_layer_mod].reshape(B, DEPTH, 2, 3, D)
    kv_mod = cond[:, n_layer_mod:].reshape(B, 2, D)
    slopes = alibi_slopes(ATTN_HEADS)
    kv = None
    for layer in range(DEPTH):
        shift, scale, gate = mods[:, layer, 0, 0], mods[:, layer, 0, 1], 1.0 + mods[:, layer, 0, 2]
        h = modulate(x, shift, scale)
        if layer < N_A_LAYERS:
            i = layer
            y = mlstm_layer(h, a_w_in[i], a_conv_w[i], a_conv_b[i], a_wq[i], a_wk[i], a_wv[i], a_w_if[i],
                            a_b_if[i], a_gn_g[i], a_skip[i], a_w_out[i])
        else:
            if kv is None:
                kv = shared_kv(x, kv_mod[:, 0], kv_mod[:, 1], b_w_kv)
            j = layer - N_A_LAYERS
            y = moba_layer(h, b_wq[j], b_wo[j], kv[0], kv[1], kv[2], slopes)
        x = layer_norm(DEEPNORM_ALPHA * x + gate[:, None, :] * y, ln_g[layer, 0], ln_b[layer, 0])
        shift, scale, gate = mods[:, layer, 1, 0], mods[:, layer, 1, 1], 1.0 + mods[:, layer, 1, 2]
        h = modulate(x, shift, scale)
        y = moe_ffn(h, moe_w_router, moe_b_router, moe_w_gate[layer], moe_w_up[layer], moe_w_down[layer])
        x = layer_norm(DEEPNORM_ALPHA * x + gate[:, None, :] * y, ln_g[layer, 1], ln_b[layer, 1])
    return x


DEPTH_2 = 4

CHUNK = 64
N_MIXERS = 3
EPS = 1e-6

POOL_WINDOWS = (2, 4, 8, 16)
N_POOL_GROUPS = len(POOL_WINDOWS)
POOL_GROUP = D_MODEL // N_POOL_GROUPS

SB_HEAD_DIM = 64
SB_HEADS = D_MODEL // SB_HEAD_DIM
Q_BLOCK = 128

S5_GROUP = 16
S5_GROUPS = D_MODEL // S5_GROUP
S5_STATE = 64
S5_DT_MIN = 1e-3
S5_DT_MAX = 1e-1

MEM_LEN = 256
XA_HEADS = 4
XA_HEAD_DIM = D_MODEL // XA_HEADS

D_FF = ((8 * D_MODEL // 3 + 127) // 128) * 128
CONV_WIDTH_2 = 3

N_POOL_LAYERS = (DEPTH_2 + 2) // 3
N_SB_LAYERS = (DEPTH_2 + 1) // 3
N_S5_LAYERS = DEPTH_2 // 3


def rms_norm(x, g):
    xf = x.astype(jnp.float32)
    y = xf * lax.rsqrt(jnp.mean(xf * xf, axis=-1, keepdims=True) + EPS)
    return (y * g.astype(jnp.float32)).astype(x.dtype)

def causal_shift(x, k):
    return jnp.pad(x, ((0, 0), (k, 0), (0, 0)))[:, : x.shape[1]]

def pool_mixer(h, w, scale):
    B, S, D = h.shape
    hf = h.astype(jnp.float32)
    cs = jnp.cumsum(hf, axis=1)
    counts = jnp.arange(1, S + 1, dtype=jnp.float32)
    groups = []
    for gi, win in enumerate(POOL_WINDOWS):
        sl = slice(gi * POOL_GROUP, (gi + 1) * POOL_GROUP)
        c = cs[..., sl]
        win_sum = c - causal_shift(c, win)
        cnt = jnp.minimum(counts, float(win))[None, :, None]
        groups.append(win_sum / cnt - hf[..., sl])
    p = jnp.stack(groups, axis=2).astype(h.dtype)
    y = jnp.einsum('bsgc,gcd->bsgd', p, w).reshape(B, S, D)
    return y * scale

def stick_breaking_attention(h, w_qkv, w_o):
    B, S, D = h.shape
    qkv = (h @ w_qkv).reshape(B, S, 3, SB_HEADS, SB_HEAD_DIM)
    q, k, v = qkv[:, :, 0], qkv[:, :, 1], qkv[:, :, 2]
    scale = SB_HEAD_DIM ** -0.5
    outs = []
    for i in range(S // Q_BLOCK):
        q0 = i * Q_BLOCK
        kend = q0 + Q_BLOCK
        z = jnp.einsum('bqhd,bkhd->bhqk', q[:, q0:kend], k[:, :kend]).astype(jnp.float32) * scale
        qpos = q0 + jnp.arange(Q_BLOCK)
        kpos = jnp.arange(kend)
        mask = kpos[None, :] < qpos[:, None]
        log_one_minus = jnp.where(mask, jax.nn.log_sigmoid(-z), 0.0)
        between = lax.cumsum(log_one_minus, axis=3, reverse=True) - log_one_minus
        a = jnp.where(mask, jnp.exp(jax.nn.log_sigmoid(z) + between), 0.0)
        outs.append(jnp.einsum('bhqk,bkhd->bqhd', a.astype(v.dtype), v[:, :kend]))
    o = jnp.concatenate(outs, axis=1).reshape(B, S, D)
    return o @ w_o

def _lin_rec_combine(left, right):
    a1, b1 = left
    a2, b2 = right
    return a1 * a2, a2 * b1 + b2

def s5_mixer(h, a_re, a_im, log_dt, b_re, b_im, c_re, c_im, d, w_glu):
    B, S, D = h.shape
    f32 = jnp.float32
    u = h.astype(f32)
    lam = lax.complex(a_re.astype(f32), a_im.astype(f32))
    dt = jnp.exp(log_dt.astype(f32))[:, None]
    dt_lam = lam * dt
    a_bar = jnp.exp(dt_lam)
    b_bar = ((a_bar - 1.0) / lam)[..., None] * lax.complex(b_re.astype(f32), b_im.astype(f32))
    c_mat = lax.complex(c_re.astype(f32), c_im.astype(f32))
    steps = jnp.arange(1, CHUNK + 1, dtype=f32)
    a_pow = jnp.exp(steps[:, None, None] * dt_lam[None])
    n_chunks = S // CHUNK
    u_chunks = u.reshape(B, n_chunks, CHUNK, S5_GROUPS, S5_GROUP).transpose(1, 0, 2, 3, 4)

    def chunk_step(state, u_blk):
        bu = jnp.einsum('bcgi,gpi->bcgp', u_blk.astype(jnp.complex64), b_bar)
        a_seq = jnp.broadcast_to(a_bar, bu.shape)
        _, xs = lax.associative_scan(_lin_rec_combine, (a_seq, bu), axis=1)
        xs = xs + a_pow[None] * state[:, None]
        y = jnp.real(jnp.einsum('bcgp,gip->bcgi', xs, c_mat))
        return xs[:, -1], y

    state0 = jnp.zeros((B, S5_GROUPS, S5_STATE), jnp.complex64)
    _, ys = lax.scan(chunk_step, state0, u_chunks)
    y = ys.transpose(1, 0, 2, 3, 4).reshape(B, S, D) + d.astype(f32) * u
    y = jax.nn.gelu(y).astype(h.dtype)
    val, gate = jnp.split(y @ w_glu, 2, axis=-1)
    return val * jax.nn.sigmoid(gate)

def memory_cross_attention(h, mem_n, wq, wkv, wo):
    B, S, D = h.shape
    M = mem_n.shape[1]
    q = (h @ wq).reshape(B, S, XA_HEADS, XA_HEAD_DIM)
    kv = (mem_n @ wkv).reshape(B, M, 2, XA_HEADS, XA_HEAD_DIM)
    k, v = kv[:, :, 0], kv[:, :, 1]
    s = jnp.einsum('bshd,bmhd->bhsm', q, k).astype(jnp.float32) * (XA_HEAD_DIM ** -0.5)
    p = jax.nn.softmax(s, axis=-1).astype(v.dtype)
    o = jnp.einsum('bhsm,bmhd->bshd', p, v).reshape(B, S, D)
    return o @ wo

def conv_glu_ffn(h, w_up, conv_w, conv_b, w_down):
    u = h @ w_up
    u = sum(conv_w[CONV_WIDTH_2 - 1 - k] * causal_shift(u, k) for k in range(CONV_WIDTH_2)) + conv_b
    val, gate = jnp.split(u, 2, axis=-1)
    return (jax.nn.silu(gate) * val) @ w_down

def second_inputs(seed: int = 0) -> dict:
    key = jax.random.key(seed)
    keys = iter(jax.random.split(key, 40))
    f32 = jnp.float32

    def nrm(shape, scale):
        return jax.random.normal(next(keys), shape, f32) * scale

    def gain(shape):
        return 1.0 + nrm(shape, 0.02)

    D, F = D_MODEL, D_FF
    G, P, Cg = S5_GROUPS, S5_STATE, S5_GROUP
    a_im_init = jnp.pi * jnp.arange(P, dtype=f32)
    return {
        "x": nrm((BATCH, SEQ, D), 1.0),
        "mem": nrm((BATCH, MEM_LEN, D), 1.0),
        "mix_norm_g": gain((DEPTH_2, D)),
        "pool_w": nrm((N_POOL_LAYERS, N_POOL_GROUPS, POOL_GROUP, POOL_GROUP), POOL_GROUP ** -0.5),
        "pool_scale": gain((N_POOL_LAYERS, D)),
        "sb_w_qkv": nrm((N_SB_LAYERS, D, 3 * D), D ** -0.5),
        "sb_w_o": nrm((N_SB_LAYERS, D, D), D ** -0.5),
        "s5_a_re": -0.5 + nrm((N_S5_LAYERS, G, P), 0.01),
        "s5_a_im": a_im_init + nrm((N_S5_LAYERS, G, P), 0.01),
        "s5_log_dt": jax.random.uniform(next(keys), (N_S5_LAYERS, G), f32,
                                        minval=math.log(S5_DT_MIN), maxval=math.log(S5_DT_MAX)),
        "s5_b_re": nrm((N_S5_LAYERS, G, P, Cg), (2 * Cg) ** -0.5),
        "s5_b_im": nrm((N_S5_LAYERS, G, P, Cg), (2 * Cg) ** -0.5),
        "s5_c_re": nrm((N_S5_LAYERS, G, Cg, P), (2 * P) ** -0.5),
        "s5_c_im": nrm((N_S5_LAYERS, G, Cg, P), (2 * P) ** -0.5),
        "s5_d": nrm((N_S5_LAYERS, D), 1.0),
        "s5_w_glu": nrm((N_S5_LAYERS, D, 2 * D), D ** -0.5),
        "xa_norm_g": gain((DEPTH_2, D)),
        "mem_norm_g": gain((DEPTH_2, D)),
        "xa_wq": nrm((DEPTH_2, D, D), D ** -0.5),
        "xa_wkv": nrm((DEPTH_2, D, 2 * D), D ** -0.5),
        "xa_wo": nrm((DEPTH_2, D, D), D ** -0.5),
        "ffn_norm_g": gain((DEPTH_2, D)),
        "ffn_w_up": nrm((DEPTH_2, D, 2 * F), D ** -0.5),
        "ffn_conv_w": nrm((DEPTH_2, CONV_WIDTH_2, 2 * F), CONV_WIDTH_2 ** -0.5),
        "ffn_conv_b": nrm((DEPTH_2, 2 * F), 0.01),
        "ffn_w_down": nrm((DEPTH_2, F, D), F ** -0.5),
        "final_norm_g": gain((D,)),
    }

def second_block(x, mem, mix_norm_g, pool_w, pool_scale, sb_w_qkv, sb_w_o,
              s5_a_re, s5_a_im, s5_log_dt, s5_b_re, s5_b_im, s5_c_re, s5_c_im, s5_d, s5_w_glu,
              xa_norm_g, mem_norm_g, xa_wq, xa_wkv, xa_wo,
              ffn_norm_g, ffn_w_up, ffn_conv_w, ffn_conv_b, ffn_w_down, final_norm_g):
    h = x
    for i in range(DEPTH_2):
        kind = i % N_MIXERS
        j = i // N_MIXERS
        hn = rms_norm(h, mix_norm_g[i])
        if kind == 0:
            t = pool_mixer(hn, pool_w[j], pool_scale[j])
        elif kind == 1:
            t = stick_breaking_attention(hn, sb_w_qkv[j], sb_w_o[j])
        else:
            t = s5_mixer(hn, s5_a_re[j], s5_a_im[j], s5_log_dt[j], s5_b_re[j], s5_b_im[j],
                         s5_c_re[j], s5_c_im[j], s5_d[j], s5_w_glu[j])
        h = h + t.astype(h.dtype)
        m = memory_cross_attention(rms_norm(h, xa_norm_g[i]), rms_norm(mem, mem_norm_g[i]),
                                   xa_wq[i], xa_wkv[i], xa_wo[i])
        h = h + m.astype(h.dtype)
        f = conv_glu_ffn(rms_norm(h, ffn_norm_g[i]), ffn_w_up[i], ffn_conv_w[i], ffn_conv_b[i], ffn_w_down[i])
        h = h + f.astype(h.dtype)
    return rms_norm(h, final_norm_g)


def setup_inputs(seed=0):
    out = dict(first_inputs(seed))
    for name, value in second_inputs(seed + 1).items():
        if name != "x":
            out[name + "_2"] = value
    return out


def reference(
    x, c, w_ada, b_ada, ln_g, ln_b, a_w_in, a_conv_w, a_conv_b, a_wq, a_wk, a_wv, a_w_if,
    a_b_if, a_gn_g, a_skip, a_w_out, b_w_kv, b_wq, b_wo, moe_w_router, moe_b_router, moe_w_gate,
    moe_w_up, moe_w_down, mem_2, mix_norm_g_2, pool_w_2, pool_scale_2, sb_w_qkv_2, sb_w_o_2,
    s5_a_re_2, s5_a_im_2, s5_log_dt_2, s5_b_re_2, s5_b_im_2, s5_c_re_2, s5_c_im_2, s5_d_2,
    s5_w_glu_2, xa_norm_g_2, mem_norm_g_2, xa_wq_2, xa_wkv_2, xa_wo_2, ffn_norm_g_2, ffn_w_up_2,
    ffn_conv_w_2, ffn_conv_b_2, ffn_w_down_2, final_norm_g_2,
):
    x = first_block(
        x, c, w_ada, b_ada, ln_g, ln_b, a_w_in, a_conv_w, a_conv_b, a_wq, a_wk, a_wv, a_w_if,
        a_b_if, a_gn_g, a_skip, a_w_out, b_w_kv, b_wq, b_wo, moe_w_router, moe_b_router,
        moe_w_gate, moe_w_up, moe_w_down,
    )
    return second_block(
        x, mem_2, mix_norm_g_2, pool_w_2, pool_scale_2, sb_w_qkv_2, sb_w_o_2, s5_a_re_2,
        s5_a_im_2, s5_log_dt_2, s5_b_re_2, s5_b_im_2, s5_c_re_2, s5_c_im_2, s5_d_2, s5_w_glu_2,
        xa_norm_g_2, mem_norm_g_2, xa_wq_2, xa_wkv_2, xa_wo_2, ffn_norm_g_2, ffn_w_up_2,
        ffn_conv_w_2, ffn_conv_b_2, ffn_w_down_2, final_norm_g_2,
    )


_drawn_inputs = setup_inputs


def setup_inputs(seed=0):
    import zlib

    import numpy as np

    out = dict(_drawn_inputs(seed))
    spreads = {}
    factors = {'a_gn_g': 8.0,
     'a_skip': 8.0,
     'pool_scale_2': 2.833,
     's5_a_re_2': 64.0,
     's5_a_im_2': 38.192,
     's5_log_dt_2': 38.888,
     's5_b_re_2': 53.048,
     's5_b_im_2': 53.584,
     's5_c_re_2': 54.856,
     's5_c_im_2': 53.768,
     'xa_norm_g_2': 8.0,
     'mem_norm_g_2': 8.0,
     'ffn_conv_b_2': 5.161,
     'final_norm_g_2': 7.629}
    for name, (base, spread) in spreads.items():
        noise = np.random.default_rng([zlib.crc32(name.encode()), seed]).standard_normal(out[name].shape)
        drawn = base * np.exp(spread * noise) if base else spread * noise
        out[name] = __import__('jax').numpy.asarray(drawn.astype(out[name].dtype))
    for name, factor in factors.items():
        out[name] = (out[name] * factor).astype(out[name].dtype)
    return out
```

```python
from contextlib import ExitStack

import numpy as np

import concourse.bass as bass
from concourse import mybir

F32 = mybir.dt.float32
ALU = mybir.AluOpType
ACT = mybir.ActivationFunctionType
AX = mybir.AxisListType

P = 128
T = 256
TT = T // P
D = 1024
KD = D // P
DEPTH = 2
ALPHA = (2.0 * DEPTH) ** 0.25
LN_EPS = 1e-5
RMS_EPS = 1e-6
MH = 4
MI = 2 * D
MD = MI // MH
AH = 16
AD = D // AH
NE = 16
NG = 4
EG = NE // NG
FE = 512
DEPTH2 = 4
WINDOWS = (2, 4, 8, 16)
SG = 64
SP = 64
SC = D // SG
NT5 = SG // 2
XH = 4
XD = D // XH
FF = ((8 * D // 3 + 127) // 128) * 128
KF = FF // P
NSLOT = 5
NARENA = 16400
SLOT = 4096
NEG = 1e30
TWO_PI_HI = 6.28125
TWO_PI_LO = 2.0 * float(np.pi) - 6.28125
ROUND_MAGIC = 12582912.0


COLS = [("c", 8), ("b_ada", 112), ("a_conv_w", 64), ("a_conv_b", 16), ("a_gn_g", 16), ("a_skip", 16),
        ("bi", 1), ("bf", 1), ("mix_norm_g_2", 32), ("xa_norm_g_2", 32), ("mem_norm_g_2", 32),
        ("ffn_norm_g_2", 32), ("s5_d_2", 8), ("ffn_conv_w_2", 3 * DEPTH2 * 2 * KF),
        ("ffn_conv_b_2", DEPTH2 * 2 * KF)]
COL_AT = {}
NCOLS = 0
for _name, _n in COLS:
    COL_AT[_name] = NCOLS
    NCOLS += _n

CONSTS = [("ident", 128), ("dist0", 128), ("dist1", 256), ("causal", 128), ("later", 128), ("negone", 128),
          ("ones", 128), ("past0", 256), ("past1", 128), ("count", 4 * T), ("prio16", 16), ("prio4", 4)]
CONST_AT = {}
NCONST = 0
for _name, _n in CONSTS:
    CONST_AT[_name] = NCONST
    NCONST += _n


def constants():
    out = np.zeros((P, NCONST), np.float32)
    i, j = np.arange(P)[:, None], np.arange(T)[None, :]

    def put(name, v):
        out[:, CONST_AT[name]:CONST_AT[name] + v.shape[1]] = v

    put("ident", np.eye(P, dtype=np.float32))
    put("dist0", np.where(j[:, :P] <= i, i - j[:, :P], NEG))
    put("dist1", np.where(j <= i + P, i + P - j, NEG))
    put("causal", np.where(j[:, :P] <= i, 0.0, -NEG))
    put("later", np.where(i > j[:, :P], -1.0, 0.0))
    put("negone", -np.ones((P, P)))
    put("ones", np.ones((P, P)))
    put("past0", np.where(i < j, 1.0, 0.0))
    put("past1", np.where(i < j[:, :P], 1.0, 0.0))
    cnt = np.stack([1.0 / np.minimum(np.arange(1, T + 1), w) for w in WINDOWS]).reshape(1, -1)
    put("count", np.broadcast_to(cnt, (P, 4 * T)))
    put("prio16", np.broadcast_to(np.arange(16, 0, -1.0), (P, 16)))
    put("prio4", np.broadcast_to(np.arange(4, 0, -1.0), (P, 4)))
    return out


class Queue:

    def __init__(self, sem, chained):
        self.sem, self.chained, self.steps, self.count = sem, chained, [], 0

    def add(self, emit, *waits, signal=True):
        self.steps.append((waits, emit, signal))
        if signal:
            self.count += 1
        return (self.sem, self.count)

    def hold(self, *waits):
        self.steps.append((waits, None, False))

    def last(self):
        return (self.sem, self.count)

    def run(self, eng):
        met, done = {}, 0

        def wait(w):
            if w is None:
                return
            if isinstance(w, list):
                for x in w:
                    wait(x)
                return
            sem, value = w() if callable(w) else w
            if value > 0 and met.get(id(sem), 0) < value:
                met[id(sem)] = value
                eng.wait_ge(sem, value)

        for waits, emit, signal in self.steps:
            if self.chained:
                wait((self.sem, done))
            wait(list(waits))
            if emit is None:
                continue
            ins = emit(eng)
            if signal:
                ins.then_inc(self.sem, 1)
                done += 1


def build(nc, A, out, upto=99):
    ctx = ExitStack()
    with ctx:
        def sb(name, shape):
            return ctx.enter_context(nc.sbuf_tensor(name, shape, F32))

        nsem = [0]

        def sem(name):
            nsem[0] += 1
            return ctx.enter_context(nc.semaphore(name))

        ring = [sb(f"ring{i}", [P, SLOT]) for i in range(NSLOT)]
        X = sb("X", [P, TT, D])
        HT = sb("HT", [P, KD, T])
        CONST = sb("CONST", [P, NCONST])
        COL = sb("COL", [P, NCOLS])
        SHARED = sb("SHARED", [P, 4096])
        ROWG = sb("ROWG", [P, D])
        ROWB = sb("ROWB", [P, D])
        MOD = sb("MOD", [P, 112])
        WR = sb("WR", [P, KD, NE])
        BR = sb("BR", [P, NE])
        WIF = sb("WIF", [P, MI // P, 2 * MH])
        CSIL = sb("CSIL", [P, KD])
        STAT = sb("STAT", [P, 64])
        ARENA = sb("ARENA", [P, NARENA])
        RT = sb("RT", [P, D])
        GATE = SHARED[:, :].rearrange("p (g n) -> p g n", g=4)
        MEMN = SHARED[:, 0:2048].rearrange("p (k t) -> p k t", k=KD)
        MEMG = SHARED[:, 2048:4096].rearrange("p (k t) -> p k t", k=KD)
        banks = [ctx.enter_context(nc.psum_tensor(f"bank{i}", [P, 512], F32)) for i in range(8)]

        PE = Queue(sem("pe_done"), False)
        DV = Queue(sem("vector_done"), True)
        AC = Queue(sem("scalar_done"), True)
        LD = Queue(sem("weights_queue"), False)
        ML = Queue(sem("misc_queue"), False)

        def const(name, n=None):
            a = CONST_AT[name]
            return CONST[:, a:a + (n or dict(CONSTS)[name])]

        def col(name, j=0, n=1):
            a = COL_AT[name] + j
            return COL[:, a:a + n]

        ident = const("ident")
        arena_at = [0]

        def fence():
            arena_at[0] = 0
            now = [PE.last(), DV.last(), AC.last()]
            DV.hold(now)
            AC.hold(now)
            return now

        def arena(*shape):
            n = int(np.prod(shape))
            a = arena_at[0]
            arena_at[0] += n
            assert arena_at[0] <= NARENA, arena_at[0]
            v = ARENA[:, a:a + n]
            if len(shape) == 2:
                v = v.rearrange("p (a b) -> p a b", a=shape[0])
            elif len(shape) == 3:
                v = v.rearrange("p (a b c) -> p a b c", a=shape[0], b=shape[1])
            return v

        slot_sem = [sem(f"slot{i}") for i in range(NSLOT)]
        slot_count = [0] * NSLOT
        slot_free = []

        def take(*parts):
            n = len(slot_free)
            s = n % NSLOT
            slot_free.append(None)
            at = 0
            views = []
            for src in parts:
                k, w = src.shape[1], src.shape[2]
                dst = ring[s][:, at:at + k * w].rearrange("p (k n) -> p k n", k=k)
                at += k * w
                freed = (lambda m=n - NSLOT: slot_free[m]) if n >= NSLOT else None
                slot_count[s] += 16
                LD.add(lambda e, dst=dst, src=src, s=s: e.dma_start(dst, src).then_inc(slot_sem[s], 16),
                       freed, signal=False)
                views.append(dst)
            return n, views, (slot_sem[s], slot_count[s])

        def give(n, token):
            slot_free[n] = token

        def cols_of(w, c0, n):
            return w[:, c0:c0 + n].rearrange("(k p) n -> p k n", p=P)

        def rows_of(w, k0, nk):
            return w[k0 * P:(k0 + nk) * P, :].rearrange("(k p) n -> p k n", p=P)

        def small(dst, src, *waits):
            s = sem(f"small{nsem[0]}")
            ML.add(lambda e: e.dma_start(dst, src).then_inc(s, 16), *waits, signal=False)
            return (s, 16)

        def row(v):
            return v.rearrange("(a n) -> a n", a=1).broadcast_to([P, v.shape[0]])

        bank_free = [None] * 8
        turn = [0]

        def rot():
            turn[0] = (turn[0] + 1) % 4
            return 4 + turn[0]

        def mm(o, l, r, k, K, *waits, signal=False):
            return PE.add(lambda e: e.matmul(o, l, r, start=(k == 0), stop=(k == K - 1)), *waits, signal=signal)

        def transposes(b, pairs, *waits):
            for n, (at, src) in enumerate(pairs):
                m, w = src.shape[0], src.shape[1]
                o = banks[b][0:w, at:at + m]
                tok = PE.add(lambda e, o=o, src=src, m=m: e.transpose(o, src, ident[0:m, 0:m]),
                             *((list(waits) + [bank_free[b]]) if n == 0 else ()), signal=(n == len(pairs) - 1))
            return tok

        flip = [0]

        def affine(o, i, scale, bias, *waits, on=None):
            if on is None:
                flip[0] ^= 1
                on = "AD"[flip[0]]
            if on == "A":
                return AC.add(lambda e: e.activation(o, i, ACT.Identity, bias=0.0 if bias is None else bias,
                                                     scale=scale), *waits)
            if bias is None:
                return DV.add(lambda e: e.tensor_scalar(o, i, scale, None, ALU.mult), *waits)
            return DV.add(lambda e: e.tensor_scalar(o, i, scale, bias, ALU.mult, ALU.add), *waits)

        def copy(o, i, *waits, on=None):
            if on is None:
                flip[0] ^= 1
                on = "AD"[flip[0]]
            if on == "A":
                return AC.add(lambda e: e.copy(o, i), *waits)
            return DV.add(lambda e: e.tensor_copy(o, i), *waits)

        def tt(o, a, b, op, *waits):
            return DV.add(lambda e: e.tensor_tensor(o, a, b, op), *waits)

        def ts(o, a, s1, s2, op0, op1=None, *waits):
            if s2 is None:
                return DV.add(lambda e: e.tensor_scalar(o, a, s1, None, op0), *waits)
            return DV.add(lambda e: e.tensor_scalar(o, a, s1, s2, op0, op1), *waits)

        def stt(o, a, s, b, op0, op1, *waits, acc=None):
            if acc is None:
                return DV.add(lambda e: e.scalar_tensor_tensor(o, a, s, b, op0, op1), *waits)
            return DV.add(lambda e: e.scalar_tensor_tensor(o, a, s, b, op0, op1, accum_out=acc), *waits)

        def act(o, i, f, *waits, bias=0.0, scale=1.0, acc=None):
            return AC.add(lambda e: e.activation(o, i, f, bias=bias, scale=scale, accum_out=acc), *waits)

        def bank2(b):
            return banks[b][:, :].rearrange("p (a t) -> p a t", a=2)

        def to_channels(w, src, nk, n_out, evac, ready, n0=0):
            tok = None
            for n in range(0, n_out, 2):
                b = rot()
                for j in range(min(2, n_out - n)):
                    for k in range(nk):
                        tok = mm(bank2(b)[:, j, :], w[:, k, (n + j) * P:(n + j + 1) * P], src[:, k, :], k, nk,
                                 *([ready, bank_free[b]] if j == 0 and k == 0 else []),
                                 signal=(k == nk - 1))
                bank_free[b] = evac(n0 + n, b, tok)
            return tok

        def to_tokens(w, src, nk, first, last, ready, k0=0, halves=(0, 1), acc=lambda t, h: 2 * t + h):
            tok = None
            for t in range(TT):
                for h in halves:
                    b = acc(t, h)
                    for k in range(nk):
                        fresh = first and k == 0
                        end = last and k == nk - 1
                        tok = PE.add(lambda e, b=b, t=t, h=h, k=k, fresh=fresh, end=end: e.matmul(
                            banks[b][:, :], src[:, k0 + k, t * P:(t + 1) * P],
                            w[:, k, (h - halves[0]) * 512:(h - halves[0] + 1) * 512], start=fresh, stop=end),
                            *([ready] + ([bank_free[b]] if fresh else []) if k == 0 else []),
                            signal=(k == nk - 1))
            return tok

        def stats(t, *waits):
            bn = STAT[:, 8 + 12 * t:20 + 12 * t].rearrange("p (a b) -> p a b", a=2)
            for h in range(2):
                DV.add(lambda e, h=h: e.bn_stats(bn[:, h, :], X[:, t, h * 512:(h + 1) * 512]), *waits)
            return DV.add(lambda e: e.bn_aggr(STAT[:, 2 * t:2 * t + 2],
                                              STAT[:, 8 + 12 * t:20 + 12 * t].rearrange("p (a b) -> p a b", a=2)))

        def inv_sqrt(o, v, eps, *waits):
            tok = ts(o, v, 1.0, eps, ALU.mult, ALU.add, *waits)
            tok = act(o, o, ACT.Sqrt, tok)
            return DV.add(lambda e: e.reciprocal(o, o), tok)

        def layer_norm(g_ready):
            mv = STAT[:, 0:4].rearrange("p (t c) -> p t c", t=2)
            for t in range(TT):
                tok = stats(t)
            inv_sqrt(STAT[:, 4:6], mv[:, :, 1], LN_EPS, tok)
            for t in range(TT):
                ts(X[:, t, :], X[:, t, :], STAT[:, 2 * t:2 * t + 1], STAT[:, 4 + t:5 + t], ALU.subtract, ALU.mult)
                tt(X[:, t, :], X[:, t, :], ROWG[:, :], ALU.mult, *g_ready)
                tok = tt(X[:, t, :], X[:, t, :], ROWB[:, :], ALU.add)
            return tok

        def rms(src, dst, *waits):
            DV.hold(*waits)
            for t in range(TT):
                tok = act(RT[:, :], src[:, t, :], ACT.Square, *waits, acc=STAT[:, 32 + t:33 + t])
            ts(STAT[:, 34:36], STAT[:, 32:34], 1.0 / D, RMS_EPS, ALU.mult, ALU.add, tok)
            tok = act(STAT[:, 34:36], STAT[:, 34:36], ACT.Sqrt, DV.last())
            tok = DV.add(lambda e: e.reciprocal(STAT[:, 34:36], STAT[:, 34:36]), tok)
            for t in range(TT):
                tok = ts(dst[:, t, :], src[:, t, :], STAT[:, 34 + t:35 + t], None, ALU.mult)
            return tok

        def channels(src, moves, *waits):
            toks = []
            for k in range(0, KD, 2):
                b = rot()
                tok = transposes(b, [((j * 2 + t) * P, src[:, t, (k + j) * P:(k + j + 1) * P])
                                     for j in range(2) for t in range(TT)], *waits)
                flip[0] ^= 1
                on = "AD"[flip[0]]
                for j in range(2):
                    for dst, scale, bias in moves:
                        got = affine(dst[:, k + j, :], bank2(b)[:, j, :], scale(k + j),
                                     bias(k + j) if bias else None, tok, on=on)
                bank_free[b] = got
                toks = [AC.last(), DV.last()]
            return toks

        c_ready = small(CONST[:, :], A["consts"])
        col_ready = small(COL[:, :], A["cols"])
        x_ready = small(X[:, :, :], A["x"].rearrange("(t p) n -> p t n", p=P))
        xt_ready = small(HT[:, :, :], A["xT"].rearrange("(k p) t -> p k t", p=P))
        gate_rows = [small(GATE[:, g, :], row(A["b_ada"][(3 * g + 2) * D:(3 * g + 3) * D])) for g in range(4)]
        wif_ready = small(WIF[:, :, :], A["a_w_if"].rearrange("(k p) n -> p k n", p=P))
        wr_ready = small(WR[:, :, :], A["moe_w_router"].rearrange("(k p) n -> p k n", p=P))
        br_ready = small(BR[:, :], row(A["moe_b_router"]))
        DV.add(lambda e: e.memset(STAT[:, :], 0.0))
        csil_ready = act(CSIL[:, :], col("c", 0, 8), ACT.Silu, col_ready)
        DV.hold(c_ready, col_ready)
        AC.hold(c_ready)

        def ada(v):
            gate = v < 12 and v % 3 == 2
            bc = None if gate else rot()
            for h in range(2):
                n, (w,), arrived = take(cols_of(A["w_ada"], v * D + h * 512, 512))
                if gate:
                    b = rot()
                    for k in range(KD):
                        tok = mm(banks[b][:, :], CSIL[:, k:k + 1].broadcast_to([P, P]), w[:, k, :], k, KD,
                                 arrived, csil_ready, c_ready, bank_free[b], signal=(k == KD - 1))
                    g = GATE[:, v // 3, h * 512:(h + 1) * 512]
                    bank_free[b] = stt(g, banks[b][:, :], 1.0, g, ALU.add, ALU.add, tok, gate_rows[v // 3])
                else:
                    for j in range(4):
                        for k in range(KD):
                            tok = mm(banks[bc][:, 4 * h + j:4 * h + j + 1], w[:, k, j * P:(j + 1) * P],
                                     CSIL[:, k:k + 1], k, KD, arrived, csil_ready, c_ready, bank_free[bc],
                                     signal=(k == KD - 1))
                give(n, tok)
            if gate:
                return bank_free[b]
            scale = v == 13 or (v < 12 and v % 3 == 1)
            m = MOD[:, 8 * v:8 * v + 8]
            tok = tt(m, banks[bc][:, 0:8], col("b_ada", 8 * v, 8), ALU.add, tok)
            bank_free[bc] = tok
            if scale:
                tok = ts(m, m, 1.0, None, ALU.add)
            return tok

        def shift_of(v):
            return lambda k: MOD[:, 8 * v + k:8 * v + k + 1]

        def residual(g, lng, lnb):
            rows = [small(ROWG[:, :], row(lng), DV.last()), small(ROWB[:, :], row(lnb), DV.last())]
            acc_ready = PE.last()
            for t in range(TT):
                for h in range(2):
                    s = slice(h * 512, (h + 1) * 512)
                    b = 2 * t + h
                    o = RT[:, s]
                    tok = tt(o, banks[b][:, :], GATE[:, g, s], ALU.mult, acc_ready)
                    bank_free[b] = tok
                    stt(X[:, t, s], X[:, t, s], ALPHA, o, ALU.mult, ALU.add, x_ready)
            return layer_norm(rows)

        def mlstm():
            nm = MI // P
            xm = arena(nm, 3 + T)
            xc = arena(nm, T)
            ada(0)
            ready = ada(1)
            for k in range(KD):
                tok = affine(HT[:, k, :], HT[:, k, :], MOD[:, 8 + k:9 + k], MOD[:, k:k + 1], ready, xt_ready, on="D")
            h_ready = tok
            pad = DV.add(lambda e: e.memset(xm[:, :, 0:3], 0.0))
            xm_ready = {}

            def evac_x(n, b, tok):
                t1 = copy(xm[:, n:n + 2, 3:3 + T], bank2(b), tok, on="A")
                xm_ready[n] = t1
                for c in (n, n + 1):
                    w = lambda j: col("a_conv_w", 16 * j + c)
                    ts(xc[:, c, :], xm[:, c, 3:3 + T], w(3), col("a_conv_b", c), ALU.mult, ALU.add, t1)
                    for j in (2, 1, 0):
                        t2 = stt(xc[:, c, :], xm[:, c, j:j + T], w(j), xc[:, c, :], ALU.mult, ALU.add)
                act(xc[:, n:n + 2, :], xc[:, n:n + 2, :], ACT.Silu, t2)
                return t1

            for s in range(MI // 512):
                n, (w,), arrived = take(cols_of(A["a_w_in"], s * 512, 512))
                give(n, to_channels(w, HT, KD, 4, evac_x, [arrived, h_ready], n0=4 * s))
                if s == 1:
                    ada(2)
            xc_ready = AC.last()
            LI, LF, BC, GR, R8 = arena(T), arena(T), arena(T), arena(T), arena(16)
            b = rot()
            for half in range(2):
                for k in range(nm):
                    tok = mm(banks[b][0:MH, half * T:half * T + T], WIF[:, k, half * MH:half * MH + MH], xc[:, k, :],
                             k, nm, xc_ready, wif_ready, bank_free[b], signal=(k == nm - 1))
            ts(LI[0:MH, :], banks[b][0:MH, 0:T], col("bi")[0:MH, :], None, ALU.add, None, tok)
            tok = ts(LF[0:MH, :], banks[b][0:MH, T:2 * T], col("bf")[0:MH, :], None, ALU.add)
            bank_free[b] = tok
            act(GR[0:MH, :], LF[0:MH, :], ACT.Abs, tok)
            act(GR[0:MH, :], GR[0:MH, :], ACT.Exp, scale=-1.0)
            tok = act(GR[0:MH, :], GR[0:MH, :], ACT.Ln, bias=1.0)
            stt(LF[0:MH, :], LF[0:MH, :], 0.0, GR[0:MH, :], ALU.min, ALU.subtract, tok)
            for c in range(2):
                s = slice(c * P, (c + 1) * P)
                DV.add(lambda e, s=s: e.tensor_tensor_scan(BC[0:MH, s], const("ones")[0:MH, :], LF[0:MH, s], 0.0,
                                                           ALU.mult, ALU.add))
            tt(GR[0:MH, :], LI[0:MH, :], BC[0:MH, :], ALU.subtract)
            DV.add(lambda e: e.tensor_reduce(R8[0:MH, 8:9], GR[0:MH, 0:P], AX.X, ALU.max))
            ts(R8[0:MH, 8:9], R8[0:MH, 8:9], 0.0, None, ALU.max)
            tt(R8[0:MH, 9:10], BC[0:MH, P - 1:P], R8[0:MH, 8:9], ALU.add)
            ts(R8[0:MH, 8:9], R8[0:MH, 8:9], -1.0, None, ALU.mult)
            ts(R8[0:MH, 0:4], ident[0:MH, 0:MH], R8[0:MH, 9:10], None, ALU.mult)
            tok = ts(R8[0:MH, 4:8], ident[0:MH, 0:MH], R8[0:MH, 8:9], None, ALU.mult)
            BV = arena(20)
            b = rot()
            mm(banks[b][:, 0:4], BC[0:MH, 0:P], ident[0:MH, 0:MH], 0, 1, tok, bank_free[b])
            mm(banks[b][:, 4:8], BC[0:MH, P:T], ident[0:MH, 0:MH], 0, 1)
            tok = mm(banks[b][:, 8:16], const("ones")[0:MH, :], R8[0:MH, 0:8], 0, 1, signal=True)
            bank_free[b] = copy(BV[:, 0:16], banks[b][:, 0:16], tok, on="D")
            bv_ready = tt(BV[:, 16:20], BV[:, 4:8], BV[:, 8:12], ALU.add)
            q, k_, v = arena(4, T), arena(4, T), arena(TT, MD)
            HH = arena(TT, MD)
            E, S, ST = arena(3 * P), arena(3 * P), arena(3 * P)
            m, bn = arena(16), arena(TT * 6)
            for h in range(MH):
                r = {}

                def evac_to(dst, name, scale):
                    def f(n, b, tok):
                        r[name] = affine(dst[:, n:n + 2, :], bank2(b), scale, None, tok)
                        r.setdefault("all", []).append(r[name])
                        return r[name]
                    return f

                n, (wq, wk), arrived = take(rows_of(A["a_wq"][h], 0, 4), rows_of(A["a_wk"][h], 0, 4))
                src = xc[:, 4 * h:4 * h + 4, :]
                to_channels(wq, src, 4, 4, evac_to(q, "q", 1.0), [arrived, xc_ready])
                give(n, to_channels(wk, src, 4, 4, evac_to(k_, "k", MD ** -0.5), [arrived]))
                n, (wv,), arrived = take(rows_of(A["a_wv"][h], 0, 4))
                for t in range(TT):
                    b = rot()
                    for k in range(4):
                        tok = mm(banks[b][:, :], xm[:, 4 * h + k, 3 + t * P:3 + (t + 1) * P], wv[:, k, :], k, 4,
                                 arrived, bank_free[b], signal=(k == 3))
                    bank_free[b] = copy(v[:, t, :], banks[b][:, :], tok)
                    r["all"].append(bank_free[b])
                give(n, tok)
                bg, bs = rot(), rot()
                gtok = mm(banks[bg][:, 0:T], ident[0:MH, h:h + 1].broadcast_to([MH, P]), GR[0:MH, :], 0, 1,
                          bank_free[bg], signal=True)
                for n, (tq, tk) in enumerate(((0, 0), (1, 1), (1, 0))):
                    for k in range(4):
                        stok = mm(banks[bs][:, n * P:(n + 1) * P], q[:, k, tq * P:(tq + 1) * P],
                                  k_[:, k, tk * P:(tk + 1) * P], k, 4, r["all"], bank_free[bs], signal=(k == 3))
                for c in range(2):
                    bcol = BV[:, 4 * c + h:4 * c + h + 1]
                    d = E[:, c * P:(c + 1) * P]
                    stt(d, banks[bg][:, c * P:(c + 1) * P], bcol, const("causal"), ALU.add, ALU.add, gtok, bv_ready)
                    DV.add(lambda e, c=c, d=d: e.tensor_reduce(m[:, c:c + 1], d, AX.X, ALU.max))
                    a = bcol if c == 0 else BV[:, 16 + h:17 + h]
                    tt(m[:, c:c + 1], m[:, c:c + 1], a, ALU.max)
                mtok = ts(m[:, 2:4], m[:, 0:2], -1.0, None, ALU.mult)
                for c in range(2):
                    act(E[:, c * P:(c + 1) * P], E[:, c * P:(c + 1) * P], ACT.Exp, mtok, bias=m[:, 2 + c:3 + c])
                bank_free[bg] = act(E[:, 2 * P:3 * P], banks[bg][:, 0:P], ACT.Exp, bias=BV[:, 12 + h:13 + h])
                act(m[:, 4:5], BV[:, 16 + h:17 + h], ACT.Exp, bias=m[:, 3:4])
                etok = act(m[:, 5:7], m[:, 2:4], ACT.Exp)
                for n, (sc, ac) in enumerate(((1.0, 7), (1.0, 8), (m[:, 4:5], 9))):
                    tok = stt(S[:, n * P:(n + 1) * P], banks[bs][:, n * P:(n + 1) * P], sc, E[:, n * P:(n + 1) * P],
                              ALU.mult, ALU.mult, etok, stok, acc=m[:, ac:ac + 1])
                bank_free[bs] = sw = tok
                tt(m[:, 8:9], m[:, 8:9], m[:, 9:10], ALU.add)
                stt(m[:, 10:12], m[:, 7:9], -1.0, m[:, 7:9], ALU.mult, ALU.max)
                tt(m[:, 10:12], m[:, 10:12], m[:, 5:7], ALU.max)
                rtok = DV.add(lambda e: e.reciprocal(m[:, 10:12], m[:, 10:12]))
                b = rot()
                tok = transposes(b, [(n * P, S[:, n * P:(n + 1) * P]) for n in range(3)], sw)
                bank_free[b] = st = copy(ST[:, :], banks[b][:, 0:3 * P], tok, on="A")
                for t in range(TT):
                    b = rot()
                    for k in range(t + 1):
                        blk = (0, 1)[t] if k == 0 else 2
                        src_v = v[:, (0, 1)[t] if k == 0 else 0, :]
                        tok = mm(banks[b][:, :], ST[:, blk * P:(blk + 1) * P], src_v, k, t + 1, st, bank_free[b],
                                 signal=(k == t))
                    htok = ts(HH[:, t, :], banks[b][:, :], m[:, 10 + t:11 + t], None, ALU.mult, None, tok, rtok)
                    bank_free[b] = htok
                    DV.add(lambda e, t=t: e.bn_stats(bn[:, 6 * t:6 * t + 6], HH[:, t, :]))
                    DV.add(lambda e, t=t: e.bn_aggr(m[:, 12 + 2 * t:14 + 2 * t], bn[:, 6 * t:6 * t + 6]))
                mv = m[:, 12:16].rearrange("p (t c) -> p t c", t=2)
                inv_sqrt(m[:, 10:12], mv[:, :, 1], LN_EPS, DV.last())
                for t in range(TT):
                    htok = ts(HH[:, t, :], HH[:, t, :], m[:, 12 + 2 * t:13 + 2 * t], m[:, 10 + t:11 + t],
                              ALU.subtract, ALU.mult)
                for c in range(4):
                    ts(xc[:, 4 * h + c, :], xc[:, 4 * h + c, :], col("a_skip", 4 * h + c), None, ALU.mult, None, stok)
                for c in range(0, 4, 2):
                    b = rot()
                    tok = transposes(b, [((j * 2 + t) * P, HH[:, t, (c + j) * P:(c + j + 1) * P])
                                         for j in range(2) for t in range(TT)], htok)
                    for j in range(2):
                        ch = 4 * h + c + j
                        tok2 = stt(xc[:, ch, :], bank2(b)[:, j, :], col("a_gn_g", ch), xc[:, ch, :],
                                   ALU.mult, ALU.add, tok)
                    bank_free[b] = tok2


            z_free = [None, None]

            def evac_z(n, b, tok):
                i = (n // 2) % 2
                z = RT[:, 512 * i:512 * i + 512].rearrange("p (a t) -> p a t", a=2)
                t1 = act(z, bank2(b), ACT.Silu, tok, z_free[i])
                z_free[i] = tt(xc[:, n:n + 2, :], xc[:, n:n + 2, :], z, ALU.mult, t1)
                return t1

            for s in range(MI // 512):
                n, (w,), arrived = take(cols_of(A["a_w_in"], MI + s * 512, 512))
                give(n, to_channels(w, HT, KD, 4, evac_z, [arrived], n0=4 * s))
            zr = DV.last()
            for s in range(4):
                n, (w,), arrived = take(rows_of(A["a_w_out"], 4 * s, 4))
                give(n, to_tokens(w, xc, 4, s == 0, s == 3, [arrived, zr], k0=4 * s))
            return residual(0, A["ln_g"][0, 0], A["ln_b"][0, 0])

        def moe(layer, x_done):
            v = 6 * layer + 3
            ada(v)
            ada(v + 1)
            ada(v + 2)
            fence()
            h_ready = channels(X, [(HT, shift_of(v + 1), shift_of(v))], x_done)
            b = rot()
            for t in range(TT):
                for k in range(KD):
                    tok = mm(banks[b][:, t * NE:(t + 1) * NE], HT[:, k, t * P:(t + 1) * P], WR[:, k, :], k, KD,
                             h_ready, wr_ready, bank_free[b], signal=(k == KD - 1))
            L = banks[b][:, 0:TT * NE].rearrange("p (t e) -> p t e", t=TT)
            pr, sel, w1, w2, comb = (arena(TT, NE) for _ in range(5))
            c2 = arena(4)
            pairs, gs, gm = arena(TT * NG, 6), arena(TT, NG), arena(TT, NG)

            def wide(x, n=NE):
                return x.unsqueeze(2).broadcast_to([P, TT, n])

            def reduce(o, i, op):
                return DV.add(lambda e: e.tensor_reduce(o, i, AX.X, op))

            DV.add(lambda e: e.tensor_reduce(c2[:, 0:2], L, AX.X, ALU.max), tok)
            bank_free[b] = tt(pr, L, wide(c2[:, 0:2]), ALU.subtract)
            tok = act(pr, pr, ACT.Exp, bank_free[b])
            DV.hold(tok)
            reduce(c2[:, 0:2], pr, ALU.add)
            DV.add(lambda e: e.reciprocal(c2[:, 0:2], c2[:, 0:2]))
            tt(pr, pr, wide(c2[:, 0:2]), ALU.mult)
            tt(sel, pr, BR[:, :].unsqueeze(1).broadcast_to([P, TT, NE]), ALU.add, br_ready)
            s4 = sel.rearrange("p t (g e) -> p (t g) e", g=NG)
            tt(pairs[:, :, 0:3], s4[:, :, 0:3], s4[:, :, 1:4], ALU.add)
            tt(pairs[:, :, 3:5], s4[:, :, 0:2], s4[:, :, 2:4], ALU.add)
            tt(pairs[:, :, 5:6], s4[:, :, 0:1], s4[:, :, 3:4], ALU.add)
            DV.add(lambda e: e.tensor_reduce(gs.rearrange("p t g -> p (t g)"), pairs, AX.X, ALU.max))

            def first_max(o, x, n, prio):
                reduce(c2[:, 0:2], x, ALU.max)
                tt(o, x, wide(c2[:, 0:2], n), ALU.is_equal)
                tt(o, o, const(prio).unsqueeze(1).broadcast_to([P, TT, n]), ALU.mult)
                reduce(c2[:, 0:2], o, ALU.max)
                return tt(o, o, wide(c2[:, 0:2], n), ALU.is_equal)

            first_max(gm, gs, NG, "prio4")
            gmw = gm.rearrange("p t g -> p (t g)").unsqueeze(2).broadcast_to([P, TT * NG, EG])
            tt(s4, s4, gmw, ALU.mult)
            w1g = w1.rearrange("p t (g e) -> p (t g) e", g=NG)
            DV.add(lambda e: e.tensor_scalar(w1g, gmw, NEG, -NEG, ALU.mult, ALU.add))
            tt(sel, sel, w1, ALU.add)
            first_max(w1, sel, NE, "prio16")
            stt(sel, w1, -2.0 * NEG, sel, ALU.mult, ALU.add)
            first_max(w2, sel, NE, "prio16")
            tt(w1, w1, w2, ALU.add)
            tt(comb, w1, pr, ALU.mult)
            reduce(c2[:, 0:2], comb, ALU.add)
            DV.add(lambda e: e.reciprocal(c2[:, 0:2], c2[:, 0:2]))
            comb_ready = tt(comb, comb, wide(c2[:, 0:2]), ALU.mult)

            HID = [arena(4, T) for _ in range(2)]
            CB = [arena(T) for _ in range(2)]
            SGT = [arena(2, T) for _ in range(2)]
            hid_free, cb_free, hid_ready = [None] * 2, [None] * 2, [None] * 2
            sg_free = [None, None]
            turns = [0]

            def up(e_):
                i = e_ % 2
                ng, (wg,), ag = take(cols_of(A["moe_w_gate"][layer, e_], 0, FE))
                nu, (wu,), au = take(cols_of(A["moe_w_up"][layer, e_], 0, FE))
                b = rot()
                for t in range(TT):
                    tok = mm(banks[b][:, t * P:(t + 1) * P], comb[:, t, e_:e_ + 1].broadcast_to([P, P]), ident, 0, 1,
                             comb_ready, bank_free[b], signal=(t == TT - 1))
                bank_free[b] = cb = copy(CB[i], banks[b][:, 0:T], tok, cb_free[i], on="A")
                for n in range(0, 4, 2):
                    bg, bu = rot(), rot()
                    for w, b, arrived in ((wg, bg, ag), (wu, bu, au)):
                        for j in range(2):
                            for k in range(KD):
                                tok = mm(bank2(b)[:, j, :], w[:, k, (n + j) * P:(n + j + 1) * P], HT[:, k, :], k, KD,
                                         arrived, bank_free[b], signal=(k == KD - 1))
                        if w is wg:
                            gtok = tok
                        give(ng if w is wg else nu, tok)
                    q = turns[0] % 2
                    turns[0] += 1
                    bank_free[bg] = act(SGT[q], bank2(bg), ACT.Silu, gtok, sg_free[q])
                    o = HID[i][:, n:n + 2, :]
                    bank_free[bu] = tt(o, bank2(bu), CB[i].unsqueeze(1).broadcast_to([P, 2, T]), ALU.mult,
                                       tok, cb, hid_free[i])
                    sg_free[q] = hid_ready[i] = tt(o, o, SGT[q], ALU.mult, bank_free[bg])
                cb_free[i] = hid_ready[i]

            def down(e_):
                i = e_ % 2
                n, (w,), arrived = take(rows_of(A["moe_w_down"][layer, e_], 0, 4))
                hid_free[i] = to_tokens(w, HID[i], 4, e_ == 0, e_ == NE - 1, [arrived, hid_ready[i]])
                give(n, hid_free[i])

            up(0)
            for e_ in range(1, NE):
                up(e_)
                down(e_ - 1)
            down(NE - 1)
            return residual(2 * layer + 1, A["ln_g"][layer, 1], A["ln_b"][layer, 1])

        def project_heads(dst, w, c0, scale, src, ready, on=None):
            toks = []
            for s in range(2):
                n, (v,), arrived = take(cols_of(w, c0 + s * 512, 512))

                def evac(m, b, tok):
                    toks.append(affine(dst[:, m:m + 2, :], bank2(b), scale, None, tok, on=on))
                    return toks[-1]

                give(n, to_channels(v, src, KD, 4, evac, [arrived, ready], n0=4 * s))
            return toks

        def project_values(dst, w, c0, src, ready):
            toks = []
            for s in range(2):
                n, (v,), arrived = take(cols_of(w, c0 + s * 512, 512))
                for t in range(TT):
                    b = rot()
                    for k in range(KD):
                        tok = mm(banks[b][:, :], src[:, k, t * P:(t + 1) * P], v[:, k, :], k, KD,
                                 arrived, ready, bank_free[b], signal=(k == KD - 1))
                    bank_free[b] = copy(dst[:, t, s * 512:(s + 1) * 512], banks[b][:, :], tok)
                    toks.append(bank_free[b])
                give(n, tok)
            return toks

        def out_product(w, src, ready):
            for s in range(2):
                n, (v,), arrived = take(rows_of(w, 4 * s, 4))
                give(n, to_tokens(v, src, 4, s == 0, s == 1, [arrived, ready], k0=4 * s))

        def add_acc():
            ready = PE.last()
            for t in range(TT):
                for h in range(2):
                    s = slice(h * 512, (h + 1) * 512)
                    b = 2 * t + h
                    tok = tt(X[:, t, s], X[:, t, s], banks[b][:, :], ALU.add, ready)
                    bank_free[b] = tok
            return tok

        def moba(x_done):
            for v in (6, 7, 8, 12, 13):
                ada(v)
            fence()
            KVH, q, k_, v_, o = arena(KD, T), arena(KD, T), arena(KD, T), arena(TT, D), arena(KD, T)
            h_ready = channels(X, [(HT, shift_of(7), shift_of(6)), (KVH, shift_of(13), shift_of(12))], x_done)
            ready = project_heads(k_, A["b_w_kv"], 0, 1.0, KVH, h_ready)
            ready += project_values(v_, A["b_w_kv"], D, KVH, h_ready)
            ready += project_heads(q, A["b_wq"], 0, AD ** -0.5, HT, h_ready)
            NB = 3
            E, ET, sm = [arena(3 * P) for _ in range(NB)], [arena(3 * P) for _ in range(NB)], arena(4 * NB)
            e_free, et_free, s_tok, s_bank = [None] * NB, [None] * NB, {}, {}

            def scores(h):
                b = h % 4
                p0 = AD * (h % 2)
                qh, kh = q[p0:p0 + AD, h // 2, :], k_[p0:p0 + AD, h // 2, :]
                mm(banks[b][:, 0:P], qh[:, 0:P], kh[:, 0:P], 0, 1, ready, bank_free[b])
                s_tok[h] = mm(banks[b][:, P:3 * P], qh[:, P:T], kh[:, 0:T], 0, 1, signal=True)

            def soft(h):
                i, b = h % NB, h % 4
                slope = 2.0 ** (-8.0 * (h + 1) / AH)
                c = sm[:, 4 * i:4 * i + 4]
                dist = CONST[:, CONST_AT["dist0"]:CONST_AT["dist0"] + 3 * P]
                bank_free[b] = stt(E[i], dist, -slope, banks[b][:, 0:3 * P], ALU.mult, ALU.add, s_tok[h], e_free[i])
                parts = (slice(0, P), slice(P, 3 * P))
                for t, s in enumerate(parts):
                    tok = DV.add(lambda e, t=t, s=s: e.tensor_reduce(c[:, t:t + 1], E[i][:, s], AX.X, ALU.max,
                                                                     negate=True))
                for t, s in enumerate(parts):
                    t2 = act(E[i][:, s], E[i][:, s], ACT.Exp, tok, bias=c[:, t:t + 1], acc=c[:, 2 + t:3 + t])
                DV.add(lambda e: e.reciprocal(c[:, 2:4], c[:, 2:4]), t2)
                for t, s in enumerate(parts):
                    tok = ts(E[i][:, s], E[i][:, s], c[:, 2 + t:3 + t], None, ALU.mult)
                return tok

            o_bank = {}

            def values(h, p_tok):
                i = h % NB
                b = rot()
                e_free[i] = transposes(b, [(n * P, E[i][:, n * P:(n + 1) * P]) for n in range(3)], p_tok)
                bank_free[b] = tok = copy(ET[i], banks[b][:, 0:3 * P], e_free[i], et_free[i], on="A")
                if h % 2 == 0:
                    o_bank[0] = rot()
                b = o_bank[0]
                et_free[i] = attend(b, h, v_, ET[i], tok)
                if h % 2:
                    bank_free[b] = copy(o[:, h // 2, :], banks[b][:, 0:T], et_free[i], on="A")

            for h in range(3):
                scores(h)
            p_tok = {}
            for h in range(AH):
                p_tok[h] = soft(h)
                if h + 3 < AH:
                    scores(h + 3)
                if h:
                    values(h - 1, p_tok[h - 1])
            values(AH - 1, p_tok[AH - 1])
            out_product(A["b_wo"], o, AC.last())
            return residual(2, A["ln_g"][1, 0], A["ln_b"][1, 0])

        def attend(b, h, v_, PT, tok):
            p0 = AD * (h % 2)
            o = banks[b][p0:p0 + AD, :]
            vh = [v_[:, s, h * AD:(h + 1) * AD] for s in range(TT)]
            mm(o[:, 0:P], vh[0], PT[:, 0:P], 0, 1, tok, bank_free[b])
            mm(o[:, P:T], vh[0], PT[:, P:T], 0, 2)
            return mm(o[:, P:T], vh[1], PT[:, T:3 * P], 1, 2, signal=True)

        def normed(gain, layer, x_done):
            xn = arena(TT, D)
            tok = rms(X, xn, x_done)
            return channels(xn, [(HT, lambda k: col(gain, 8 * layer + k), None)], tok)

        def pool_mixer(layer, j, x_done):
            fence()
            h_ready = normed("mix_norm_g_2", layer, x_done)
            pt = arena(KD, T)
            buf = [arena(2, T) for _ in range(2)]
            DV.hold(h_ready)
            for g, win in enumerate(WINDOWS):
                src = cur = HT[:, 2 * g:2 * g + 2, :]
                sh, i = 1, 0
                while sh < win:
                    nxt = buf[i % 2]
                    DV.add(lambda e, nxt=nxt, cur=cur, sh=sh: e.tensor_copy(nxt[:, :, 0:sh], cur[:, :, 0:sh]))
                    tt(nxt[:, :, sh:T], cur[:, :, sh:T], cur[:, :, 0:T - sh], ALU.add)
                    cur, sh, i = nxt, 2 * sh, i + 1
                inv = const("count")[:, g * T:(g + 1) * T].unsqueeze(1).broadcast_to([P, 2, T])
                tt(cur, cur, inv, ALU.mult)
                tok = tt(pt[:, 2 * g:2 * g + 2, :], cur, src, ALU.subtract)
            scale = small(ROWG[:, :], row(A["pool_scale_2"][j]), DV.last())
            n, (w,), arrived = take(A["pool_w_2"][j].rearrange("g (k p) n -> p (g k) n", p=P))
            for t in range(TT):
                for g in range(4):
                    b = 2 * t + g // 2
                    for k in range(2):
                        ready = mm(banks[b][:, (g % 2) * T:(g % 2 + 1) * T], pt[:, 2 * g + k, t * P:(t + 1) * P],
                                   w[:, 2 * g + k, :], k, 2, arrived, tok, bank_free[b], signal=(k == 1))
            give(n, ready)
            for t in range(TT):
                for h in range(2):
                    s = slice(h * 512, (h + 1) * 512)
                    b = 2 * t + h
                    bank_free[b] = tt(RT[:, s], banks[b][:, :], ROWG[:, s], ALU.mult, ready, scale)
                    x_done = tt(X[:, t, s], X[:, t, s], RT[:, s], ALU.add)
            return x_done

        def stick_breaking(layer, x_done):
            fence()
            h_ready = normed("mix_norm_g_2", layer, x_done)
            q, k_, v_, o = arena(KD, T), arena(KD, T), arena(TT, D), arena(KD, T)
            w = A["sb_w_qkv_2"][0]
            ready = project_heads(q, w, 0, AD ** -0.5, HT, h_ready)
            ready += project_heads(k_, w, D, 1.0, HT, h_ready)
            ready += project_values(v_, w, 2 * D, HT, h_ready)
            NB = 3
            SPL, MIN, LS, AT = ([arena(3 * P) for _ in range(NB)] for _ in range(4))
            past = CONST[:, CONST_AT["past0"]:CONST_AT["past0"] + 3 * P]
            s_tok, r_tok, l_free, a_free = {}, {}, [None] * NB, [None] * NB
            o_bank = {}

            def scores(h):
                b = h % 4
                p0 = AD * (h % 2)
                qh, kh = q[p0:p0 + AD, h // 2, :], k_[p0:p0 + AD, h // 2, :]
                mm(banks[b][:, 0:T], kh[:, 0:P], qh, 0, 1, ready, bank_free[b])
                s_tok[h] = mm(banks[b][:, T:3 * P], kh[:, P:T], qh[:, P:T], 0, 1, signal=True)

            def logs(h):
                i, b = h % NB, h % 4
                z = banks[b][:, 0:3 * P]
                act(SPL[i], z, ACT.Abs, s_tok[h], a_free[i])
                tok = act(SPL[i], SPL[i], ACT.Exp, scale=-1.0)
                t1 = act(SPL[i], SPL[i], ACT.Ln, bias=1.0)
                stt(LS[i], z, 0.0, SPL[i], ALU.max, ALU.add, t1, l_free[i])
                r_tok[h] = tt(LS[i], LS[i], past, ALU.mult)
                bank_free[b] = stt(MIN[i], z, 0.0, SPL[i], ALU.min, ALU.subtract)

            def finish_head(h):
                i = h % NB
                b = rot()
                later, negone = const("later"), const("negone")
                mm(banks[b][:, 0:P], later, LS[i][:, 0:P], 0, 1, r_tok[h], bank_free[b])
                mm(banks[b][:, P:T], later, LS[i][:, P:T], 0, 2)
                mm(banks[b][:, P:T], negone, LS[i][:, T:3 * P], 1, 2)
                l_free[i] = mm(banks[b][:, T:3 * P], later, LS[i][:, T:3 * P], 0, 1, signal=True)
                t1 = tt(AT[i], MIN[i], banks[b][:, 0:3 * P], ALU.add, l_free[i], a_free[i])
                bank_free[b] = t1
                t2 = act(AT[i], AT[i], ACT.Exp, t1)
                t3 = tt(AT[i], AT[i], past, ALU.mult, t2)
                if h % 2 == 0:
                    o_bank[0] = rot()
                b = o_bank[0]
                return b, t3

            def put(h, b, tok):
                i = h % NB
                a_free[i] = attend(b, h, v_, AT[i], tok)
                if h % 2:
                    bank_free[b] = copy(o[:, h // 2, :], banks[b][:, 0:T], a_free[i], on="A")

            for h in range(3):
                scores(h)
            for h in range(AH):
                logs(h)
                if h + 3 < AH:
                    scores(h + 3)
                if h:
                    put(h - 1, *finish_head(h - 1))
            put(AH - 1, *finish_head(AH - 1))
            out_product(A["sb_w_o_2"][0], o, AC.last())
            return add_acc()

        def s5(layer, x_done):
            fence()
            h_ready = normed("mix_norm_g_2", layer, x_done)
            PE.hold(h_ready)
            now = fence()
            par = arena(3, NT5)
            br, bi, cr, ci = (arena(NT5, 2 * SC) for _ in range(4))
            got = [small(par, A["s5_par"], now), small(br, A["s5_b_re"], now), small(bi, A["s5_b_im"], now),
                   small(cr, A["s5_c_re"], now), small(ci, A["s5_c_im"], now)]
            tm = [arena(NT5) for _ in range(16)]
            are, aim, ldt = par[:, 0, :], par[:, 1, :], par[:, 2, :]
            dt, x, th, r, cs, sn, er, em, sh, nr, ni, rd, cor, coi, u1, u2 = tm
            AC.hold(got)
            DV.hold(got)
            tok = act(dt, ldt, ACT.Exp)
            tt(x, are, dt, ALU.mult, tok)
            tt(th, aim, dt, ALU.mult)
            ts(u1, th, 1.0 / (2.0 * float(np.pi)), ROUND_MAGIC, ALU.mult, ALU.add)
            ts(u1, u1, -ROUND_MAGIC, None, ALU.add)
            stt(r, u1, -TWO_PI_HI, th, ALU.mult, ALU.add)
            stt(r, u1, -TWO_PI_LO, r, ALU.mult, ALU.add)
            ts(r, r, 3.1415925, -3.1415925, ALU.min, ALU.max)
            stt(u2, r, -1.0, r, ALU.mult, ALU.max)
            tok = ts(u2, u2, -1.0, float(np.pi) / 2, ALU.mult, ALU.add)
            act(er, x, ACT.Exp, tok)
            act(em, x, ACT.Tanh, scale=0.5)
            act(sn, r, ACT.Sin)
            act(sh, r, ACT.Sin, scale=0.5)
            tok = act(cs, u2, ACT.Sin)
            ts(u1, em, -1.0, 1.0, ALU.mult, ALU.add, tok)
            DV.add(lambda e: e.reciprocal(u1, u1))
            stt(em, em, 2.0, u1, ALU.mult, ALU.mult)
            tt(nr, em, cs, ALU.mult)
            tt(sh, sh, sh, ALU.mult)
            stt(nr, sh, -2.0, nr, ALU.mult, ALU.add)
            tt(ni, er, sn, ALU.mult)
            tt(u1, are, are, ALU.mult)
            tt(rd, aim, aim, ALU.mult)
            tt(rd, rd, u1, ALU.add)
            DV.add(lambda e: e.reciprocal(rd, rd))
            tt(cor, nr, are, ALU.mult)
            tt(u1, ni, aim, ALU.mult)
            tt(cor, cor, u1, ALU.add)
            tt(cor, cor, rd, ALU.mult)
            tt(coi, ni, are, ALU.mult)
            tt(u1, nr, aim, ALU.mult)
            tt(coi, coi, u1, ALU.subtract)
            tt(coi, coi, rd, ALU.mult)
            G8 = 8
            CT, ST_ = arena(G8, T), arena(G8, T)
            W1, W2 = arena(G8, P), arena(G8, P)
            wide = lambda v: v.unsqueeze(2).broadcast_to([P, NT5, 2 * SC])
            b1 = W1.rearrange("p a b -> p (a b)").rearrange("p (a b) -> p a b", a=NT5)
            b2 = W2.rearrange("p a b -> p (a b)").rearrange("p (a b) -> p a b", a=NT5)
            tt(b1, br, wide(coi), ALU.mult)
            tt(b2, bi, wide(coi), ALU.mult)
            tt(br, br, wide(cor), ALU.mult)
            tt(br, br, b2, ALU.subtract)
            tt(bi, bi, wide(cor), ALU.mult)
            tt(bi, bi, b1, ALU.add)
            bar_ready = ts(ci, ci, -1.0, None, ALU.mult)
            BT = [arena(KD, P) for _ in range(2)]
            for src, dst in ((br, BT[0]), (bi, BT[1])):
                for k in range(0, KD, 4):
                    b = rot()
                    tok = transposes(b, [(j * P, src[:, 4 * (k + j):4 * (k + j) + 4, :].rearrange("p a b -> p (a b)"))
                                         for j in range(4)], bar_ready)
                    bank_free[b] = bt_ready = copy(dst[:, k:k + 4, :], banks[b][:, :].rearrange(
                        "p (a b) -> p a b", a=4), tok, on="D")
            V = arena(4, T)
            Z = [arena(2, T) for _ in range(2)]
            z_free = [None, None]
            DV.hold(h_ready)
            yb = None
            for i in range(NT5):
                if i % G8 == 0:
                    c8, s8 = cs[:, i:i + G8].unsqueeze(2), sn[:, i:i + G8].unsqueeze(2)
                    DV.add(lambda e, c8=c8: e.tensor_copy(CT[:, :, 0:1], c8))
                    DV.add(lambda e, s8=s8: e.tensor_copy(ST_[:, :, 0:1], s8))
                    n = 1
                    while n < T:
                        cn = CT[:, :, n - 1:n].broadcast_to([P, G8, n])
                        sn_ = ST_[:, :, n - 1:n].broadcast_to([P, G8, n])
                        lo, hi = slice(0, n), slice(n, 2 * n)
                        tt(W1[:, :, lo], ST_[:, :, lo], sn_, ALU.mult)
                        tt(W2[:, :, lo], ST_[:, :, lo], cn, ALU.mult)
                        tt(ST_[:, :, hi], CT[:, :, lo], sn_, ALU.mult)
                        tt(CT[:, :, hi], CT[:, :, lo], cn, ALU.mult)
                        tt(CT[:, :, hi], CT[:, :, hi], W1[:, :, lo], ALU.subtract)
                        tt(ST_[:, :, hi], ST_[:, :, hi], W2[:, :, lo], ALU.add)
                        n *= 2
                ct, st = CT[:, i % G8, :], ST_[:, i % G8, :]
                kt, p0 = i // 4, 32 * (i % 4)
                b = rot()
                for j in range(2):
                    tok = mm(bank2(b)[:, j, :], BT[j][p0:p0 + 32, kt, :], HT[p0:p0 + 32, kt, :], 0, 1,
                             bt_ready, bank_free[b], signal=(j == 1))
                bu = bank2(b)
                two = lambda v: v.unsqueeze(1).broadcast_to([P, 2, T])
                tt(V[:, 0:2, :], bu, two(ct), ALU.mult, tok)
                bank_free[b] = tt(V[:, 2:4, :], bu, two(st), ALU.mult)
                tt(V[:, 0, :], V[:, 0, :], V[:, 3, :], ALU.add)
                tt(V[:, 1, :], V[:, 1, :], V[:, 2, :], ALU.subtract)
                for j in range(2):
                    DV.add(lambda e, j=j, i=i: e.tensor_tensor_scan(
                        V[:, 2 + j, :], er[:, i:i + 1].broadcast_to([P, T]), V[:, j, :], 0.0, ALU.mult, ALU.add))
                z = Z[i % 2]
                tt(z, V[:, 2:4, :], two(ct), ALU.mult, z_free[i % 2])
                tt(V[:, 0:2, :], V[:, 2:4, :], two(st), ALU.mult)
                tt(z[:, 0, :], z[:, 0, :], V[:, 1, :], ALU.subtract)
                ztok = tt(z[:, 1, :], z[:, 1, :], V[:, 0, :], ALU.add)
                if i % 4 == 0:
                    yb = (i // 4) % 2
                o = banks[yb][p0:p0 + 32, 0:T]
                mm(o, cr[:, i, :], z[:, 0, :], 0, 2, ztok, bank_free[yb])
                z_free[i % 2] = mm(o, ci[:, i, :], z[:, 1, :], 1, 2, signal=True)
                if i % 4 == 3:
                    g = MEMG[:, kt, :]
                    bank_free[yb] = stt(g, HT[:, kt, :], col("s5_d_2", kt), banks[yb][:, 0:T], ALU.mult, ALU.add,
                                        z_free[i % 2])
                    gtok = act(g, g, ACT.Gelu_apprx_tanh, bank_free[yb])
            for h in range(2):
                nv, (wv,), av = take(cols_of(A["s5_w_glu_2"][0], h * 512, 512))
                ng, (wg,), ag = take(cols_of(A["s5_w_glu_2"][0], D + h * 512, 512))
                for t in range(TT):
                    bv, bg = rot(), rot()
                    for b, w, a, n in ((bv, wv, av, nv), (bg, wg, ag, ng)):
                        for k in range(KD):
                            tok = mm(banks[b][:, :], MEMG[:, k, t * P:(t + 1) * P], w[:, k, :], k, KD,
                                     a, gtok, bank_free[b], signal=(k == KD - 1))
                        give(n, tok)
                    rt = RT[:, 512 * (t % 2):512 * (t % 2) + 512]
                    bank_free[bg] = act(rt, banks[bg][:, :], ACT.Sigmoid, tok, DV.last())
                    bank_free[bv] = tt(rt, rt, banks[bv][:, :], ALU.mult, bank_free[bg])
                    s = slice(h * 512, (h + 1) * 512)
                    x_done = tt(X[:, t, s], X[:, t, s], rt, ALU.add)
            return x_done

        def cross(layer, x_done):
            fence()
            h_ready = normed("xa_norm_g_2", layer, x_done)
            for k in range(KD):
                m_ready = ts(MEMG[:, k, :], MEMN[:, k, :], col("mem_norm_g_2", 8 * layer + k), None, ALU.mult)
            q, k_, v_, o = arena(KD, T), arena(KD, T), arena(TT, D), arena(KD, T)
            E, ET, sm = arena(XH, TT, T), [arena(2, T) for _ in range(2)], arena(4 * XH)
            ready = project_heads(k_, A["xa_wkv_2"][layer], 0, 1.0, MEMG, m_ready)
            vready = project_values(v_, A["xa_wkv_2"][layer], D, MEMG, m_ready)
            ready += project_heads(q, A["xa_wq_2"][layer], 0, XD ** -0.5, HT, h_ready)
            s_tok, p_tok, et_free = {}, {}, [None, None]
            for h in range(XH):
                for t in range(TT):
                    for c in range(2):
                        s_tok[h] = mm(banks[h][:, t * T:(t + 1) * T], q[:, 2 * h + c, t * P:(t + 1) * P],
                                      k_[:, 2 * h + c, :], c, 2, ready, bank_free[h], signal=(c == 1))
            for h in range(XH):
                c = sm[:, 4 * h:4 * h + 4]
                tok = DV.add(lambda e, h=h, c=c: e.tensor_reduce(c[:, 0:2], bank2(h), AX.X, ALU.max, negate=True),
                             s_tok[h])
                for t in range(TT):
                    t2 = act(E[:, h, t, :], bank2(h)[:, t, :], ACT.Exp, tok, bias=c[:, t:t + 1],
                             acc=c[:, 2 + t:3 + t])
                bank_free[h] = t2
                DV.add(lambda e, c=c: e.reciprocal(c[:, 2:4], c[:, 2:4]), t2)
                p_tok[h] = tt(E[:, h, :, :], E[:, h, :, :], c[:, 2:4].unsqueeze(2).broadcast_to([P, TT, T]), ALU.mult)
            for h in range(XH):
                b = rot()
                tok = transposes(b, [((m * 2 + t) * P, E[:, h, t, m * P:(m + 1) * P])
                                     for m in range(2) for t in range(TT)], p_tok[h])
                bank_free[b] = tok = copy(ET[h % 2], bank2(b), tok, et_free[h % 2], on="A")
                b = rot()
                for d in range(2):
                    for m in range(2):
                        t2 = mm(bank2(b)[:, d, :], v_[:, m, h * XD + d * P:h * XD + (d + 1) * P], ET[h % 2][:, m, :],
                                m, 2, tok, vready, bank_free[b], signal=(m == 1))
                et_free[h % 2] = t2
                bank_free[b] = copy(o[:, 2 * h:2 * h + 2, :], bank2(b), t2, on="A")
            out_product(A["xa_wo_2"][layer], o, AC.last())
            return add_acc()

        def ffn(layer, x_done):
            fence()
            h_ready = normed("ffn_norm_g_2", layer, x_done)
            hid = arena(KF, T)
            U = [arena(2, 2 + T) for _ in range(4)]
            CV = [arena(2, T) for _ in range(2)]
            for u in U:
                DV.add(lambda e, u=u: e.memset(u[:, :, 0:2], 0.0))
            w_up, w_dn = A["ffn_w_up_2"][layer], A["ffn_w_down_2"][layer]
            u_free, cv_free, hid_tok = [None] * 4, [None] * 2, {}

            def conv(dst, u, c, *waits):
                w = lambda j: col("ffn_conv_w_2", (layer * 3 + j) * 2 * KF + c)
                ts(dst, u[:, 2:2 + T], w(2), col("ffn_conv_b_2", layer * 2 * KF + c), ALU.mult, ALU.add, *waits)
                stt(dst, u[:, 1:1 + T], w(1), dst, ALU.mult, ALU.add)
                return stt(dst, u[:, 0:T], w(0), dst, ALU.mult, ALU.add)

            def up(s):
                n, (wv, wg), arrived = take(cols_of(w_up, s * 256, 256), cols_of(w_up, FF + s * 256, 256))
                i = s % 2

                def evac(u, dst, c0, cv):
                    def f(_, b, tok):
                        t1 = copy(U[u][:, :, 2:2 + T], bank2(b), tok, u_free[u], on="A")
                        for j in range(2):
                            t2 = conv(dst[:, j, :], U[u][:, j, :], c0 + j, t1, cv)
                        u_free[u] = t2
                        return t1
                    return f

                to_channels(wg, HT, KD, 2, evac(2 * i + 1, CV[i], KF + 2 * s, cv_free[i]), [arrived, h_ready])
                t3 = act(CV[i], CV[i], ACT.Silu, u_free[2 * i + 1])
                give(n, to_channels(wv, HT, KD, 2, evac(2 * i, hid[:, 2 * s:2 * s + 2, :], 2 * s, None), [arrived]))
                hid_tok[s] = cv_free[i] = tt(hid[:, 2 * s:2 * s + 2, :], hid[:, 2 * s:2 * s + 2, :], CV[i],
                                             ALU.mult, t3)

            nd = -(-KF // 4)

            def down(d):
                nk = min(4, KF - 4 * d)
                n, (w,), arrived = take(rows_of(w_dn, 4 * d, nk))
                give(n, to_tokens(w, hid, nk, d == 0, d == nd - 1,
                                  [arrived, hid_tok[min(2 * d + 1, KF // 2 - 1)]], k0=4 * d))

            for s in range(KF // 2):
                up(s)
                if s >= 2 and s % 2 == 0:
                    down(s // 2 - 1)
            down(nd - 1)
            return add_acc()

        fence()
        x_done = mlstm()
        steps = []
        if upto >= 1:
            x_done = moe(0, x_done)
        if upto >= 2:
            x_done = moba(x_done)
        if upto >= 3:
            x_done = moe(1, x_done)
        if upto >= 4:
            now = fence()
            mem = arena(TT, D)
            got = small(mem, A["mem_2"].rearrange("(t p) n -> p t n", p=P), now)
            tok = rms(mem, mem, got)
            DV.hold(PE.last())
            m_ready = channels(mem, [(MEMN, lambda k: 1.0, None)], tok)
            AC.hold(m_ready)
            DV.hold(m_ready)
            for layer in range(DEPTH2):
                if upto < 5 + 3 * layer:
                    break
                if layer % 3 == 0:
                    x_done = pool_mixer(layer, layer // 3, x_done)
                elif layer % 3 == 1:
                    x_done = stick_breaking(layer, x_done)
                else:
                    x_done = s5(layer, x_done)
                if upto >= 6 + 3 * layer:
                    x_done = cross(layer, x_done)
                if upto >= 7 + 3 * layer:
                    x_done = ffn(layer, x_done)
        if upto >= 99:
            g_ready = small(ROWG[:, :], row(A["final_norm_g_2"]), DV.last())
            x_done = rms(X, X, x_done)
            for t in range(TT):
                x_done = tt(X[:, t, :], X[:, t, :], ROWG[:, :], ALU.mult, g_ready)
        done = small(out.rearrange("(t p) n -> p t n", p=P), X[:, :, :], x_done)
        ML.hold(done)

        block = ctx.enter_context(nc.Block())

        @block.sync
        def _(eng):
            LD.run(eng)

        @block.gpsimd
        def _(eng):
            ML.run(eng)

        @block.tensor
        def _(eng):
            PE.run(eng)

        @block.vector
        def _(eng):
            DV.run(eng)

        @block.scalar
        def _(eng):
            AC.run(eng)


def host_layout(inputs, np):
    f = lambda name: np.asarray(inputs[name])
    cols = np.zeros((P, NCOLS), np.float32)
    for name, n in COLS:
        if name in ("bi", "bf"):
            b = f("a_b_if")[0]
            cols[0:MH, COL_AT[name]] = b[0:MH] if name == "bi" else b[MH:]
        else:
            cols[:, COL_AT[name]:COL_AT[name] + n] = f(name).reshape(n, P).T
    states = lambda a: a.reshape(NT5, 2, SP).transpose(1, 2, 0).reshape(P, NT5)

    def blocks(a):
        o = np.zeros((2, SP, NT5, 2, SC), np.float32)
        for g in range(2):
            o[g, :, :, g, :] = a[g::2].transpose(1, 0, 2)
        return o.reshape(P, NT5, 2 * SC)

    out = {
        "consts": constants(), "cols": cols,
        "x": f("x")[0], "xT": f("x")[0].T, "mem_2": f("mem_2")[0],
        "s5_par": np.stack([states(f("s5_a_re_2")[0]), states(f("s5_a_im_2")[0]),
                            states(np.broadcast_to(f("s5_log_dt_2")[0][:, None], (SG, SP)))], axis=1),
        "s5_b_re": blocks(f("s5_b_re_2")[0]), "s5_b_im": blocks(f("s5_b_im_2")[0]),
        "s5_c_re": blocks(f("s5_c_re_2")[0].transpose(0, 2, 1)),
        "s5_c_im": blocks(f("s5_c_im_2")[0].transpose(0, 2, 1)),
        "a_w_in": f("a_w_in")[0], "a_wq": f("a_wq")[0], "a_wk": f("a_wk")[0], "a_wv": f("a_wv")[0],
        "a_w_if": f("a_w_if")[0], "a_w_out": f("a_w_out")[0], "b_wq": f("b_wq")[0], "b_wo": f("b_wo")[0],
    }
    for name in ("w_ada", "b_ada", "ln_g", "ln_b", "b_w_kv", "moe_w_router", "moe_b_router", "moe_w_gate",
                 "moe_w_up", "moe_w_down", "pool_w_2", "pool_scale_2", "sb_w_qkv_2", "sb_w_o_2", "s5_w_glu_2",
                 "xa_wq_2", "xa_wkv_2", "xa_wo_2", "ffn_w_up_2", "ffn_w_down_2", "final_norm_g_2"):
        out[name] = f(name)
    return out


def kernel(**inputs):
    import concourse.bacc as bacc
    from concourse.bass_utils import run_bass_kernel_spmd

    nc = bacc.Bacc("TRN2", target_bir_lowering=False, num_devices=1)
    arrays, args = {}, {}
    for name, a in host_layout(inputs, np).items():
        a = np.ascontiguousarray(a)
        arrays[f"in_{name}"] = a
        args[name] = nc.dram_tensor(f"in_{name}", a.shape, mybir.dt.from_np(a.dtype), kind="ExternalInput").ap()
    out = nc.dram_tensor("out_0", (T, D), F32, kind="ExternalOutput").ap()
    build(nc, args, out, UPTO)
    r = run_bass_kernel_spmd(nc, [arrays], core_ids=[0])
    return r.results[0]["out_0"].reshape(1, T, D)


UPTO = 99
```

```python
from contextlib import ExitStack

import numpy as np

import concourse.bass as bass
from concourse import mybir

F32 = mybir.dt.float32
F32R = mybir.dt.float32r
ALU = mybir.AluOpType
ACT = mybir.ActivationFunctionType
AX = mybir.AxisListType

P = 128
T = 256
TT = T // P
D = 1024
KD = D // P
DEPTH = 2
ALPHA = (2.0 * DEPTH) ** 0.25
LN_EPS = 1e-5
RMS_EPS = 1e-6
MH = 4
MI = 2 * D
MD = MI // MH
AH = 16
AD = D // AH
NE = 16
NG = 4
EG = NE // NG
FE = 512
DEPTH2 = 4
WINDOWS = (2, 4, 8, 16)
SG = 64
SP = 64
SC = D // SG
NT5 = SG // 2
XH = 4
XD = D // XH
FF = ((8 * D // 3 + 127) // 128) * 128
KF = FF // P
NSLOT = 5
NSPLIT = 3
NARENA = 16900
SLOT = 2048
NEG = 1e30
TWO_PI_HI = 6.28125
TWO_PI_LO = 2.0 * float(np.pi) - 6.28125
ROUND_MAGIC = 12582912.0


COLS = [("c", 8), ("b_ada", 112), ("a_conv_w", 64), ("a_conv_b", 16), ("a_gn_g", 16), ("a_skip", 16),
        ("bi", 1), ("bf", 1), ("mem_norm_g_2", 32), ("s5_d_2", 8), ("ffn_conv_w_2", 3 * DEPTH2 * 2 * KF),
        ("ffn_conv_b_2", DEPTH2 * 2 * KF)]
COL_AT = {}
NCOLS = 0
for _name, _n in COLS:
    COL_AT[_name] = NCOLS
    NCOLS += _n

CONSTS = [("ident", 128), ("dist0", 128), ("dist1", 256), ("causal", 128), ("later", 128), ("negone", 128),
          ("ones", 128), ("past0", 256), ("past1", 128), ("count", 4 * T), ("prio16", 16), ("prio4", 4)]
CONST_AT = {}
NCONST = 0
for _name, _n in CONSTS:
    CONST_AT[_name] = NCONST
    NCONST += _n


def constants():
    out = np.zeros((P, NCONST), np.float32)
    i, j = np.arange(P)[:, None], np.arange(T)[None, :]

    def put(name, v):
        out[:, CONST_AT[name]:CONST_AT[name] + v.shape[1]] = v

    put("ident", np.eye(P, dtype=np.float32))
    put("dist0", np.where(j[:, :P] <= i, i - j[:, :P], NEG))
    put("dist1", np.where(j <= i + P, i + P - j, NEG))
    put("causal", np.where(j[:, :P] <= i, 0.0, -NEG))
    put("later", np.where(i > j[:, :P], -1.0, 0.0))
    put("negone", -np.ones((P, P)))
    put("ones", np.ones((P, P)))
    put("past0", np.where(i < j, 1.0, 0.0))
    put("past1", np.where(i < j[:, :P], 1.0, 0.0))
    cnt = np.stack([1.0 / np.minimum(np.arange(1, T + 1), w) for w in WINDOWS]).reshape(1, -1)
    put("count", np.broadcast_to(cnt, (P, 4 * T)))
    put("prio16", np.broadcast_to(np.arange(16, 0, -1.0), (P, 16)))
    put("prio4", np.broadcast_to(np.arange(4, 0, -1.0), (P, 4)))
    return out


class Queue:

    def __init__(self, sem, chained):
        self.sem, self.chained, self.steps, self.count = sem, chained, [], 0

    def add(self, emit, *waits, signal=True):
        self.steps.append((waits, emit, signal))
        if signal:
            self.count += 1
        return (self.sem, self.count)

    def hold(self, *waits):
        self.steps.append((waits, None, False))

    def last(self):
        return (self.sem, self.count)

    def run(self, eng):
        met, done = {}, 0

        def wait(w):
            if w is None:
                return
            if isinstance(w, list):
                for x in w:
                    wait(x)
                return
            sem, value = w() if callable(w) else w
            if value > 0 and met.get(id(sem), 0) < value:
                met[id(sem)] = value
                eng.wait_ge(sem, value)

        for waits, emit, signal in self.steps:
            if self.chained:
                wait((self.sem, done))
            wait(list(waits))
            if emit is None:
                continue
            ins = emit(eng)
            if signal:
                ins.then_inc(self.sem, 1)
                done += 1


class Split:

    def __init__(self, hi, lo):
        self.hi, self.lo = hi, lo

    def __getitem__(self, key):
        return Split(self.hi[key], self.lo[key])


def build(nc, A, out, upto, plan=None):
    ctx = ExitStack()
    with ctx:
        def sb(name, shape):
            return ctx.enter_context(nc.sbuf_tensor(name, shape, F32))

        nsem = [0]

        def sem(name):
            nsem[0] += 1
            return ctx.enter_context(nc.semaphore(name))

        ring = [sb(f"ring{i}", [P, SLOT]) for i in range(NSLOT)]
        parts = [ctx.enter_context(nc.sbuf_tensor(f"parts{i}", [P, 2, SLOT], F32R)) for i in range(NSPLIT)]
        X = sb("X", [P, TT, D])
        CONST = sb("CONST", [P, NCONST])
        COL = sb("COL", [P, NCOLS])
        SHARED = sb("SHARED", [P, 4096])
        ROWG = sb("ROWG", [P, D])
        ROWB = sb("ROWB", [P, D])
        MOD = sb("MOD", [P, 112])
        WR = sb("WR", [P, KD, NE])
        BR = sb("BR", [P, NE])
        WIF = sb("WIF", [P, MI // P, 2 * MH])
        CSIL = sb("CSIL", [P, KD])
        STAT = sb("STAT", [P, 64])
        with nc.sbuf_tensor("ARENA_R", [P, NARENA], F32R) as ARENA_R:
            pass
        ARENA = sb("ARENA", [P, NARENA])
        RT = sb("RT", [P, D])
        GATE = SHARED[:, :].rearrange("p (g n) -> p g n", g=4)
        MEMN = SHARED[:, 0:2048].rearrange("p (k t) -> p k t", k=KD)
        MEMG = SHARED[:, 2048:4096].rearrange("p (k t) -> p k t", k=KD)
        banks = [ctx.enter_context(nc.psum_tensor(f"bank{i}", [P, 512], F32)) for i in range(8)]

        PE = Queue(sem("pe_done"), False)
        DV = Queue(sem("vector_done"), True)
        AC = Queue(sem("scalar_done"), True)
        LD = Queue(sem("weights_queue"), False)
        ML = Queue(sem("misc_queue"), False)

        def const(name, n=None):
            a = CONST_AT[name]
            return CONST[:, a:a + (n or dict(CONSTS)[name])]

        def col(name, j=0, n=1):
            a = COL_AT[name] + j
            return COL[:, a:a + n]

        ident = const("ident")
        arena_at = [0]

        def fence():
            arena_at[0] = 0
            now = [PE.last(), DV.last(), AC.last()]
            DV.hold(now)
            AC.hold(now)
            return now

        def arena(*shape, at=None, whole=None):
            n = int(np.prod(shape))
            a = arena_at[0] if at is None else at
            if at is None:
                arena_at[0] += n
            assert arena_at[0] <= NARENA, arena_at[0]
            v = (ARENA if whole is None else whole)[:, a:a + n]
            if len(shape) == 2:
                v = v.rearrange("p (a b) -> p a b", a=shape[0])
            elif len(shape) == 3:
                v = v.rearrange("p (a b c) -> p a b c", a=shape[0], b=shape[1])
            return v

        def arena2(*shape, at=None):
            n = int(np.prod(shape))
            return Split(arena(*shape, at=at, whole=ARENA_R),
                         arena(*shape, at=None if at is None else at + n, whole=ARENA_R))

        slot_sem = [sem(f"slot{i}") for i in range(NSLOT)]
        units = []
        raw_free, part_free, part_ready = {}, {}, {}
        split_no = {}
        pending = [0]

        def raw_view(n, src):
            return ring[n % NSLOT][:, 0:src.shape[1] * src.shape[2]]

        def split_unit(n):
            src, _ = plan[n]
            m = split_no[n] = len(split_no)
            w, p = raw_view(n, src), parts[m % NSPLIT]
            size = w.shape[1]
            t = AC.add(lambda e: e.copy(p[:, 0, 0:size], w), (slot_sem[n % NSLOT], 16 * (n // NSLOT + 1)),
                       part_free.get(m - NSPLIT))
            raw_free[n] = part_ready[n] = DV.add(
                lambda e: e.tensor_tensor(p[:, 1, 0:size], w, p[:, 0, 0:size].bitcast(F32), ALU.subtract), t)

        def take(src, split=True):
            n = len(units)
            units.append((src, split))
            k = src.shape[1]
            dst = raw_view(n, src)
            freed = (lambda: raw_free[n - NSLOT]) if n >= NSLOT else None
            LD.add(lambda e: e.dma_start(dst.rearrange("p (k n) -> p k n", k=k), src)
                   .then_inc(slot_sem[n % NSLOT], 16), freed, signal=False)
            if plan is not None:
                while pending[0] <= min(n + NSPLIT - 1, len(plan) - 1):
                    if plan[pending[0]][1]:
                        split_unit(pending[0])
                    pending[0] += 1
            if not split:
                return n, dst.rearrange("p (k n) -> p k n", k=k), (slot_sem[n % NSLOT], 16 * (n // NSLOT + 1))
            p = parts[split_no.get(n, 0) % NSPLIT]
            v = [p[:, i, 0:dst.shape[1]].rearrange("p (k n) -> p k n", k=k) for i in range(2)]
            return n, Split(*v), part_ready.get(n)

        def give(n, token):
            if units[n][1]:
                part_free[split_no.get(n, 0)] = token
            else:
                raw_free[n] = token

        def cols_of(w, c0, n):
            return w[:, c0:c0 + n].rearrange("(k p) n -> p k n", p=P)

        def rows_of(w, k0, nk):
            return w[k0 * P:(k0 + nk) * P, :].rearrange("(k p) n -> p k n", p=P)

        def small(dst, src, *waits):
            s = sem(f"small{nsem[0]}")
            ML.add(lambda e: e.dma_start(dst, src).then_inc(s, 16), *waits, signal=False)
            return (s, 16)

        def row(v):
            return v.rearrange("(a n) -> a n", a=1).broadcast_to([P, v.shape[0]])

        bank_free = [None] * 8
        turn = [0]

        def rot():
            turn[0] = (turn[0] + 1) % 4
            return 4 + turn[0]

        def mm(o, l, r, k, K, *waits, signal=False):
            if isinstance(l, Split):
                PE.add(lambda e: e.matmul(o, l.hi, r.hi, start=(k == 0), stop=False), *waits, signal=False)
                PE.add(lambda e: e.matmul(o, l.hi, r.lo, start=False, stop=False), signal=False)
                return PE.add(lambda e: e.matmul(o, l.lo, r.hi, start=False, stop=(k == K - 1)), signal=signal)
            return PE.add(lambda e: e.matmul(o, l, r, start=(k == 0), stop=(k == K - 1)), *waits, signal=signal)

        def transposes(b, pairs, *waits):
            for n, (at, src) in enumerate(pairs):
                m, w = src.shape[0], src.shape[1]
                o = banks[b][0:w, at:at + m]
                tok = PE.add(lambda e, o=o, src=src, m=m: e.transpose(o, src, ident[0:m, 0:m]),
                             *((list(waits) + [bank_free[b]]) if n == 0 else ()), signal=(n == len(pairs) - 1))
            return tok

        flip = [0]

        def affine(o, i, scale, bias, *waits, on=None):
            if on is None:
                flip[0] ^= 1
                on = "AD"[flip[0]]
            if on == "A":
                return AC.add(lambda e: e.activation(o, i, ACT.Identity, bias=0.0 if bias is None else bias,
                                                     scale=scale), *waits)
            if bias is None:
                return DV.add(lambda e: e.tensor_scalar(o, i, scale, None, ALU.mult), *waits)
            return DV.add(lambda e: e.tensor_scalar(o, i, scale, bias, ALU.mult, ALU.add), *waits)

        def copy(o, i, *waits, on=None):
            if on is None:
                flip[0] ^= 1
                on = "AD"[flip[0]]
            if on == "A":
                return AC.add(lambda e: e.copy(o, i), *waits)
            return DV.add(lambda e: e.tensor_copy(o, i), *waits)

        def tt(o, a, b, op, *waits):
            return DV.add(lambda e: e.tensor_tensor(o, a, b, op), *waits)

        def ts(o, a, s1, s2, op0, op1=None, *waits):
            if s2 is None:
                return DV.add(lambda e: e.tensor_scalar(o, a, s1, None, op0), *waits)
            return DV.add(lambda e: e.tensor_scalar(o, a, s1, s2, op0, op1), *waits)

        def stt(o, a, s, b, op0, op1, *waits, acc=None):
            if acc is None:
                return DV.add(lambda e: e.scalar_tensor_tensor(o, a, s, b, op0, op1), *waits)
            return DV.add(lambda e: e.scalar_tensor_tensor(o, a, s, b, op0, op1, accum_out=acc), *waits)

        def act(o, i, f, *waits, bias=0.0, scale=1.0, acc=None):
            return AC.add(lambda e: e.activation(o, i, f, bias=bias, scale=scale, accum_out=acc), *waits)

        def bank2(b):
            return banks[b][:, :].rearrange("p (a t) -> p a t", a=2)

        def to_channels(w, src, nk, n_out, evac, ready, n0=0):
            tok = None
            for n in range(0, n_out, 2):
                b = rot()
                for j in range(min(2, n_out - n)):
                    for k in range(nk):
                        tok = mm(bank2(b)[:, j, :], w[:, k, (n + j) * P:(n + j + 1) * P], src[:, k, :], k, nk,
                                 *([ready, bank_free[b]] if j == 0 and k == 0 else []),
                                 signal=(k == nk - 1))
                bank_free[b] = evac(n0 + n, b, tok)
            return tok

        acc_tok = {}

        def to_tokens(w, src, nk, first, last, ready, k0=0):
            tok = None
            for t in range(TT):
                for h in range(2):
                    b = 2 * t + h
                    for k in range(nk):
                        fresh, end = first and k == 0, last and k == nk - 1
                        tok = mm(banks[b][:, :], src[:, k0 + k, t * P:(t + 1) * P], w[:, k, h * 512:(h + 1) * 512],
                                 0 if fresh else 1, 2 if end else 9,
                                 *([ready] + ([bank_free[b]] if fresh else []) if k == 0 else []),
                                 signal=(k == nk - 1))
                    acc_tok[b] = tok
            return tok

        def split_out(dst, src, scale, *waits):
            t = act(dst.hi, src, ACT.Identity, *waits, scale=scale)
            return stt(dst.lo, src, scale, dst.hi.bitcast(F32), ALU.mult, ALU.subtract, t, *waits)

        def stats(t, *waits):
            bn = STAT[:, 8 + 12 * t:20 + 12 * t].rearrange("p (a b) -> p a b", a=2)
            for h in range(2):
                DV.add(lambda e, h=h: e.bn_stats(bn[:, h, :], X[:, t, h * 512:(h + 1) * 512]), *waits)
            return DV.add(lambda e: e.bn_aggr(STAT[:, 2 * t:2 * t + 2],
                                              STAT[:, 8 + 12 * t:20 + 12 * t].rearrange("p (a b) -> p a b", a=2)))

        def inv_sqrt(o, v, eps, *waits):
            tok = ts(o, v, 1.0, eps, ALU.mult, ALU.add, *waits)
            tok = act(o, o, ACT.Sqrt, tok)
            return DV.add(lambda e: e.reciprocal(o, o), tok)

        def layer_norm(t, g_ready):
            tok = stats(t)
            inv_sqrt(STAT[:, 4 + t:5 + t], STAT[:, 2 * t + 1:2 * t + 2], LN_EPS, tok)
            ts(X[:, t, :], X[:, t, :], STAT[:, 2 * t:2 * t + 1], STAT[:, 4 + t:5 + t], ALU.subtract, ALU.mult)
            tt(X[:, t, :], X[:, t, :], ROWG[:, :], ALU.mult, *g_ready)
            return tt(X[:, t, :], X[:, t, :], ROWB[:, :], ALU.add)

        def rms(src, dst, gain, x_done):
            toks = []
            for t in range(TT):
                c = STAT[:, 32 + t:33 + t]
                tok = act(RT[:, :], src[:, t, :], ACT.Square, x_done[t], DV.last(), acc=c)
                tok = ts(c, c, 1.0 / D, RMS_EPS, ALU.mult, ALU.add, tok)
                tok = act(c, c, ACT.Sqrt, tok)
                DV.add(lambda e, c=c: e.reciprocal(c, c), tok)
                if gain is None:
                    toks.append(ts(dst[:, t, :], src[:, t, :], c, None, ALU.mult))
                else:
                    toks.append(stt(dst[:, t, :], src[:, t, :], c, ROWG[:, :], ALU.mult, ALU.mult, gain))
            return toks

        def channels(src, move, x_done):
            toks = []
            for t in range(TT):
                for k in range(0, KD, 4):
                    b = rot()
                    tok = transposes(b, [(j * P, src[:, t, (k + j) * P:(k + j + 1) * P]) for j in range(4)],
                                     x_done[t])
                    toks.append(move(slice(k, k + 4), slice(t * P, (t + 1) * P),
                                     banks[b][:, :].rearrange("p (a b) -> p a b", a=4), tok))
                    bank_free[b] = toks[-1]
            return toks

        c_ready = small(CONST[:, :], A["consts"])
        col_ready = small(COL[:, :], A["cols"])
        x_ready = small(X[:, :, :], A["x"].rearrange("(t p) n -> p t n", p=P))
        gate_rows = [small(GATE[:, g, :], row(A["b_ada"][(3 * g + 2) * D:(3 * g + 3) * D])) for g in range(4)]
        wif_ready = small(WIF[:, :, :], A["a_w_if"].rearrange("(k p) n -> p k n", p=P))
        wr_ready = small(WR[:, :, :], A["moe_w_router"].rearrange("(k p) n -> p k n", p=P))
        br_ready = small(BR[:, :], row(A["moe_b_router"]))
        DV.add(lambda e: e.memset(STAT[:, :], 0.0))
        csil_ready = act(CSIL[:, :], col("c", 0, 8), ACT.Silu, col_ready)
        DV.hold(c_ready, col_ready)
        AC.hold(c_ready)

        def ada(v):
            gate = v < 12 and v % 3 == 2
            b = rot()
            for h in range(4):
                n, w, arrived = take(cols_of(A["w_ada"], v * D + h * 256, 256), split=False)
                if gate:
                    if h == 2:
                        b = rot()
                    o = bank2(b)[:, h % 2, :]
                    for k in range(KD):
                        tok = mm(o, CSIL[:, k:k + 1].broadcast_to([P, P]), w[:, k, :], k, KD,
                                 arrived, csil_ready, c_ready, bank_free[b], signal=(k == KD - 1))
                    if h % 2:
                        g = GATE[:, v // 3, (h // 2) * 512:(h // 2 + 1) * 512]
                        bank_free[b] = stt(g, banks[b][:, :], 1.0, g, ALU.add, ALU.add, tok, gate_rows[v // 3])
                else:
                    for j in range(2):
                        for k in range(KD):
                            tok = mm(banks[b][:, 2 * h + j:2 * h + j + 1], w[:, k, j * P:(j + 1) * P],
                                     CSIL[:, k:k + 1], k, KD, arrived, csil_ready, c_ready, bank_free[b],
                                     signal=(k == KD - 1))
                give(n, tok)
            if gate:
                return bank_free[b]
            bc = b
            scale = v == 13 or (v < 12 and v % 3 == 1)
            m = MOD[:, 8 * v:8 * v + 8]
            tok = tt(m, banks[bc][:, 0:8], col("b_ada", 8 * v, 8), ALU.add, tok)
            bank_free[bc] = tok
            if scale:
                tok = ts(m, m, 1.0, None, ALU.add)
            return tok

        def shift_of(v):
            return lambda k: MOD[:, 8 * v + k:8 * v + k + 1]

        def residual(g, lng, lnb):
            rows = [small(ROWG[:, :], row(lng), DV.last()), small(ROWB[:, :], row(lnb), DV.last())]
            toks = []
            for t in range(TT):
                for h in range(2):
                    s = slice(h * 512, (h + 1) * 512)
                    b = 2 * t + h
                    o = RT[:, s]
                    tok = tt(o, banks[b][:, :], GATE[:, g, s], ALU.mult, acc_tok[b])
                    bank_free[b] = tok
                    stt(X[:, t, s], X[:, t, s], ALPHA, o, ALU.mult, ALU.add, x_ready)
                toks.append(layer_norm(t, rows))
            return toks

        def modulated(scale, shift, tmp, dst, also=None):
            def one(ks, cs, o, tmp, dst, scale, shift, tok):
                n = ks.stop - ks.start
                wide = lambda v: MOD[:, 8 * v + ks.start:8 * v + ks.stop].unsqueeze(2).broadcast_to([P, n, P])
                got = tt(tmp[:, ks, cs], o, wide(scale), ALU.mult, tok)
                t1 = tt(tmp[:, ks, cs], tmp[:, ks, cs], wide(shift), ALU.add)
                split_out(dst[:, ks, cs], tmp[:, ks, cs], 1.0, t1)
                return got

            def move(ks, cs, o, tok):
                one(ks, cs, o, tmp, dst, scale, shift, tok)
                if also:
                    one(ks, cs, o, *also, tok)
                return DV.last()
            return move

        def mlstm():
            nm = MI // P
            xm = arena(nm, 3 + T)
            xc = arena(nm, T)
            HT = arena(KD, T)
            xt_ready = small(HT, A["xT"].rearrange("(k p) t -> p k t", p=P))
            ada(0)
            ready = ada(1)
            for k in range(KD):
                tok = affine(HT[:, k, :], HT[:, k, :], MOD[:, 8 + k:9 + k], MOD[:, k:k + 1], ready, xt_ready, on="D")
            h_ready = tok
            pad = DV.add(lambda e: e.memset(xm[:, :, 0:3], 0.0))
            xm_ready = {}

            def evac_x(n, b, tok):
                t1 = copy(xm[:, n:n + 2, 3:3 + T], bank2(b), tok, on="A")
                xm_ready[n] = t1
                for c in (n, n + 1):
                    w = lambda j: col("a_conv_w", 16 * j + c)
                    ts(xc[:, c, :], xm[:, c, 3:3 + T], w(3), col("a_conv_b", c), ALU.mult, ALU.add, t1)
                    for j in (2, 1, 0):
                        t2 = stt(xc[:, c, :], xm[:, c, j:j + T], w(j), xc[:, c, :], ALU.mult, ALU.add)
                act(xc[:, n:n + 2, :], xc[:, n:n + 2, :], ACT.Silu, t2)
                return t1

            for s in range(MI // 256):
                n, w, arrived = take(cols_of(A["a_w_in"], s * 256, 256), split=False)
                give(n, to_channels(w, HT, KD, 2, evac_x, [arrived, h_ready, pad], n0=2 * s))
                if s == 3:
                    ada(2)
            xc_ready = AC.last()
            LI, LF, BC, GR, R8 = arena(T), arena(T), arena(T), arena(T), arena(16)
            b = rot()
            for half in range(2):
                for k in range(nm):
                    tok = mm(banks[b][0:MH, half * T:half * T + T], WIF[:, k, half * MH:half * MH + MH], xc[:, k, :],
                             k, nm, xc_ready, wif_ready, bank_free[b], signal=(k == nm - 1))
            ts(LI[0:MH, :], banks[b][0:MH, 0:T], col("bi")[0:MH, :], None, ALU.add, None, tok)
            tok = ts(LF[0:MH, :], banks[b][0:MH, T:2 * T], col("bf")[0:MH, :], None, ALU.add)
            bank_free[b] = tok
            act(GR[0:MH, :], LF[0:MH, :], ACT.Abs, tok)
            act(GR[0:MH, :], GR[0:MH, :], ACT.Exp, scale=-1.0)
            tok = act(GR[0:MH, :], GR[0:MH, :], ACT.Ln, bias=1.0)
            stt(LF[0:MH, :], LF[0:MH, :], 0.0, GR[0:MH, :], ALU.min, ALU.subtract, tok)
            for c in range(2):
                s = slice(c * P, (c + 1) * P)
                DV.add(lambda e, s=s: e.tensor_tensor_scan(BC[0:MH, s], const("ones")[0:MH, :], LF[0:MH, s], 0.0,
                                                           ALU.mult, ALU.add))
            tt(GR[0:MH, :], LI[0:MH, :], BC[0:MH, :], ALU.subtract)
            DV.add(lambda e: e.tensor_reduce(R8[0:MH, 8:9], GR[0:MH, 0:P], AX.X, ALU.max))
            ts(R8[0:MH, 8:9], R8[0:MH, 8:9], 0.0, None, ALU.max)
            tt(R8[0:MH, 9:10], BC[0:MH, P - 1:P], R8[0:MH, 8:9], ALU.add)
            ts(R8[0:MH, 8:9], R8[0:MH, 8:9], -1.0, None, ALU.mult)
            ts(R8[0:MH, 0:4], ident[0:MH, 0:MH], R8[0:MH, 9:10], None, ALU.mult)
            tok = ts(R8[0:MH, 4:8], ident[0:MH, 0:MH], R8[0:MH, 8:9], None, ALU.mult)
            BV = arena(20)
            b = rot()
            mm(banks[b][:, 0:4], BC[0:MH, 0:P], ident[0:MH, 0:MH], 0, 1, tok, bank_free[b])
            mm(banks[b][:, 4:8], BC[0:MH, P:T], ident[0:MH, 0:MH], 0, 1)
            tok = mm(banks[b][:, 8:16], const("ones")[0:MH, :], R8[0:MH, 0:8], 0, 1, signal=True)
            bank_free[b] = copy(BV[:, 0:16], banks[b][:, 0:16], tok, on="D")
            bv_ready = tt(BV[:, 16:20], BV[:, 4:8], BV[:, 8:12], ALU.add)
            q, k_, v = arena(4, T), arena(4, T), arena(TT, MD)
            HH = arena(TT, MD)
            E, S, ST = arena(3 * P), arena(3 * P), arena(3 * P)
            m, bn = arena(16), arena(TT * 6)
            for h in range(MH):
                r = {}

                def evac_to(dst, name, scale):
                    def f(n, b, tok):
                        r[name] = affine(dst[:, n:n + 2, :], bank2(b), scale, None, tok)
                        r.setdefault("all", []).append(r[name])
                        return r[name]
                    return f

                src = xc[:, 4 * h:4 * h + 4, :]
                n, wq, arrived = take(rows_of(A["a_wq"][h], 0, 4), split=False)
                give(n, to_channels(wq, src, 4, 4, evac_to(q, "q", 1.0), [arrived, xc_ready]))
                n, wk, arrived = take(rows_of(A["a_wk"][h], 0, 4), split=False)
                give(n, to_channels(wk, src, 4, 4, evac_to(k_, "k", MD ** -0.5), [arrived]))
                n, wv, arrived = take(rows_of(A["a_wv"][h], 0, 4), split=False)
                for t in range(TT):
                    b = rot()
                    for k in range(4):
                        tok = mm(banks[b][:, :], xm[:, 4 * h + k, 3 + t * P:3 + (t + 1) * P], wv[:, k, :], k, 4,
                                 arrived, bank_free[b], signal=(k == 3))
                    bank_free[b] = copy(v[:, t, :], banks[b][:, :], tok)
                    r["all"].append(bank_free[b])
                give(n, tok)
                bg, bs = rot(), rot()
                gtok = mm(banks[bg][:, 0:T], ident[0:MH, h:h + 1].broadcast_to([MH, P]), GR[0:MH, :], 0, 1,
                          bank_free[bg], signal=True)
                for n, (tq, tk) in enumerate(((0, 0), (1, 1), (1, 0))):
                    for k in range(4):
                        stok = mm(banks[bs][:, n * P:(n + 1) * P], q[:, k, tq * P:(tq + 1) * P],
                                  k_[:, k, tk * P:(tk + 1) * P], k, 4, r["all"], bank_free[bs], signal=(k == 3))
                for c in range(2):
                    bcol = BV[:, 4 * c + h:4 * c + h + 1]
                    d = E[:, c * P:(c + 1) * P]
                    stt(d, banks[bg][:, c * P:(c + 1) * P], bcol, const("causal"), ALU.add, ALU.add, gtok, bv_ready)
                    DV.add(lambda e, c=c, d=d: e.tensor_reduce(m[:, c:c + 1], d, AX.X, ALU.max))
                    a = bcol if c == 0 else BV[:, 16 + h:17 + h]
                    tt(m[:, c:c + 1], m[:, c:c + 1], a, ALU.max)
                mtok = ts(m[:, 2:4], m[:, 0:2], -1.0, None, ALU.mult)
                for c in range(2):
                    act(E[:, c * P:(c + 1) * P], E[:, c * P:(c + 1) * P], ACT.Exp, mtok, bias=m[:, 2 + c:3 + c])
                bank_free[bg] = act(E[:, 2 * P:3 * P], banks[bg][:, 0:P], ACT.Exp, bias=BV[:, 12 + h:13 + h])
                act(m[:, 4:5], BV[:, 16 + h:17 + h], ACT.Exp, bias=m[:, 3:4])
                etok = act(m[:, 5:7], m[:, 2:4], ACT.Exp)
                for n, (sc, ac) in enumerate(((1.0, 7), (1.0, 8), (m[:, 4:5], 9))):
                    tok = stt(S[:, n * P:(n + 1) * P], banks[bs][:, n * P:(n + 1) * P], sc, E[:, n * P:(n + 1) * P],
                              ALU.mult, ALU.mult, etok, stok, acc=m[:, ac:ac + 1])
                bank_free[bs] = sw = tok
                tt(m[:, 8:9], m[:, 8:9], m[:, 9:10], ALU.add)
                stt(m[:, 10:12], m[:, 7:9], -1.0, m[:, 7:9], ALU.mult, ALU.max)
                tt(m[:, 10:12], m[:, 10:12], m[:, 5:7], ALU.max)
                rtok = DV.add(lambda e: e.reciprocal(m[:, 10:12], m[:, 10:12]))
                b = rot()
                tok = transposes(b, [(n * P, S[:, n * P:(n + 1) * P]) for n in range(3)], sw)
                bank_free[b] = st = copy(ST[:, :], banks[b][:, 0:3 * P], tok, on="A")
                for t in range(TT):
                    b = rot()
                    for k in range(t + 1):
                        blk = (0, 1)[t] if k == 0 else 2
                        src_v = v[:, (0, 1)[t] if k == 0 else 0, :]
                        tok = mm(banks[b][:, :], ST[:, blk * P:(blk + 1) * P], src_v, k, t + 1, st, bank_free[b],
                                 signal=(k == t))
                    htok = ts(HH[:, t, :], banks[b][:, :], m[:, 10 + t:11 + t], None, ALU.mult, None, tok, rtok)
                    bank_free[b] = htok
                    DV.add(lambda e, t=t: e.bn_stats(bn[:, 6 * t:6 * t + 6], HH[:, t, :]))
                    DV.add(lambda e, t=t: e.bn_aggr(m[:, 12 + 2 * t:14 + 2 * t], bn[:, 6 * t:6 * t + 6]))
                mv = m[:, 12:16].rearrange("p (t c) -> p t c", t=2)
                inv_sqrt(m[:, 10:12], mv[:, :, 1], LN_EPS, DV.last())
                for t in range(TT):
                    htok = ts(HH[:, t, :], HH[:, t, :], m[:, 12 + 2 * t:13 + 2 * t], m[:, 10 + t:11 + t],
                              ALU.subtract, ALU.mult)
                for c in range(4):
                    ts(xc[:, 4 * h + c, :], xc[:, 4 * h + c, :], col("a_skip", 4 * h + c), None, ALU.mult, None, stok)
                for c in range(0, 4, 2):
                    b = rot()
                    tok = transposes(b, [((j * 2 + t) * P, HH[:, t, (c + j) * P:(c + j + 1) * P])
                                         for j in range(2) for t in range(TT)], htok)
                    for j in range(2):
                        ch = 4 * h + c + j
                        tok2 = stt(xc[:, ch, :], bank2(b)[:, j, :], col("a_gn_g", ch), xc[:, ch, :],
                                   ALU.mult, ALU.add, tok)
                    bank_free[b] = tok2


            z_free = [None, None]

            def evac_z(n, b, tok):
                i = (n // 2) % 2
                z = RT[:, 512 * i:512 * i + 512].rearrange("p (a t) -> p a t", a=2)
                t1 = act(z, bank2(b), ACT.Silu, tok, z_free[i])
                z_free[i] = tt(xc[:, n:n + 2, :], xc[:, n:n + 2, :], z, ALU.mult, t1)
                return t1

            for s in range(MI // 256):
                n, w, arrived = take(cols_of(A["a_w_in"], MI + s * 256, 256), split=False)
                give(n, to_channels(w, HT, KD, 2, evac_z, [arrived], n0=2 * s))
            zr = DV.last()
            for s in range(8):
                n, w, arrived = take(rows_of(A["a_w_out"], 2 * s, 2), split=False)
                give(n, to_tokens(w, xc, 2, s == 0, s == 7, [arrived, zr], k0=2 * s))
            return residual(0, A["ln_g"][0, 0], A["ln_b"][0, 0])

        def moe(layer, x_done):
            v = 6 * layer + 3
            ada(v)
            ada(v + 1)
            ada(v + 2)
            fence()
            H, HT = arena(KD, T), arena2(KD, T)
            h_ready = channels(X, modulated(v + 1, v, H, HT), x_done)
            h_ready = [DV.last()]
            b = rot()
            for t in range(TT):
                for k in range(KD):
                    tok = mm(banks[b][:, t * NE:(t + 1) * NE], H[:, k, t * P:(t + 1) * P], WR[:, k, :], k, KD,
                             h_ready, wr_ready, bank_free[b], signal=(k == KD - 1))
            L = banks[b][:, 0:TT * NE].rearrange("p (t e) -> p t e", t=TT)
            pr, sel, w1, w2, comb = (arena(TT, NE) for _ in range(5))
            c2 = arena(4)
            pairs, gs, gm = arena(TT * NG, 6), arena(TT, NG), arena(TT, NG)

            def wide(x, n=NE):
                return x.unsqueeze(2).broadcast_to([P, TT, n])

            def reduce(o, i, op):
                return DV.add(lambda e: e.tensor_reduce(o, i, AX.X, op))

            DV.add(lambda e: e.tensor_reduce(c2[:, 0:2], L, AX.X, ALU.max), tok)
            bank_free[b] = tt(pr, L, wide(c2[:, 0:2]), ALU.subtract)
            tok = act(pr, pr, ACT.Exp, bank_free[b])
            DV.hold(tok)
            reduce(c2[:, 0:2], pr, ALU.add)
            DV.add(lambda e: e.reciprocal(c2[:, 0:2], c2[:, 0:2]))
            tt(pr, pr, wide(c2[:, 0:2]), ALU.mult)
            tt(sel, pr, BR[:, :].unsqueeze(1).broadcast_to([P, TT, NE]), ALU.add, br_ready)
            s4 = sel.rearrange("p t (g e) -> p (t g) e", g=NG)
            tt(pairs[:, :, 0:3], s4[:, :, 0:3], s4[:, :, 1:4], ALU.add)
            tt(pairs[:, :, 3:5], s4[:, :, 0:2], s4[:, :, 2:4], ALU.add)
            tt(pairs[:, :, 5:6], s4[:, :, 0:1], s4[:, :, 3:4], ALU.add)
            DV.add(lambda e: e.tensor_reduce(gs.rearrange("p t g -> p (t g)"), pairs, AX.X, ALU.max))

            def first_max(o, x, n, prio):
                reduce(c2[:, 0:2], x, ALU.max)
                tt(o, x, wide(c2[:, 0:2], n), ALU.is_equal)
                tt(o, o, const(prio).unsqueeze(1).broadcast_to([P, TT, n]), ALU.mult)
                reduce(c2[:, 0:2], o, ALU.max)
                return tt(o, o, wide(c2[:, 0:2], n), ALU.is_equal)

            first_max(gm, gs, NG, "prio4")
            gmw = gm.rearrange("p t g -> p (t g)").unsqueeze(2).broadcast_to([P, TT * NG, EG])
            tt(s4, s4, gmw, ALU.mult)
            w1g = w1.rearrange("p t (g e) -> p (t g) e", g=NG)
            DV.add(lambda e: e.tensor_scalar(w1g, gmw, NEG, -NEG, ALU.mult, ALU.add))
            tt(sel, sel, w1, ALU.add)
            first_max(w1, sel, NE, "prio16")
            stt(sel, w1, -2.0 * NEG, sel, ALU.mult, ALU.add)
            first_max(w2, sel, NE, "prio16")
            tt(w1, w1, w2, ALU.add)
            tt(comb, w1, pr, ALU.mult)
            reduce(c2[:, 0:2], comb, ALU.add)
            DV.add(lambda e: e.reciprocal(c2[:, 0:2], c2[:, 0:2]))
            comb_ready = tt(comb, comb, wide(c2[:, 0:2]), ALU.mult)

            HID = [arena2(4, T) for _ in range(2)]
            CB = [arena(T) for _ in range(2)]
            SGT = [arena(2, T) for _ in range(2)]
            PR = [arena(2, T) for _ in range(2)]
            hid_free, hid_ready = [None] * 2, [None] * 2
            free = [None, None]

            def up(e_):
                i = e_ % 2
                b = rot()
                for t in range(TT):
                    tok = mm(banks[b][:, t * P:(t + 1) * P], comb[:, t, e_:e_ + 1].broadcast_to([P, P]), ident, 0, 1,
                             comb_ready, bank_free[b], signal=(t == TT - 1))
                bank_free[b] = cb = copy(CB[i], banks[b][:, 0:T], tok, hid_ready[i], on="A")
                for n in range(2):
                    ng, wg, ag = take(cols_of(A["moe_w_gate"][layer, e_], 256 * n, 256))

                    def evac_gate(_, b, tok):
                        return act(SGT[n], bank2(b), ACT.Silu, tok, free[n])

                    give(ng, to_channels(wg, HT, KD, 2, evac_gate, [ag, h_ready]))
                    silu = AC.last()
                    nu, wu, au = take(cols_of(A["moe_w_up"][layer, e_], 256 * n, 256))

                    def evac_up(_, b, tok):
                        return tt(PR[n], bank2(b), CB[i].unsqueeze(1).broadcast_to([P, 2, T]), ALU.mult, tok, cb)

                    give(nu, to_channels(wu, HT, KD, 2, evac_up, [au]))
                    tok = tt(PR[n], PR[n], SGT[n], ALU.mult, silu)
                    free[n] = hid_ready[i] = split_out(HID[i][:, 2 * n:2 * n + 2, :], PR[n], 1.0, tok, hid_free[i])

            def down(e_):
                i = e_ % 2
                for s in range(2):
                    n, w, arrived = take(rows_of(A["moe_w_down"][layer, e_], 2 * s, 2))
                    hid_free[i] = to_tokens(w, HID[i], 2, e_ == 0 and s == 0, e_ == NE - 1 and s == 1,
                                            [arrived, down_ready[e_]], k0=2 * s)
                    give(n, hid_free[i])

            down_ready = {}
            for e_ in range(NE):
                up(e_)
                down_ready[e_] = hid_ready[e_ % 2]
                if e_:
                    down(e_ - 1)
            down(NE - 1)
            return residual(2 * layer + 1, A["ln_g"][layer, 1], A["ln_b"][layer, 1])

        def project_heads(dst, w, c0, scale, src, ready, on=None):
            toks = []
            for s in range(4):
                n, v, arrived = take(cols_of(w, c0 + s * 256, 256))

                def evac(m, b, tok):
                    toks.append(affine(dst[:, m:m + 2, :], bank2(b), scale, None, tok, on=on))
                    return toks[-1]

                give(n, to_channels(v, src, KD, 2, evac, [arrived, ready], n0=2 * s))
            return toks

        def project_values(dst, w, c0, src, ready):
            toks = []
            for s in range(2):
                bs = [rot() for _ in range(TT)]
                for half in range(2):
                    n, v, arrived = take(w[half * 512:(half + 1) * 512, c0 + s * 512:c0 + (s + 1) * 512]
                                         .rearrange("(k p) n -> p k n", p=P))
                    for t, b in enumerate(bs):
                        for k in range(4):
                            tok = mm(banks[b][:, :], src[:, 4 * half + k, t * P:(t + 1) * P], v[:, k, :],
                                     4 * half + k, KD, arrived, ready, bank_free[b], signal=(k == 3))
                        if half:
                            bank_free[b] = copy(dst[:, t, s * 512:(s + 1) * 512], banks[b][:, :], tok)
                            toks.append(bank_free[b])
                    give(n, tok)
            return toks

        def out_product(w, src, ready):
            for s in range(4):
                n, v, arrived = take(rows_of(w, 2 * s, 2))
                give(n, to_tokens(v, src, 2, s == 0, s == 3, [arrived, ready], k0=2 * s))

        def add_acc():
            toks = []
            for t in range(TT):
                for h in range(2):
                    s = slice(h * 512, (h + 1) * 512)
                    b = 2 * t + h
                    tok = tt(X[:, t, s], X[:, t, s], banks[b][:, :], ALU.add, acc_tok[b])
                    bank_free[b] = tok
                toks.append(tok)
            return toks

        def moba(x_done):
            for v in (6, 7, 8, 12, 13):
                ada(v)
            fence()
            HT, KVH = arena2(KD, T), arena2(KD, T)
            q, k_, v_ = arena(KD, T), arena(KD, T), arena(TT, D)
            o = arena2(KD, T, at=2 * KD * T)
            tmp = arena(KD, T, at=arena_at[0])
            h_ready = channels(X, modulated(7, 6, tmp, HT, also=(tmp, KVH, 13, 12)), x_done)
            h_ready = [DV.last(), AC.last()]
            ready = project_heads(k_, A["b_w_kv"], 0, 1.0, KVH, h_ready)
            ready += project_values(v_, A["b_w_kv"], D, KVH, h_ready)
            ready += project_heads(q, A["b_wq"], 0, AD ** -0.5, HT, h_ready)
            NB = 3
            DV.hold(PE.last())
            AC.hold(PE.last())
            E, ET = ([arena(3 * P, at=3 * P * (NB * j + i)) for i in range(NB)] for j in range(2))
            sm = arena(4 * NB, at=6 * NB * P)
            e_free, et_free, s_tok, s_bank = [None] * NB, [None] * NB, {}, {}

            def scores(h):
                b = h % 4
                p0 = AD * (h % 2)
                qh, kh = q[p0:p0 + AD, h // 2, :], k_[p0:p0 + AD, h // 2, :]
                mm(banks[b][:, 0:P], qh[:, 0:P], kh[:, 0:P], 0, 1, ready, bank_free[b])
                s_tok[h] = mm(banks[b][:, P:3 * P], qh[:, P:T], kh[:, 0:T], 0, 1, signal=True)

            def soft(h):
                i, b = h % NB, h % 4
                slope = 2.0 ** (-8.0 * (h + 1) / AH)
                c = sm[:, 4 * i:4 * i + 4]
                dist = CONST[:, CONST_AT["dist0"]:CONST_AT["dist0"] + 3 * P]
                bank_free[b] = stt(E[i], dist, -slope, banks[b][:, 0:3 * P], ALU.mult, ALU.add, s_tok[h], e_free[i])
                parts = (slice(0, P), slice(P, 3 * P))
                for t, s in enumerate(parts):
                    tok = DV.add(lambda e, t=t, s=s: e.tensor_reduce(c[:, t:t + 1], E[i][:, s], AX.X, ALU.max,
                                                                     negate=True))
                for t, s in enumerate(parts):
                    t2 = act(E[i][:, s], E[i][:, s], ACT.Exp, tok, bias=c[:, t:t + 1], acc=c[:, 2 + t:3 + t])
                DV.add(lambda e: e.reciprocal(c[:, 2:4], c[:, 2:4]), t2)
                for t, s in enumerate(parts):
                    tok = ts(E[i][:, s], E[i][:, s], c[:, 2 + t:3 + t], None, ALU.mult)
                return tok

            o_bank = {}

            def values(h, p_tok):
                i = h % NB
                b = rot()
                e_free[i] = transposes(b, [(n * P, E[i][:, n * P:(n + 1) * P]) for n in range(3)], p_tok)
                bank_free[b] = tok = copy(ET[i], banks[b][:, 0:3 * P], e_free[i], et_free[i], on="A")
                if h % 2 == 0:
                    o_bank[0] = rot()
                b = o_bank[0]
                et_free[i] = attend(b, h, v_, ET[i], tok)
                if h % 2:
                    bank_free[b] = split_out(o[:, h // 2, :], banks[b][:, 0:T], 1.0, et_free[i])

            for h in range(3):
                scores(h)
            p_tok = {}
            for h in range(AH):
                p_tok[h] = soft(h)
                if h + 3 < AH:
                    scores(h + 3)
                if h:
                    values(h - 1, p_tok[h - 1])
            values(AH - 1, p_tok[AH - 1])
            out_product(A["b_wo"], o, DV.last())
            return residual(2, A["ln_g"][1, 0], A["ln_b"][1, 0])

        def attend(b, h, v_, PT, tok):
            p0 = AD * (h % 2)
            o = banks[b][p0:p0 + AD, :]
            vh = [v_[:, s, h * AD:(h + 1) * AD] for s in range(TT)]
            mm(o[:, 0:P], vh[0], PT[:, 0:P], 0, 1, tok, bank_free[b])
            mm(o[:, P:T], vh[0], PT[:, P:T], 0, 2)
            return mm(o[:, P:T], vh[1], PT[:, T:3 * P], 1, 2, signal=True)

        def normed(gain, layer, x_done, dst):
            xn = arena(TT, D)
            row_ready = small(ROWG[:, :], row(A[gain][layer]), rowg_read[0])
            toks = rms(X, xn, row_ready, x_done)
            rowg_read[0] = toks[-1]

            def move(ks, cs, o, tok):
                if isinstance(dst, Split):
                    return split_out(dst[:, ks, cs], o, 1.0, tok)
                return copy(dst[:, ks, cs], o, tok)

            return lambda: (channels(xn, move, toks), [AC.last(), DV.last()])[1]

        rowg_read = [None]

        def pool_mixer(layer, j, x_done):
            fence()
            HT = arena(KD, T)
            h_ready = normed("mix_norm_g_2", layer, x_done, HT)()
            pt = arena(KD, T)
            buf = [arena(2, T) for _ in range(2)]
            DV.hold(h_ready)
            for g, win in enumerate(WINDOWS):
                src = cur = HT[:, 2 * g:2 * g + 2, :]
                sh, i = 1, 0
                while sh < win:
                    nxt = buf[i % 2]
                    DV.add(lambda e, nxt=nxt, cur=cur, sh=sh: e.tensor_copy(nxt[:, :, 0:sh], cur[:, :, 0:sh]))
                    tt(nxt[:, :, sh:T], cur[:, :, sh:T], cur[:, :, 0:T - sh], ALU.add)
                    cur, sh, i = nxt, 2 * sh, i + 1
                inv = const("count")[:, g * T:(g + 1) * T].unsqueeze(1).broadcast_to([P, 2, T])
                tt(cur, cur, inv, ALU.mult)
                tok = tt(pt[:, 2 * g:2 * g + 2, :], cur, src, ALU.subtract)
            scale = small(ROWG[:, :], row(A["pool_scale_2"][j]), rowg_read[0])
            n, w, arrived = take(A["pool_w_2"][j].rearrange("g (k p) n -> p (g k) n", p=P), split=False)
            for t in range(TT):
                for g in range(4):
                    b = 2 * t + g // 2
                    for k in range(2):
                        ready = mm(banks[b][:, (g % 2) * T:(g % 2 + 1) * T], pt[:, 2 * g + k, t * P:(t + 1) * P],
                                   w[:, 2 * g + k, :], k, 2, arrived, tok, bank_free[b], signal=(k == 1))
            give(n, ready)
            for t in range(TT):
                for h in range(2):
                    s = slice(h * 512, (h + 1) * 512)
                    b = 2 * t + h
                    bank_free[b] = tt(RT[:, s], banks[b][:, :], ROWG[:, s], ALU.mult, ready, scale)
                    rowg_read[0] = bank_free[b]
                    tok = tt(X[:, t, s], X[:, t, s], RT[:, s], ALU.add)
            return [tok, tok]

        def stick_breaking(layer, x_done):
            fence()
            HT = arena2(KD, T)
            h_ready = normed("mix_norm_g_2", layer, x_done, HT)()
            q, k_, v_, o = arena(KD, T), arena(KD, T), arena(TT, D), arena2(KD, T)
            w = A["sb_w_qkv_2"][0]
            ready = project_heads(q, w, 0, AD ** -0.5, HT, h_ready)
            ready += project_heads(k_, w, D, 1.0, HT, h_ready)
            ready += project_values(v_, w, 2 * D, HT, h_ready)
            NB = 3
            DV.hold(PE.last())
            AC.hold(PE.last())
            SPL, MIN, LS, AT = ([arena(3 * P, at=3 * P * (NB * j + i)) for i in range(NB)] for j in range(4))
            past = CONST[:, CONST_AT["past0"]:CONST_AT["past0"] + 3 * P]
            s_tok, r_tok, l_free, a_free = {}, {}, [None] * NB, [None] * NB
            o_bank = {}

            def scores(h):
                b = h % 4
                p0 = AD * (h % 2)
                qh, kh = q[p0:p0 + AD, h // 2, :], k_[p0:p0 + AD, h // 2, :]
                mm(banks[b][:, 0:T], kh[:, 0:P], qh, 0, 1, ready, bank_free[b])
                s_tok[h] = mm(banks[b][:, T:3 * P], kh[:, P:T], qh[:, P:T], 0, 1, signal=True)

            def logs(h):
                i, b = h % NB, h % 4
                z = banks[b][:, 0:3 * P]
                act(SPL[i], z, ACT.Abs, s_tok[h], a_free[i])
                tok = act(SPL[i], SPL[i], ACT.Exp, scale=-1.0)
                t1 = act(SPL[i], SPL[i], ACT.Ln, bias=1.0)
                stt(LS[i], z, 0.0, SPL[i], ALU.max, ALU.add, t1, l_free[i])
                r_tok[h] = tt(LS[i], LS[i], past, ALU.mult)
                bank_free[b] = stt(MIN[i], z, 0.0, SPL[i], ALU.min, ALU.subtract)

            def finish_head(h):
                i = h % NB
                b = rot()
                later, negone = const("later"), const("negone")
                mm(banks[b][:, 0:P], later, LS[i][:, 0:P], 0, 1, r_tok[h], bank_free[b])
                mm(banks[b][:, P:T], later, LS[i][:, P:T], 0, 2)
                mm(banks[b][:, P:T], negone, LS[i][:, T:3 * P], 1, 2)
                l_free[i] = mm(banks[b][:, T:3 * P], later, LS[i][:, T:3 * P], 0, 1, signal=True)
                t1 = tt(AT[i], MIN[i], banks[b][:, 0:3 * P], ALU.add, l_free[i], a_free[i])
                bank_free[b] = t1
                t2 = act(AT[i], AT[i], ACT.Exp, t1)
                t3 = tt(AT[i], AT[i], past, ALU.mult, t2)
                if h % 2 == 0:
                    o_bank[0] = rot()
                b = o_bank[0]
                return b, t3

            def put(h, b, tok):
                i = h % NB
                a_free[i] = attend(b, h, v_, AT[i], tok)
                if h % 2:
                    bank_free[b] = split_out(o[:, h // 2, :], banks[b][:, 0:T], 1.0, a_free[i])

            for h in range(3):
                scores(h)
            for h in range(AH):
                logs(h)
                if h + 3 < AH:
                    scores(h + 3)
                if h:
                    put(h - 1, *finish_head(h - 1))
            put(AH - 1, *finish_head(AH - 1))
            out_product(A["sb_w_o_2"][0], o, DV.last())
            return add_acc()

        def s5(layer, x_done):
            fence()
            HT = arena(KD, T)
            h_ready = normed("mix_norm_g_2", layer, x_done, HT)()
            PE.hold(h_ready)
            now = fence()
            arena_at[0] = KD * T
            par = arena(3, NT5)
            br, bi, cr, ci = (arena(NT5, 2 * SC) for _ in range(4))
            got = [small(par, A["s5_par"], now), small(br, A["s5_b_re"], now), small(bi, A["s5_b_im"], now),
                   small(cr, A["s5_c_re"], now), small(ci, A["s5_c_im"], now)]
            tm = [arena(NT5) for _ in range(16)]
            are, aim, ldt = par[:, 0, :], par[:, 1, :], par[:, 2, :]
            dt, x, th, r, cs, sn, er, em, sh, nr, ni, rd, cor, coi, u1, u2 = tm
            AC.hold(got)
            DV.hold(got)
            tok = act(dt, ldt, ACT.Exp)
            tt(x, are, dt, ALU.mult, tok)
            tt(th, aim, dt, ALU.mult)
            ts(u1, th, 1.0 / (2.0 * float(np.pi)), ROUND_MAGIC, ALU.mult, ALU.add)
            ts(u1, u1, -ROUND_MAGIC, None, ALU.add)
            stt(r, u1, -TWO_PI_HI, th, ALU.mult, ALU.add)
            stt(r, u1, -TWO_PI_LO, r, ALU.mult, ALU.add)
            ts(r, r, 3.1415925, -3.1415925, ALU.min, ALU.max)
            stt(u2, r, -1.0, r, ALU.mult, ALU.max)
            tok = ts(u2, u2, -1.0, float(np.pi) / 2, ALU.mult, ALU.add)
            act(er, x, ACT.Exp, tok)
            act(em, x, ACT.Tanh, scale=0.5)
            act(sn, r, ACT.Sin)
            act(sh, r, ACT.Sin, scale=0.5)
            tok = act(cs, u2, ACT.Sin)
            ts(u1, em, -1.0, 1.0, ALU.mult, ALU.add, tok)
            DV.add(lambda e: e.reciprocal(u1, u1))
            stt(em, em, 2.0, u1, ALU.mult, ALU.mult)
            tt(nr, em, cs, ALU.mult)
            tt(sh, sh, sh, ALU.mult)
            stt(nr, sh, -2.0, nr, ALU.mult, ALU.add)
            tt(ni, er, sn, ALU.mult)
            tt(u1, are, are, ALU.mult)
            tt(rd, aim, aim, ALU.mult)
            tt(rd, rd, u1, ALU.add)
            DV.add(lambda e: e.reciprocal(rd, rd))
            tt(cor, nr, are, ALU.mult)
            tt(u1, ni, aim, ALU.mult)
            tt(cor, cor, u1, ALU.add)
            tt(cor, cor, rd, ALU.mult)
            tt(coi, ni, are, ALU.mult)
            tt(u1, nr, aim, ALU.mult)
            tt(coi, coi, u1, ALU.subtract)
            tt(coi, coi, rd, ALU.mult)
            G8 = 4
            CT, ST_ = arena(G8, T), arena(G8, T)
            W1, W2 = arena(8, P), arena(8, P)
            wide = lambda v: v.unsqueeze(2).broadcast_to([P, NT5, 2 * SC])
            b1 = W1.rearrange("p a b -> p (a b)").rearrange("p (a b) -> p a b", a=NT5)
            b2 = W2.rearrange("p a b -> p (a b)").rearrange("p (a b) -> p a b", a=NT5)
            tt(b1, br, wide(coi), ALU.mult)
            tt(b2, bi, wide(coi), ALU.mult)
            tt(br, br, wide(cor), ALU.mult)
            tt(br, br, b2, ALU.subtract)
            tt(bi, bi, wide(cor), ALU.mult)
            tt(bi, bi, b1, ALU.add)
            bar_ready = ts(ci, ci, -1.0, None, ALU.mult)
            BT = [arena(KD, P) for _ in range(2)]
            for src, dst in ((br, BT[0]), (bi, BT[1])):
                for k in range(0, KD, 4):
                    b = rot()
                    tok = transposes(b, [(j * P, src[:, 4 * (k + j):4 * (k + j) + 4, :].rearrange("p a b -> p (a b)"))
                                         for j in range(4)], bar_ready)
                    bank_free[b] = bt_ready = copy(dst[:, k:k + 4, :], banks[b][:, :].rearrange(
                        "p (a b) -> p a b", a=4), tok, on="D")
            V = arena(4, T)
            Z = [arena(2, T) for _ in range(2)]
            z_free = [None, None]
            DV.hold(h_ready)
            yb = None
            for i in range(NT5):
                if i % G8 == 0:
                    c8, s8 = cs[:, i:i + G8].unsqueeze(2), sn[:, i:i + G8].unsqueeze(2)
                    DV.add(lambda e, c8=c8: e.tensor_copy(CT[:, :, 0:1], c8))
                    DV.add(lambda e, s8=s8: e.tensor_copy(ST_[:, :, 0:1], s8))
                    n = 1
                    while n < T:
                        cn = CT[:, :, n - 1:n].broadcast_to([P, G8, n])
                        sn_ = ST_[:, :, n - 1:n].broadcast_to([P, G8, n])
                        lo, hi = slice(0, n), slice(n, 2 * n)
                        tt(W1[:, 0:G8, lo], ST_[:, :, lo], sn_, ALU.mult)
                        tt(W2[:, 0:G8, lo], ST_[:, :, lo], cn, ALU.mult)
                        tt(ST_[:, :, hi], CT[:, :, lo], sn_, ALU.mult)
                        tt(CT[:, :, hi], CT[:, :, lo], cn, ALU.mult)
                        tt(CT[:, :, hi], CT[:, :, hi], W1[:, 0:G8, lo], ALU.subtract)
                        tt(ST_[:, :, hi], ST_[:, :, hi], W2[:, 0:G8, lo], ALU.add)
                        n *= 2
                ct, st = CT[:, i % G8, :], ST_[:, i % G8, :]
                kt, p0 = i // 4, 32 * (i % 4)
                b = rot()
                for j in range(2):
                    tok = mm(bank2(b)[:, j, :], BT[j][p0:p0 + 32, kt, :], HT[p0:p0 + 32, kt, :], 0, 1,
                             bt_ready, bank_free[b], signal=(j == 1))
                bu = bank2(b)
                two = lambda v: v.unsqueeze(1).broadcast_to([P, 2, T])
                tt(V[:, 0:2, :], bu, two(ct), ALU.mult, tok)
                bank_free[b] = tt(V[:, 2:4, :], bu, two(st), ALU.mult)
                tt(V[:, 0, :], V[:, 0, :], V[:, 3, :], ALU.add)
                tt(V[:, 1, :], V[:, 1, :], V[:, 2, :], ALU.subtract)
                for j in range(2):
                    DV.add(lambda e, j=j, i=i: e.tensor_tensor_scan(
                        V[:, 2 + j, :], er[:, i:i + 1].broadcast_to([P, T]), V[:, j, :], 0.0, ALU.mult, ALU.add))
                z = Z[i % 2]
                tt(z, V[:, 2:4, :], two(ct), ALU.mult, z_free[i % 2])
                tt(V[:, 0:2, :], V[:, 2:4, :], two(st), ALU.mult)
                tt(z[:, 0, :], z[:, 0, :], V[:, 1, :], ALU.subtract)
                ztok = tt(z[:, 1, :], z[:, 1, :], V[:, 0, :], ALU.add)
                if i % 4 == 0:
                    yb = (i // 4) % 2
                o = banks[yb][p0:p0 + 32, 0:T]
                mm(o, cr[:, i, :], z[:, 0, :], 0, 2, ztok, bank_free[yb])
                z_free[i % 2] = mm(o, ci[:, i, :], z[:, 1, :], 1, 2, signal=True)
                if i % 4 == 3:
                    g = MEMG[:, kt, :]
                    bank_free[yb] = stt(g, HT[:, kt, :], col("s5_d_2", kt), banks[yb][:, 0:T], ALU.mult, ALU.add,
                                        z_free[i % 2])
                    gtok = act(g, g, ACT.Gelu_apprx_tanh, bank_free[yb])
            for h in range(4):
                bs = [rot(), rot()]
                for m, c0 in enumerate((0, D)):
                    n, w, arrived = take(cols_of(A["s5_w_glu_2"][0], c0 + h * 256, 256), split=False)
                    for t in range(TT):
                        for k in range(KD):
                            tok = mm(bank2(bs[m])[:, t, :], MEMG[:, k, t * P:(t + 1) * P], w[:, k, :], k, KD,
                                     arrived, gtok, bank_free[bs[m]], signal=(k == KD - 1))
                    give(n, tok)
                rt = RT[:, 512 * (h % 2):512 * (h % 2) + 512].rearrange("p (t n) -> p t n", t=TT)
                bank_free[bs[1]] = act(rt, bank2(bs[1]), ACT.Sigmoid, tok, DV.last())
                bank_free[bs[0]] = tt(rt, rt, bank2(bs[0]), ALU.mult, bank_free[bs[1]])
                s = slice(h * 256, (h + 1) * 256)
                x_done = tt(X[:, :, s], X[:, :, s], rt, ALU.add)
            return [x_done, x_done]

        def cross(layer, x_done):
            fence()
            MG, HT = arena2(KD, T), arena2(KD, T)
            o = arena2(KD, T, at=0)
            move = normed("xa_norm_g_2", layer, x_done, HT)
            for k in range(KD):
                m_ready = ts(MEMG[:, k, :], MEMN[:, k, :], col("mem_norm_g_2", 8 * layer + k), None, ALU.mult)
            m_ready = split_out(MG, MEMG, 1.0, m_ready)
            q, k_, v_ = arena(KD, T), arena(KD, T), arena(TT, D)
            ready = project_heads(k_, A["xa_wkv_2"][layer], 0, 1.0, MG, m_ready)
            vready = project_values(v_, A["xa_wkv_2"][layer], D, MG, m_ready)
            h_ready = move()
            ready += project_heads(q, A["xa_wq_2"][layer], 0, XD ** -0.5, HT, h_ready)
            DV.hold(PE.last())
            AC.hold(PE.last())
            E, ET = arena(XH, TT, T, at=4096), [arena(2, T, at=6144 + 512 * i) for i in range(2)]
            sm = arena(4 * XH, at=7168)
            s_tok, p_tok, et_free = {}, {}, [None, None]
            for h in range(XH):
                for t in range(TT):
                    for c in range(2):
                        s_tok[h] = mm(banks[h][:, t * T:(t + 1) * T], q[:, 2 * h + c, t * P:(t + 1) * P],
                                      k_[:, 2 * h + c, :], c, 2, ready, bank_free[h], signal=(c == 1))
            for h in range(XH):
                c = sm[:, 4 * h:4 * h + 4]
                tok = DV.add(lambda e, h=h, c=c: e.tensor_reduce(c[:, 0:2], bank2(h), AX.X, ALU.max, negate=True),
                             s_tok[h])
                for t in range(TT):
                    t2 = act(E[:, h, t, :], bank2(h)[:, t, :], ACT.Exp, tok, bias=c[:, t:t + 1],
                             acc=c[:, 2 + t:3 + t])
                bank_free[h] = t2
                DV.add(lambda e, c=c: e.reciprocal(c[:, 2:4], c[:, 2:4]), t2)
                p_tok[h] = tt(E[:, h, :, :], E[:, h, :, :], c[:, 2:4].unsqueeze(2).broadcast_to([P, TT, T]), ALU.mult)
            for h in range(XH):
                b = rot()
                tok = transposes(b, [((m * 2 + t) * P, E[:, h, t, m * P:(m + 1) * P])
                                     for m in range(2) for t in range(TT)], p_tok[h])
                bank_free[b] = tok = copy(ET[h % 2], bank2(b), tok, et_free[h % 2], on="A")
                b = rot()
                for d in range(2):
                    for m in range(2):
                        t2 = mm(bank2(b)[:, d, :], v_[:, m, h * XD + d * P:h * XD + (d + 1) * P], ET[h % 2][:, m, :],
                                m, 2, tok, vready, bank_free[b], signal=(m == 1))
                et_free[h % 2] = t2
                bank_free[b] = split_out(o[:, 2 * h:2 * h + 2, :], bank2(b), 1.0, t2)
            out_product(A["xa_wo_2"][layer], o, DV.last())
            return add_acc()

        def ffn(layer, x_done):
            fence()
            HT = arena2(KD, T)
            h_ready = normed("ffn_norm_g_2", layer, x_done, HT)()
            hids = [arena2(4, T) for _ in range(3)]
            raw = [arena(2, T) for _ in range(2)]
            hid_free = [None] * 3
            U = [arena(2, 2 + T) for _ in range(4)]
            CV = [arena(2, T) for _ in range(2)]
            for u in U:
                DV.add(lambda e, u=u: e.memset(u[:, :, 0:2], 0.0))
            w_up, w_dn = A["ffn_w_up_2"][layer], A["ffn_w_down_2"][layer]
            u_free, cv_free, hid_tok = [None] * 4, [None] * 2, {}

            def conv(dst, u, c, *waits):
                w = lambda j: col("ffn_conv_w_2", (layer * 3 + j) * 2 * KF + c)
                ts(dst, u[:, 2:2 + T], w(2), col("ffn_conv_b_2", layer * 2 * KF + c), ALU.mult, ALU.add, *waits)
                stt(dst, u[:, 1:1 + T], w(1), dst, ALU.mult, ALU.add)
                return stt(dst, u[:, 0:T], w(0), dst, ALU.mult, ALU.add)

            def up(s):
                i, turn_ = s % 2, (s // 2) % 3
                hid = hids[turn_][:, 2 * i:2 * i + 2, :]

                def evac(u, dst, c0, cv):
                    def f(_, b, tok):
                        t1 = copy(U[u][:, :, 2:2 + T], bank2(b), tok, u_free[u], on="A")
                        for j in range(2):
                            t2 = conv(dst[:, j, :], U[u][:, j, :], c0 + j, t1, cv)
                        u_free[u] = t2
                        return t1
                    return f

                n, wg, arrived = take(cols_of(w_up, FF + s * 256, 256))
                give(n, to_channels(wg, HT, KD, 2, evac(2 * i + 1, CV[i], KF + 2 * s, None), [arrived, h_ready]))
                t3 = act(CV[i], CV[i], ACT.Silu, u_free[2 * i + 1])
                n, wv, arrived = take(cols_of(w_up, s * 256, 256))
                give(n, to_channels(wv, HT, KD, 2, evac(2 * i, raw[i], 2 * s, None), [arrived]))
                tok = tt(raw[i], raw[i], CV[i], ALU.mult, t3)
                hid_tok[s] = split_out(hid, raw[i], 1.0, tok, hid_free[turn_])

            def down(s):
                turn_ = (s // 2) % 3
                n, w, arrived = take(rows_of(w_dn, 2 * s, 2))
                hid_free[turn_] = to_tokens(w, hids[turn_], 2, s == 0, s == KF // 2 - 1, [arrived, hid_tok[s]],
                                            k0=2 * (s % 2))
                give(n, hid_free[turn_])

            for s in range(KF // 2):
                up(s)
                if s >= 2:
                    down(s - 2)
            down(KF // 2 - 2)
            down(KF // 2 - 1)
            return add_acc()

        fence()
        x_done = mlstm()
        steps = []
        if upto >= 1:
            x_done = moe(0, x_done)
        if upto >= 2:
            x_done = moba(x_done)
        if upto >= 3:
            x_done = moe(1, x_done)
        if upto >= 4:
            now = fence()
            mem = arena(TT, D)
            got = small(mem, A["mem_2"].rearrange("(t p) n -> p t n", p=P), now)
            tok = rms(mem, mem, None, [got, got])
            channels(mem, lambda ks, cs, o, tok: copy(MEMN[:, ks, cs], o, tok), tok)
            m_ready = [AC.last(), DV.last()]
            AC.hold(m_ready)
            DV.hold(m_ready)
            rowg_read[0] = DV.last()
            for layer in range(DEPTH2):
                if upto < 5 + 3 * layer:
                    break
                if layer % 3 == 0:
                    x_done = pool_mixer(layer, layer // 3, x_done)
                elif layer % 3 == 1:
                    x_done = stick_breaking(layer, x_done)
                else:
                    x_done = s5(layer, x_done)
                if upto >= 6 + 3 * layer:
                    x_done = cross(layer, x_done)
                if upto >= 7 + 3 * layer:
                    x_done = ffn(layer, x_done)
        if upto >= 99:
            g_ready = small(ROWG[:, :], row(A["final_norm_g_2"]), rowg_read[0])
            x_done = rms(X, X, g_ready, x_done)
        done = small(out.rearrange("(t p) n -> p t n", p=P), X[:, :, :], DV.last())
        ML.hold(done)
        if plan is None:
            return units

        block = ctx.enter_context(nc.Block())

        @block.sync
        def _(eng):
            LD.run(eng)

        @block.gpsimd
        def _(eng):
            ML.run(eng)

        @block.tensor
        def _(eng):
            PE.run(eng)

        @block.vector
        def _(eng):
            DV.run(eng)

        @block.scalar
        def _(eng):
            AC.run(eng)


def host_layout(inputs, np):
    f = lambda name: np.asarray(inputs[name])
    cols = np.zeros((P, NCOLS), np.float32)
    for name, n in COLS:
        if name in ("bi", "bf"):
            b = f("a_b_if")[0]
            cols[0:MH, COL_AT[name]] = b[0:MH] if name == "bi" else b[MH:]
        else:
            cols[:, COL_AT[name]:COL_AT[name] + n] = f(name).reshape(n, P).T
    states = lambda a: a.reshape(NT5, 2, SP).transpose(1, 2, 0).reshape(P, NT5)

    def blocks(a):
        o = np.zeros((2, SP, NT5, 2, SC), np.float32)
        for g in range(2):
            o[g, :, :, g, :] = a[g::2].transpose(1, 0, 2)
        return o.reshape(P, NT5, 2 * SC)

    out = {
        "consts": constants(), "cols": cols,
        "x": f("x")[0], "xT": f("x")[0].T, "mem_2": f("mem_2")[0],
        "s5_par": np.stack([states(f("s5_a_re_2")[0]), states(f("s5_a_im_2")[0]),
                            states(np.broadcast_to(f("s5_log_dt_2")[0][:, None], (SG, SP)))], axis=1),
        "s5_b_re": blocks(f("s5_b_re_2")[0]), "s5_b_im": blocks(f("s5_b_im_2")[0]),
        "s5_c_re": blocks(f("s5_c_re_2")[0].transpose(0, 2, 1)),
        "s5_c_im": blocks(f("s5_c_im_2")[0].transpose(0, 2, 1)),
        "a_w_in": f("a_w_in")[0], "a_wq": f("a_wq")[0], "a_wk": f("a_wk")[0], "a_wv": f("a_wv")[0],
        "a_w_if": f("a_w_if")[0], "a_w_out": f("a_w_out")[0], "b_wq": f("b_wq")[0], "b_wo": f("b_wo")[0],
    }
    for name in ("w_ada", "b_ada", "ln_g", "ln_b", "b_w_kv", "moe_w_router", "moe_b_router", "moe_w_gate",
                 "moe_w_up", "moe_w_down", "pool_w_2", "pool_scale_2", "sb_w_qkv_2", "sb_w_o_2", "s5_w_glu_2",
                 "xa_wq_2", "xa_wkv_2", "xa_wo_2", "ffn_w_up_2", "ffn_w_down_2", "final_norm_g_2",
                 "mix_norm_g_2", "xa_norm_g_2", "ffn_norm_g_2"):
        out[name] = f(name)
    return out


def kernel(**inputs):
    import concourse.bacc as bacc
    from concourse.bass_utils import run_bass_kernel_spmd

    arrays = {f"in_{name}": np.ascontiguousarray(a) for name, a in host_layout(inputs, np).items()}

    def program(plan):
        nc = bacc.Bacc("TRN2", target_bir_lowering=False, num_devices=1)
        args = {name[3:]: nc.dram_tensor(name, a.shape, mybir.dt.from_np(a.dtype), kind="ExternalInput").ap()
                for name, a in arrays.items()}
        out = nc.dram_tensor("out_0", (T, D), F32, kind="ExternalOutput").ap()
        return nc, build(nc, args, out, UPTO, plan)

    _, units = program(None)
    nc, _ = program(units)
    r = run_bass_kernel_spmd(nc, [arrays], core_ids=[0])
    return r.results[0]["out_0"].reshape(1, T, D)


UPTO = 99
```

```python
from contextlib import ExitStack

import numpy as np

import concourse.bass as bass
from concourse import mybir

F32 = mybir.dt.float32
F32R = mybir.dt.float32r
ALU = mybir.AluOpType
ACT = mybir.ActivationFunctionType
AX = mybir.AxisListType

P = 128
T = 256
TT = T // P
D = 1024
KD = D // P
DEPTH = 2
ALPHA = (2.0 * DEPTH) ** 0.25
LN_EPS = 1e-5
RMS_EPS = 1e-6
MH = 4
MI = 2 * D
MD = MI // MH
AH = 16
AD = D // AH
NE = 16
NG = 4
EG = NE // NG
FE = 512
DEPTH2 = 4
WINDOWS = (2, 4, 8, 16)
SG = 64
SP = 64
SC = D // SG
NT5 = SG // 2
XH = 4
XD = D // XH
FF = ((8 * D // 3 + 127) // 128) * 128
KF = FF // P
NSLOT = 5
NSPLIT = 3
NARENA = 17000
SLOT = 2048
NEG = 1e30
TWO_PI_HI = 6.28125
TWO_PI_LO = 2.0 * float(np.pi) - 6.28125
ROUND_MAGIC = 12582912.0


COLS = [("c", 8), ("b_ada", 112), ("a_conv_w", 64), ("a_conv_b", 16), ("a_gn_g", 16), ("a_skip", 16),
        ("bi", 1), ("bf", 1), ("mem_norm_g_2", 32), ("s5_d_2", 8), ("ffn_conv_w_2", 3 * DEPTH2 * 2 * KF),
        ("ffn_conv_b_2", DEPTH2 * 2 * KF)]
COL_AT = {}
NCOLS = 0
for _name, _n in COLS:
    COL_AT[_name] = NCOLS
    NCOLS += _n

CONSTS = [("ident", 128), ("dist0", 128), ("dist1", 256), ("causal", 128), ("later", 128), ("negone", 128),
          ("ones", 128), ("past0", 256), ("past1", 128), ("count", 4 * T), ("prio16", 16), ("prio4", 4)]
CONST_AT = {}
NCONST = 0
for _name, _n in CONSTS:
    CONST_AT[_name] = NCONST
    NCONST += _n


def constants():
    out = np.zeros((P, NCONST), np.float32)
    i, j = np.arange(P)[:, None], np.arange(T)[None, :]

    def put(name, v):
        out[:, CONST_AT[name]:CONST_AT[name] + v.shape[1]] = v

    put("ident", np.eye(P, dtype=np.float32))
    put("dist0", np.where(j[:, :P] <= i, i - j[:, :P], NEG))
    put("dist1", np.where(j <= i + P, i + P - j, NEG))
    put("causal", np.where(j[:, :P] <= i, 0.0, -NEG))
    put("later", np.where(i > j[:, :P], -1.0, 0.0))
    put("negone", -np.ones((P, P)))
    put("ones", np.ones((P, P)))
    put("past0", np.where(i < j, 1.0, 0.0))
    put("past1", np.where(i < j[:, :P], 1.0, 0.0))
    cnt = np.stack([1.0 / np.minimum(np.arange(1, T + 1), w) for w in WINDOWS]).reshape(1, -1)
    put("count", np.broadcast_to(cnt, (P, 4 * T)))
    put("prio16", np.broadcast_to(np.arange(16, 0, -1.0), (P, 16)))
    put("prio4", np.broadcast_to(np.arange(4, 0, -1.0), (P, 4)))
    return out


class Queue:

    def __init__(self, sem, chained):
        self.sem, self.chained, self.steps, self.count = sem, chained, [], 0
        self.lag = 0

    def add(self, emit, *waits, signal=True, alone=False):
        self.steps.append((waits, emit, signal, None if alone else self.lag))
        if signal:
            self.count += 1
        return (self.sem, self.count)

    def hold(self, *waits):
        self.steps.append((waits, None, False, None))

    def last(self):
        return (self.sem, self.count)

    def run(self, eng):
        met, done, chain = {}, 0, []

        def wait(w):
            if w is None:
                return
            if isinstance(w, list):
                for x in w:
                    wait(x)
                return
            sem, value = w() if callable(w) else w
            if value > 0 and met.get(id(sem), 0) < value:
                met[id(sem)] = value
                eng.wait_ge(sem, value)

        for waits, emit, signal, lag in self.steps:
            if self.chained and lag is not None and len(chain) > lag:
                wait((self.sem, chain[-1 - lag]))
            wait(list(waits))
            if emit is None:
                continue
            ins = emit(eng)
            if signal:
                ins.then_inc(self.sem, 1)
                done += 1
                if lag is not None:
                    chain.append(done)


class Split:

    def __init__(self, hi, lo):
        self.hi, self.lo = hi, lo

    def __getitem__(self, key):
        return Split(self.hi[key], self.lo[key])


def build(nc, A, out, plan=None):
    ctx = ExitStack()
    with ctx:
        def sb(name, shape):
            return ctx.enter_context(nc.sbuf_tensor(name, shape, F32))

        nsem = [0]

        def sem(name):
            nsem[0] += 1
            return ctx.enter_context(nc.semaphore(name))

        ring = [sb(f"ring{i}", [P, SLOT]) for i in range(NSLOT)]
        parts, parts32 = [], []
        for i in range(NSPLIT):
            with nc.sbuf_tensor(f"parts{i}", [P, 2, SLOT], F32R) as part:
                parts.append(part)
            parts32.append(sb(f"parts32_{i}", [P, 2, SLOT]))
        X = sb("X", [P, TT, D])
        CONST = sb("CONST", [P, NCONST])
        COL = sb("COL", [P, NCOLS])
        SHARED = sb("SHARED", [P, 4096])
        ROWG = sb("ROWG", [P, D])
        ROWB = sb("ROWB", [P, D])
        MOD = sb("MOD", [P, 112])
        WR = sb("WR", [P, KD, NE])
        BR = sb("BR", [P, NE])
        WIF = sb("WIF", [P, MI // P, 2 * MH])
        CSIL = sb("CSIL", [P, KD])
        STAT = sb("STAT", [P, 64])
        SCR = sb("SCR", [P, P])
        SCR = SCR[:, :]
        with nc.sbuf_tensor("ARENA_R", [P, NARENA], F32R) as ARENA_R:
            pass
        ARENA = sb("ARENA", [P, NARENA])
        RT = sb("RT", [P, D])
        GATE = SHARED[:, :].rearrange("p (g n) -> p g n", g=4)
        MEMN = SHARED[:, 0:2048].rearrange("p (k t) -> p k t", k=KD)
        MEMG = SHARED[:, 2048:4096].rearrange("p (k t) -> p k t", k=KD)
        banks = [ctx.enter_context(nc.psum_tensor(f"bank{i}", [P, 512], F32)) for i in range(8)]

        PE = Queue(sem("pe_done"), False)
        DV = Queue(sem("vector_done"), True)
        AC = Queue(sem("scalar_done"), True)
        LD = Queue(sem("weights_queue"), False)
        ML = Queue(sem("misc_queue"), False)

        def const(name, n=None):
            a = CONST_AT[name]
            return CONST[:, a:a + (n or dict(CONSTS)[name])]

        def col(name, j=0, n=1):
            a = COL_AT[name] + j
            return COL[:, a:a + n]

        ident = const("ident")
        arena_at = [0]

        def fence():
            arena_at[0] = 0
            now = [PE.last(), DV.last(), AC.last()]
            DV.hold(now)
            AC.hold(now)
            return now

        def arena(*shape, at=None, whole=None):
            n = int(np.prod(shape))
            a = arena_at[0] if at is None else at
            if at is None:
                arena_at[0] += n
            assert arena_at[0] <= NARENA, arena_at[0]
            v = (ARENA if whole is None else whole)[:, a:a + n]
            if len(shape) == 2:
                v = v.rearrange("p (a b) -> p a b", a=shape[0])
            elif len(shape) == 3:
                v = v.rearrange("p (a b c) -> p a b c", a=shape[0], b=shape[1])
            return v

        def arena2(*shape, at=None):
            n = int(np.prod(shape))
            return Split(arena(*shape, at=at, whole=ARENA_R),
                         arena(*shape, at=None if at is None else at + n, whole=ARENA_R))

        slot_sem = [sem(f"slot{i}") for i in range(NSLOT)]
        units = []
        raw_free, part_free, part_ready = {}, {}, {}
        split_no = {}
        pending = [0]
        taken = [0]

        def raw_view(n, src):
            return ring[n % NSLOT][:, 0:src.shape[1] * src.shape[2]]

        def split_unit(n):
            src, _ = plan[n]
            m = split_no[n] = len(split_no)
            w, p = raw_view(n, src), parts[m % NSPLIT]
            size = w.shape[1]
            t = AC.add(lambda e: e.copy(p[:, 0, 0:size], w), (slot_sem[n % NSLOT], 16 * (n // NSLOT + 1)),
                       part_free.get(m - NSPLIT), alone=True)
            low = lambda e: e.tensor_tensor(p[:, 1, 0:size], w, p[:, 0, 0:size].bitcast(F32), ALU.subtract)
            raw_free[n] = part_ready[n] = ML.add(low, t) if m % 3 == 2 else DV.add(low, t, alone=True)

        def take(src, split=True):
            n = len(units)
            units.append((src, split))
            k = src.shape[1]
            dst = raw_view(n, src)
            freed = (lambda: raw_free[n - NSLOT]) if n >= NSLOT else None
            LD.add(lambda e: e.dma_start(dst.rearrange("p (k n) -> p k n", k=k), src)
                   .then_inc(slot_sem[n % NSLOT], 16), freed, signal=False)
            if plan is not None:
                taken[0] += split
                while pending[0] < min(n + NSLOT, len(plan)) and (
                        not plan[pending[0]][1] or len(split_no) < taken[0] + NSPLIT - 1 + (not split)):
                    if plan[pending[0]][1]:
                        split_unit(pending[0])
                    pending[0] += 1
            if not split:
                return n, dst.rearrange("p (k n) -> p k n", k=k), (slot_sem[n % NSLOT], 16 * (n // NSLOT + 1))
            p = parts[split_no.get(n, 0) % NSPLIT]
            v = [p[:, i, 0:dst.shape[1]].rearrange("p (k n) -> p k n", k=k) for i in range(2)]
            return n, Split(*v), part_ready.get(n)

        def give(n, token):
            if units[n][1]:
                part_free[split_no.get(n, 0)] = token
            else:
                raw_free[n] = token

        def cols_of(w, c0, n):
            return w[:, c0:c0 + n].rearrange("(k p) n -> p k n", p=P)

        def rows_of(w, k0, nk):
            return w[k0 * P:(k0 + nk) * P, :].rearrange("(k p) n -> p k n", p=P)

        def small(dst, src, *waits):
            s = sem(f"small{nsem[0]}")
            ML.add(lambda e: e.dma_start(dst, src).then_inc(s, 16), *waits, signal=False)
            return (s, 16)

        def row(v):
            return v.rearrange("(a n) -> a n", a=1).broadcast_to([P, v.shape[0]])

        bank_free = [None] * 8
        turn = [0]

        def rot():
            turn[0] = (turn[0] + 1) % 4
            return 4 + turn[0]

        def mm(o, l, r, k, K, *waits, signal=False):
            if isinstance(l, Split):
                PE.add(lambda e: e.matmul(o, l.hi, r.hi, start=(k == 0), stop=False), *waits, signal=False)
                PE.add(lambda e: e.matmul(o, l.hi, r.lo, start=False, stop=False), signal=False)
                return PE.add(lambda e: e.matmul(o, l.lo, r.hi, start=False, stop=(k == K - 1)), signal=signal)
            return PE.add(lambda e: e.matmul(o, l, r, start=(k == 0), stop=(k == K - 1)), *waits, signal=signal)

        def transposes(b, pairs, *waits):
            for n, (at, src) in enumerate(pairs):
                m, w = src.shape[0], src.shape[1]
                o = banks[b][0:w, at:at + m]
                tok = PE.add(lambda e, o=o, src=src, m=m: e.transpose(o, src, ident[0:m, 0:m]),
                             *((list(waits) + [bank_free[b]]) if n == 0 else ()), signal=(n == len(pairs) - 1))
            return tok

        flip = [0]

        def affine(o, i, scale, bias, *waits, on=None):
            if on is None:
                flip[0] ^= 1
                on = "AD"[flip[0]]
            if on == "A":
                return AC.add(lambda e: e.activation(o, i, ACT.Identity, bias=0.0 if bias is None else bias,
                                                     scale=scale), *waits)
            if bias is None:
                return DV.add(lambda e: e.tensor_scalar(o, i, scale, None, ALU.mult), *waits)
            return DV.add(lambda e: e.tensor_scalar(o, i, scale, bias, ALU.mult, ALU.add), *waits)

        def copy(o, i, *waits, on=None):
            if on is None:
                flip[0] ^= 1
                on = "AD"[flip[0]]
            if on == "A":
                return AC.add(lambda e: e.copy(o, i), *waits)
            return DV.add(lambda e: e.tensor_copy(o, i), *waits)

        def tt(o, a, b, op, *waits):
            return DV.add(lambda e: e.tensor_tensor(o, a, b, op), *waits)

        def ts(o, a, s1, s2, op0, op1=None, *waits):
            if s2 is None:
                return DV.add(lambda e: e.tensor_scalar(o, a, s1, None, op0), *waits)
            return DV.add(lambda e: e.tensor_scalar(o, a, s1, s2, op0, op1), *waits)

        def stt(o, a, s, b, op0, op1, *waits, acc=None):
            if acc is None:
                return DV.add(lambda e: e.scalar_tensor_tensor(o, a, s, b, op0, op1), *waits)
            return DV.add(lambda e: e.scalar_tensor_tensor(o, a, s, b, op0, op1, accum_out=acc), *waits)

        def act(o, i, f, *waits, bias=0.0, scale=1.0, acc=None):
            return AC.add(lambda e: e.activation(o, i, f, bias=bias, scale=scale, accum_out=acc), *waits)

        def bank2(b):
            return banks[b][:, :].rearrange("p (a t) -> p a t", a=2)

        def to_channels(w, src, nk, n_out, evac, ready, n0=0):
            tok = None
            for n in range(0, n_out, 2):
                b = rot()
                for j in range(min(2, n_out - n)):
                    for k in range(nk):
                        tok = mm(bank2(b)[:, j, :], w[:, k, (n + j) * P:(n + j + 1) * P], src[:, k, :], k, nk,
                                 *([ready, bank_free[b]] if j == 0 and k == 0 else []),
                                 signal=(k == nk - 1))
                bank_free[b] = evac(n0 + n, b, tok)
            return tok

        rowg_read = [None]
        acc_tok = {}

        def to_tokens(w, src, nk, first, last, ready, k0=0):
            tok = None
            for t in range(TT):
                for h in range(2):
                    b = 2 * t + h
                    for k in range(nk):
                        fresh, end = first and k == 0, last and k == nk - 1
                        tok = mm(banks[b][:, :], src[:, k0 + k, t * P:(t + 1) * P], w[:, k, h * 512:(h + 1) * 512],
                                 0 if fresh else 1, 2 if end else 9,
                                 *([ready] + ([bank_free[b]] if fresh else []) if k == 0 else []),
                                 signal=(k == nk - 1))
                    acc_tok[b] = tok
            return tok

        def split_out(dst, src, scale, *waits):
            t = act(dst.hi, src, ACT.Identity, *waits, scale=scale)
            return stt(dst.lo, src, scale, dst.hi.bitcast(F32), ALU.mult, ALU.subtract, t, *waits)

        def stats(t, *waits):
            bn = STAT[:, 8 + 12 * t:20 + 12 * t].rearrange("p (a b) -> p a b", a=2)
            for h in range(2):
                DV.add(lambda e, h=h: e.bn_stats(bn[:, h, :], X[:, t, h * 512:(h + 1) * 512]), *waits)
            return DV.add(lambda e: e.bn_aggr(STAT[:, 2 * t:2 * t + 2],
                                              STAT[:, 8 + 12 * t:20 + 12 * t].rearrange("p (a b) -> p a b", a=2)))

        def inv_sqrt(o, v, eps, *waits):
            tok = ts(o, v, 1.0, eps, ALU.mult, ALU.add, *waits)
            tok = act(o, o, ACT.Sqrt, tok)
            return DV.add(lambda e: e.reciprocal(o, o), tok)

        def layer_norm(t, g_ready):
            tok = stats(t)
            inv_sqrt(STAT[:, 4 + t:5 + t], STAT[:, 2 * t + 1:2 * t + 2], LN_EPS, tok)
            stt(X[:, t, :], X[:, t, :], STAT[:, 2 * t:2 * t + 1], ROWG[:, :], ALU.subtract, ALU.mult, *g_ready)
            return stt(X[:, t, :], X[:, t, :], STAT[:, 4 + t:5 + t], ROWB[:, :], ALU.mult, ALU.add)

        def rms(src, dst, gain, x_done):
            c = STAT[:, 32:34]
            for t in range(TT):
                tok = act(RT[:, :], src[:, t, :], ACT.Square, x_done[t], acc=c[:, t:t + 1])
            tok = ts(c, c, 1.0 / D, RMS_EPS, ALU.mult, ALU.add, tok)
            tok = act(c, c, ACT.Sqrt, tok)
            DV.add(lambda e: e.reciprocal(c, c), tok)
            if gain is None:
                return [ts(dst[:, t, :], src[:, t, :], c[:, t:t + 1], None, ALU.mult) for t in range(TT)]
            return [stt(dst[:, t, :], src[:, t, :], c[:, t:t + 1], ROWG[:, :], ALU.mult, ALU.mult, gain)
                    for t in range(TT)]

        def channels(src, move, x_done):
            toks = []
            for t in range(TT):
                for k in range(0, KD, 4):
                    b = rot()
                    tok = transposes(b, [(j * P, src[:, t, (k + j) * P:(k + j + 1) * P]) for j in range(4)],
                                     x_done[t])
                    toks.append(move(slice(k, k + 4), slice(t * P, (t + 1) * P),
                                     banks[b][:, :].rearrange("p (a b) -> p a b", a=4), tok))
                    bank_free[b] = toks[-1]
            return toks

        col_ready = small(COL[:, :], A["cols"])
        DV.add(lambda e: e.memset(STAT[:, :], 0.0))
        csil_ready = act(CSIL[:, :], col("c", 0, 8), ACT.Silu, col_ready)
        ident_ready = small(ident, A["consts"][:, 0:P])
        DV.hold(col_ready, ident_ready)
        later_loads = {}

        def load_rest(*waits):
            c_ready = small(CONST[:, P:NCONST], A["consts"][:, P:NCONST], *waits)
            for g in range(4):
                later_loads[g] = small(GATE[:, g, :], row(A["b_ada"][(3 * g + 2) * D:(3 * g + 3) * D]))
            later_loads["x"] = small(X[:, :, :], A["x"].rearrange("(t p) n -> p t n", p=P))
            later_loads["wif"] = small(WIF[:, :, :], A["a_w_if"].rearrange("(k p) n -> p k n", p=P))
            later_loads["wr"] = small(WR[:, :, :], A["moe_w_router"].rearrange("(k p) n -> p k n", p=P))
            later_loads["br"] = small(BR[:, :], row(A["moe_b_router"]))
            for q in (PE, DV, AC):
                q.hold(c_ready, ident_ready)

        def ada_step(v, h):
            gate = v < 12 and v % 3 == 2
            b = rot()
            n, w, arrived = take(cols_of(A["w_ada"], v * D + h * 256, 256), split=False)
            for k in range(KD):
                tok = mm(banks[b][:, 0:256], CSIL[:, k:k + 1].broadcast_to([P, P]), w[:, k, :], k, KD,
                         arrived, csil_ready, bank_free[b], signal=(k == KD - 1))
            if gate:
                g = GATE[:, v // 3, h * 256:(h + 1) * 256]
                bank_free[b] = stt(g, banks[b][:, 0:256], 1.0, g, ALU.add, ALU.add, tok, later_loads[v // 3])
            else:
                at = 8 * v + 2 * h
                for j in range(2):
                    bank_free[b] = stt(SCR, banks[b][:, j * P:(j + 1) * P], 1.0, ident, ALU.mult, ALU.mult, tok,
                                       acc=MOD[:, at + j:at + j + 1])
                one = 1.0 if v == 13 or (v < 12 and v % 3 == 1) else 0.0
                stt(MOD[:, at:at + 2], MOD[:, at:at + 2], one, col("b_ada", at, 2), ALU.add, ALU.add)
            give(n, tok)
            return DV.last()

        ada_rest = [(v, h) for v in (3, 4, 5, 6, 7, 12, 13, 8, 9, 10, 11) for h in range(4)]

        def ada(v):
            return [ada_step(v, h) for h in range(4)]

        def ada_more(n=1):
            for _ in range(n):
                if ada_rest:
                    ada_step(*ada_rest.pop(0))

        def residual(g, lng, lnb):
            rows = [small(ROWG[:, :], row(lng), rowg_read[0]), small(ROWB[:, :], row(lnb), rowg_read[0])]
            toks = []
            for t in range(TT):
                for h in range(2):
                    s = slice(h * 512, (h + 1) * 512)
                    b = 2 * t + h
                    o = RT[:, s]
                    tok = tt(o, banks[b][:, :], GATE[:, g, s], ALU.mult, acc_tok[b])
                    bank_free[b] = tok
                    stt(X[:, t, s], X[:, t, s], ALPHA, o, ALU.mult, ALU.add, later_loads["x"])
                toks.append(layer_norm(t, rows))
            rowg_read[0] = toks[-1]
            return toks

        def modulated(scale, shift, tmp, dst, also=None):
            def one(ks, cs, o, tmp, dst, scale, shift, tok):
                n = ks.stop - ks.start
                wide = lambda v: MOD[:, 8 * v + ks.start:8 * v + ks.stop].unsqueeze(2).broadcast_to([P, n, P])
                got = tt(tmp[:, ks, cs], o, wide(scale), ALU.mult, tok)
                t1 = tt(tmp[:, ks, cs], tmp[:, ks, cs], wide(shift), ALU.add)
                split_out(dst[:, ks, cs], tmp[:, ks, cs], 1.0, t1)
                return got

            def move(ks, cs, o, tok):
                one(ks, cs, o, tmp, dst, scale, shift, tok)
                if also:
                    one(ks, cs, o, *also, tok)
                return DV.last()
            return move

        def mlstm():
            nm = MI // P
            xm = arena(nm, 3 + T)
            xc = arena(nm, T)
            HT = arena(KD, T)
            xt_ready = small(HT, A["xT"].rearrange("(k p) t -> p k t", p=P))
            ada(0)
            ready = ada(1)
            for k in range(KD):
                tok = affine(HT[:, k, :], HT[:, k, :], MOD[:, 8 + k:9 + k], MOD[:, k:k + 1], ready, xt_ready, on="D")
            h_ready = tok
            pad = DV.add(lambda e: e.memset(xm[:, :, 0:3], 0.0))
            xm_ready = {}

            def evac_x(n, b, tok):
                t1 = copy(xm[:, n:n + 2, 3:3 + T], bank2(b), tok, on="A")
                xm_ready[n] = t1
                for c in (n, n + 1):
                    w = lambda j: col("a_conv_w", 16 * j + c)
                    ts(xc[:, c, :], xm[:, c, 3:3 + T], w(3), col("a_conv_b", c), ALU.mult, ALU.add, t1)
                    for j in (2, 1, 0):
                        t2 = stt(xc[:, c, :], xm[:, c, j:j + T], w(j), xc[:, c, :], ALU.mult, ALU.add)
                act(xc[:, n:n + 2, :], xc[:, n:n + 2, :], ACT.Silu, t2)
                return t1

            for s in range(MI // 256):
                n, w, arrived = take(cols_of(A["a_w_in"], s * 256, 256), split=False)
                give(n, to_channels(w, HT, KD, 2, evac_x, [arrived, h_ready, pad], n0=2 * s))
                if s == 1:
                    load_rest(PE.last())
                if s == 3:
                    ada(2)
            xc_ready = AC.last()
            LI, LF, BC, GR, R8 = arena(T), arena(T), arena(T), arena(T), arena(16)
            b, b2 = rot(), rot()
            for k in range(nm):
                tok = mm(banks[b][0:2 * MH, 0:T], WIF[:, k, :], xc[:, k, :], k, nm,
                         xc_ready, later_loads["wif"], bank_free[b], signal=(k == nm - 1))
            bank_free[b] = tok = copy(GR[0:2 * MH, :], banks[b][0:2 * MH, 0:T], tok, on="D")
            tok = mm(banks[b2][0:MH, 0:T], ident[0:2 * MH, MH:2 * MH], GR[0:2 * MH, :], 0, 1, tok, bank_free[b2],
                     signal=True)
            ts(LI[0:MH, :], GR[0:MH, :], col("bi")[0:MH, :], None, ALU.add)
            tok = ts(LF[0:MH, :], banks[b2][0:MH, 0:T], col("bf")[0:MH, :], None, ALU.add, None, tok)
            bank_free[b2] = tok
            act(GR[0:MH, :], LF[0:MH, :], ACT.Abs, tok)
            act(GR[0:MH, :], GR[0:MH, :], ACT.Exp, scale=-1.0)
            tok = act(GR[0:MH, :], GR[0:MH, :], ACT.Ln, bias=1.0)
            stt(LF[0:MH, :], LF[0:MH, :], 0.0, GR[0:MH, :], ALU.min, ALU.subtract, tok)
            for c in range(2):
                s = slice(c * P, (c + 1) * P)
                DV.add(lambda e, s=s: e.tensor_tensor_scan(BC[0:MH, s], const("ones")[0:MH, :], LF[0:MH, s], 0.0,
                                                           ALU.mult, ALU.add))
            tt(GR[0:MH, :], LI[0:MH, :], BC[0:MH, :], ALU.subtract)
            DV.add(lambda e: e.tensor_reduce(R8[0:MH, 8:9], GR[0:MH, 0:P], AX.X, ALU.max))
            ts(R8[0:MH, 8:9], R8[0:MH, 8:9], 0.0, None, ALU.max)
            tt(R8[0:MH, 9:10], BC[0:MH, P - 1:P], R8[0:MH, 8:9], ALU.add)
            ts(R8[0:MH, 8:9], R8[0:MH, 8:9], -1.0, None, ALU.mult)
            ts(R8[0:MH, 0:4], ident[0:MH, 0:MH], R8[0:MH, 9:10], None, ALU.mult)
            tok = ts(R8[0:MH, 4:8], ident[0:MH, 0:MH], R8[0:MH, 8:9], None, ALU.mult)
            BV = arena(20)
            b = rot()
            mm(banks[b][:, 0:4], BC[0:MH, 0:P], ident[0:MH, 0:MH], 0, 1, tok, bank_free[b])
            mm(banks[b][:, 4:8], BC[0:MH, P:T], ident[0:MH, 0:MH], 0, 1)
            tok = mm(banks[b][:, 8:16], const("ones")[0:MH, :], R8[0:MH, 0:8], 0, 1, signal=True)
            bank_free[b] = copy(BV[:, 0:16], banks[b][:, 0:16], tok, on="D")
            bv_ready = tt(BV[:, 16:20], BV[:, 4:8], BV[:, 8:12], ALU.add)
            q, k_, v = arena(4, T), arena(4, T), arena(TT, MD)
            HH = arena(TT, MD)
            E, S, ST = arena(3 * P), arena(3 * P), arena(3 * P)
            m, bn = arena(16), arena(TT * 6)
            vs = [v, RT[:, :].rearrange("p (t n) -> p t n", t=TT)]
            proj = {}

            def project(h):
                toks = []
                src = xc[:, 4 * h:4 * h + 4, :]
                for dst, name, scale in ((q, "a_wq", 1.0), (k_, "a_wk", MD ** -0.5)):
                    def evac(n, b, tok):
                        toks.append(affine(dst[:, n:n + 2, :], bank2(b), scale, None, tok))
                        return toks[-1]

                    n, w, arrived = take(rows_of(A[name][h], 0, 4), split=False)
                    give(n, to_channels(w, src, 4, 4, evac, [arrived, xc_ready]))
                n, wv, arrived = take(rows_of(A["a_wv"][h], 0, 4), split=False)
                for t in range(TT):
                    b = rot()
                    for k in range(4):
                        tok = mm(banks[b][:, :], xm[:, 4 * h + k, 3 + t * P:3 + (t + 1) * P], wv[:, k, :], k, 4,
                                 arrived, bank_free[b], signal=(k == 3))
                    bank_free[b] = copy(vs[h % 2][:, t, :], banks[b][:, :], tok)
                    toks.append(bank_free[b])
                give(n, tok)
                proj[h] = toks

            project(0)
            for h in range(MH):
                v = vs[h % 2]
                ada_more(3)
                bg, bs = 2 * (h % 2), 2 * (h % 2) + 1
                gtok = mm(banks[bg][:, 0:T], ident[0:MH, h:h + 1].broadcast_to([MH, P]), GR[0:MH, :], 0, 1,
                          bank_free[bg], signal=True)
                for n, (tq, tk) in enumerate(((0, 0), (1, 1), (1, 0))):
                    for k in range(4):
                        stok = mm(banks[bs][:, n * P:(n + 1) * P], q[:, k, tq * P:(tq + 1) * P],
                                  k_[:, k, tk * P:(tk + 1) * P], k, 4, proj[h], bank_free[bs], signal=(k == 3))
                for c in range(2):
                    bcol = BV[:, 4 * c + h:4 * c + h + 1]
                    d = E[:, c * P:(c + 1) * P]
                    stt(d, banks[bg][:, c * P:(c + 1) * P], bcol, const("causal"), ALU.add, ALU.add, gtok, bv_ready)
                    DV.add(lambda e, c=c, d=d: e.tensor_reduce(m[:, c:c + 1], d, AX.X, ALU.max))
                    a = bcol if c == 0 else BV[:, 16 + h:17 + h]
                    tt(m[:, c:c + 1], m[:, c:c + 1], a, ALU.max)
                mtok = ts(m[:, 2:4], m[:, 0:2], -1.0, None, ALU.mult)
                for c in range(2):
                    act(E[:, c * P:(c + 1) * P], E[:, c * P:(c + 1) * P], ACT.Exp, mtok, bias=m[:, 2 + c:3 + c])
                bank_free[bg] = act(E[:, 2 * P:3 * P], banks[bg][:, 0:P], ACT.Exp, bias=BV[:, 12 + h:13 + h])
                act(m[:, 4:5], BV[:, 16 + h:17 + h], ACT.Exp, bias=m[:, 3:4])
                etok = act(m[:, 5:7], m[:, 2:4], ACT.Exp)
                for n, (sc, ac) in enumerate(((1.0, 7), (1.0, 8), (m[:, 4:5], 9))):
                    tok = stt(S[:, n * P:(n + 1) * P], banks[bs][:, n * P:(n + 1) * P], sc, E[:, n * P:(n + 1) * P],
                              ALU.mult, ALU.mult, etok, stok, acc=m[:, ac:ac + 1])
                bank_free[bs] = sw = tok
                tt(m[:, 8:9], m[:, 8:9], m[:, 9:10], ALU.add)
                stt(m[:, 10:12], m[:, 7:9], -1.0, m[:, 7:9], ALU.mult, ALU.max)
                tt(m[:, 10:12], m[:, 10:12], m[:, 5:7], ALU.max)
                rtok = DV.add(lambda e: e.reciprocal(m[:, 10:12], m[:, 10:12]))
                if h + 1 < MH:
                    project(h + 1)
                b = rot()
                tok = transposes(b, [(n * P, S[:, n * P:(n + 1) * P]) for n in range(3)], sw)
                bank_free[b] = st = copy(ST[:, :], banks[b][:, 0:3 * P], tok, on="A")
                for t in range(TT):
                    b = rot()
                    for k in range(t + 1):
                        blk = (0, 1)[t] if k == 0 else 2
                        src_v = v[:, (0, 1)[t] if k == 0 else 0, :]
                        tok = mm(banks[b][:, :], ST[:, blk * P:(blk + 1) * P], src_v, k, t + 1, st, bank_free[b],
                                 signal=(k == t))
                    htok = ts(HH[:, t, :], banks[b][:, :], m[:, 10 + t:11 + t], None, ALU.mult, None, tok, rtok)
                    bank_free[b] = htok
                    DV.add(lambda e, t=t: e.bn_stats(bn[:, 6 * t:6 * t + 6], HH[:, t, :]))
                    DV.add(lambda e, t=t: e.bn_aggr(m[:, 12 + 2 * t:14 + 2 * t], bn[:, 6 * t:6 * t + 6]))
                mv = m[:, 12:16].rearrange("p (t c) -> p t c", t=2)
                inv_sqrt(m[:, 10:12], mv[:, :, 1], LN_EPS, DV.last())
                for t in range(TT):
                    htok = ts(HH[:, t, :], HH[:, t, :], m[:, 12 + 2 * t:13 + 2 * t], m[:, 10 + t:11 + t],
                              ALU.subtract, ALU.mult)
                for c in range(4):
                    ts(xc[:, 4 * h + c, :], xc[:, 4 * h + c, :], col("a_skip", 4 * h + c), None, ALU.mult, None, stok)
                for c in range(0, 4, 2):
                    b = rot()
                    tok = transposes(b, [((j * 2 + t) * P, HH[:, t, (c + j) * P:(c + j + 1) * P])
                                         for j in range(2) for t in range(TT)], htok)
                    for j in range(2):
                        ch = 4 * h + c + j
                        tok2 = stt(xc[:, ch, :], bank2(b)[:, j, :], col("a_gn_g", ch), xc[:, ch, :],
                                   ALU.mult, ALU.add, tok)
                    bank_free[b] = tok2


            z_free = [PE.last(), PE.last()]

            def evac_z(n, b, tok):
                i = (n // 2) % 2
                z = RT[:, 512 * i:512 * i + 512].rearrange("p (a t) -> p a t", a=2)
                t1 = act(z, bank2(b), ACT.Silu, tok, z_free[i])
                z_free[i] = tt(xc[:, n:n + 2, :], xc[:, n:n + 2, :], z, ALU.mult, t1)
                return t1

            for s in range(MI // 256):
                n, w, arrived = take(cols_of(A["a_w_in"], MI + s * 256, 256), split=False)
                give(n, to_channels(w, HT, KD, 2, evac_z, [arrived], n0=2 * s))
            zr = DV.last()
            for s in range(8):
                n, w, arrived = take(rows_of(A["a_w_out"], 2 * s, 2), split=False)
                give(n, to_tokens(w, xc, 2, s == 0, s == 7, [arrived, zr], k0=2 * s))
            return residual(0, A["ln_g"][0, 0], A["ln_b"][0, 0])

        def moe(layer, x_done):
            v = 6 * layer + 3
            now = fence()
            ada_more(4)
            H, HT = arena(KD, T), arena2(KD, T)
            h_ready = channels(X, modulated(v + 1, v, H, HT), x_done)
            h_ready = [DV.last()]
            b = rot()
            for t in range(TT):
                for k in range(KD):
                    tok = mm(banks[b][:, t * NE:(t + 1) * NE], H[:, k, t * P:(t + 1) * P], WR[:, k, :], k, KD,
                             h_ready, later_loads["wr"], bank_free[b], signal=(k == KD - 1))
            L = banks[b][:, 0:TT * NE].rearrange("p (t e) -> p t e", t=TT)
            pr, sel, w1, w2, comb = (arena(TT, NE) for _ in range(5))
            c2 = arena(4)
            pairs, gs, gm = arena(TT * NG, 6), arena(TT, NG), arena(TT, NG)

            def wide(x, n=NE):
                return x.unsqueeze(2).broadcast_to([P, TT, n])

            def reduce(o, i, op):
                return DV.add(lambda e: e.tensor_reduce(o, i, AX.X, op))

            DV.add(lambda e: e.tensor_reduce(c2[:, 0:2], L, AX.X, ALU.max), tok)
            bank_free[b] = tt(pr, L, wide(c2[:, 0:2]), ALU.subtract)
            tok = act(pr, pr, ACT.Exp, bank_free[b])
            DV.hold(tok)
            reduce(c2[:, 0:2], pr, ALU.add)
            DV.add(lambda e: e.reciprocal(c2[:, 0:2], c2[:, 0:2]))
            tt(pr, pr, wide(c2[:, 0:2]), ALU.mult)
            tt(sel, pr, BR[:, :].unsqueeze(1).broadcast_to([P, TT, NE]), ALU.add, later_loads["br"])
            s4 = sel.rearrange("p t (g e) -> p (t g) e", g=NG)
            tt(pairs[:, :, 0:3], s4[:, :, 0:3], s4[:, :, 1:4], ALU.add)
            tt(pairs[:, :, 3:5], s4[:, :, 0:2], s4[:, :, 2:4], ALU.add)
            tt(pairs[:, :, 5:6], s4[:, :, 0:1], s4[:, :, 3:4], ALU.add)
            DV.add(lambda e: e.tensor_reduce(gs.rearrange("p t g -> p (t g)"), pairs, AX.X, ALU.max))

            def first_max(o, x, n, prio):
                reduce(c2[:, 0:2], x, ALU.max)
                tt(o, x, wide(c2[:, 0:2], n), ALU.is_equal)
                tt(o, o, const(prio).unsqueeze(1).broadcast_to([P, TT, n]), ALU.mult)
                reduce(c2[:, 0:2], o, ALU.max)
                return tt(o, o, wide(c2[:, 0:2], n), ALU.is_equal)

            first_max(gm, gs, NG, "prio4")
            gmw = gm.rearrange("p t g -> p (t g)").unsqueeze(2).broadcast_to([P, TT * NG, EG])
            tt(s4, s4, gmw, ALU.mult)
            w1g = w1.rearrange("p t (g e) -> p (t g) e", g=NG)
            DV.add(lambda e: e.tensor_scalar(w1g, gmw, NEG, -NEG, ALU.mult, ALU.add))
            tt(sel, sel, w1, ALU.add)
            first_max(w1, sel, NE, "prio16")
            stt(sel, w1, -2.0 * NEG, sel, ALU.mult, ALU.add)
            first_max(w2, sel, NE, "prio16")
            tt(w1, w1, w2, ALU.add)
            tt(comb, w1, pr, ALU.mult)
            reduce(c2[:, 0:2], comb, ALU.add)
            DV.add(lambda e: e.reciprocal(c2[:, 0:2], c2[:, 0:2]))
            comb_ready = tt(comb, comb, wide(c2[:, 0:2]), ALU.mult)

            HID = [arena2(4, T) for _ in range(2)]
            CB = [arena(T) for _ in range(2)]
            SGT = [arena(2, T) for _ in range(2)]
            PR = [arena(2, T) for _ in range(2)]
            hid_free, hid_ready = [None] * 2, [None] * 2
            free = [None, None]

            def up(e_):
                i = e_ % 2
                cb = None
                for n in range(2):
                    ng, wg, ag = take(cols_of(A["moe_w_gate"][layer, e_], 256 * n, 256))

                    def evac_gate(_, b, tok):
                        return act(SGT[n], bank2(b), ACT.Silu, tok, free[n])

                    give(ng, to_channels(wg, HT, KD, 2, evac_gate, [ag, h_ready]))
                    silu = AC.last()
                    if n == 0:
                        b = rot()
                        for t in range(TT):
                            tok = mm(banks[b][:, t * P:(t + 1) * P], comb[:, t, e_:e_ + 1].broadcast_to([P, P]),
                                     ident, 0, 1, comb_ready, bank_free[b], signal=(t == TT - 1))
                        bank_free[b] = cb = copy(CB[i], banks[b][:, 0:T], tok, hid_ready[i], on="A")
                    nu, wu, au = take(cols_of(A["moe_w_up"][layer, e_], 256 * n, 256))

                    def evac_up(_, b, tok):
                        return tt(PR[n], bank2(b), CB[i].unsqueeze(1).broadcast_to([P, 2, T]), ALU.mult, tok, cb)

                    give(nu, to_channels(wu, HT, KD, 2, evac_up, [au]))
                    if n and layer == 0 and e_ < 12:
                        ada_more()
                    tok = tt(PR[n], PR[n], SGT[n], ALU.mult, silu)
                    free[n] = hid_ready[i] = split_out(HID[i][:, 2 * n:2 * n + 2, :], PR[n], 1.0, tok, hid_free[i])

            def down(e_):
                i = e_ % 2
                for s in range(2):
                    n, w, arrived = take(rows_of(A["moe_w_down"][layer, e_], 2 * s, 2))
                    hid_free[i] = to_tokens(w, HID[i], 2, e_ == 0 and s == 0, e_ == NE - 1 and s == 1,
                                            [arrived, down_ready[e_]], k0=2 * s)
                    give(n, hid_free[i])

            down_ready = {}
            if layer == 1:
                mem = arena(TT, D)
                got = small(mem, A["mem_2"].rearrange("(t p) n -> p t n", p=P), now)
            for e_ in range(NE):
                up(e_)
                if layer == 1 and e_ == 3:
                    tok = rms(mem, mem, None, [got, got])
                    channels(mem, lambda ks, cs, o, tok: copy(MEMN[:, ks, cs], o, tok), tok)
                down_ready[e_] = hid_ready[e_ % 2]
                if e_:
                    down(e_ - 1)
            if layer == 1:
                memory_parts(0)
            down(NE - 1)
            return residual(2 * layer + 1, A["ln_g"][layer, 1], A["ln_b"][layer, 1])

        def project_heads(dst, w, c0, scale, src, ready, on=None, units_=range(4), split=True):
            toks = []
            for s in units_:
                n, v, arrived = take(cols_of(w, c0 + s * 256, 256), split)

                def evac(m, b, tok):
                    toks.append(affine(dst[:, m:m + 2, :], bank2(b), scale, None, tok, on=on))
                    return toks[-1]

                give(n, to_channels(v, src, KD, 2, evac, [arrived, ready], n0=2 * s))
            return toks

        def project_values(dst, w, c0, src, ready, on=None, halves=range(2), split=True):
            toks = []
            for s in halves:
                bs = [rot() for _ in range(TT)]
                for half in range(2):
                    n, v, arrived = take(w[half * 512:(half + 1) * 512, c0 + s * 512:c0 + (s + 1) * 512]
                                         .rearrange("(k p) n -> p k n", p=P), split)
                    for t, b in enumerate(bs):
                        for k in range(4):
                            tok = mm(banks[b][:, :], src[:, 4 * half + k, t * P:(t + 1) * P], v[:, k, :],
                                     4 * half + k, KD, arrived, ready, bank_free[b], signal=(k == 3))
                        if half:
                            bank_free[b] = copy(dst[:, t, s * 512:(s + 1) * 512], banks[b][:, :], tok, on=on)
                            toks.append(bank_free[b])
                    give(n, tok)
            return toks

        early = {}
        MG = arena2(KD, T, at=0)
        XK, XV = arena(KD, T, at=10 * D), arena(TT, D, at=12 * D)

        def memory_parts(layer):
            DV.hold(PE.last())
            AC.hold(PE.last())
            for k in range(KD):
                tok = split_out(MG[:, k, :], MEMN[:, k, :], col("mem_norm_g_2", 8 * layer + k))
            early[layer] = {"ready": tok, "source": MG, "keys": [], "values": []}

        def early_keys(layer, *which):
            e = early[layer]
            e["keys"] += project_heads(XK, A["xa_wkv_2"][layer], 0, 1.0, MG, e["ready"], "A", which)

        def early_values(layer, half):
            e = early[layer]
            e["values"] += project_values(XV, A["xa_wkv_2"][layer], D, MG, e["ready"], "A", [half])

        def out_product(w, src, ready):
            for s in range(4):
                n, v, arrived = take(rows_of(w, 2 * s, 2))
                give(n, to_tokens(v, src, 2, s == 0, s == 3, [arrived, ready], k0=2 * s))

        def add_acc():
            act(STAT[:, 40:41], STAT[:, 41:42], ACT.Sqrt)
            toks = []
            for t in range(TT):
                for h in range(2):
                    s = slice(h * 512, (h + 1) * 512)
                    b = 2 * t + h
                    tok = tt(X[:, t, s], X[:, t, s], banks[b][:, :], ALU.add, acc_tok[b])
                    bank_free[b] = tok
                toks.append(tok)
            return toks

        def moba(x_done):
            fence()
            ada_more(4)
            HT, KVH = arena2(KD, T), arena2(KD, T)
            q, k_, v_ = arena(KD, T), arena(KD, T), arena(TT, D)
            o = arena2(KD, T, at=2 * KD * T)
            tmp = arena(KD, T, at=arena_at[0])
            h_ready = channels(X, modulated(7, 6, tmp, HT, also=(tmp, KVH, 13, 12)), x_done)
            h_ready = [DV.last(), AC.last()]
            ready = project_heads(k_, A["b_w_kv"], 0, 1.0, KVH, h_ready)
            ready += project_values(v_, A["b_w_kv"], D, KVH, h_ready)
            ready += project_heads(q, A["b_wq"], 0, AD ** -0.5, HT, h_ready)
            NB = 4
            DV.hold(PE.last())
            AC.hold(PE.last())
            E, ET = ([arena(3 * P, at=3 * P * (NB * j + i)) for i in range(NB)] for j in range(2))
            sm = arena(4 * NB, at=6 * NB * P)
            dist = CONST[:, CONST_AT["dist0"]:CONST_AT["dist0"] + 3 * P]
            parts_ = (slice(0, P), slice(P, 3 * P))
            e_free, et_free, s_tok, p_tok, et_tok = [None] * NB, [None] * NB, {}, {}, {}

            def pair(g):
                return (2 * g, 2 * g + 1)

            def scores(g):
                for h in pair(g):
                    b, p0 = h % 4, AD * (h % 2)
                    qh, kh = q[p0:p0 + AD, h // 2, :], k_[p0:p0 + AD, h // 2, :]
                    mm(banks[b][:, 0:P], qh[:, 0:P], kh[:, 0:P], 0, 1, ready, bank_free[b])
                    s_tok[h] = mm(banks[b][:, P:3 * P], qh[:, P:T], kh[:, 0:T], 0, 1, signal=True)

            def soft(g):
                DV.hold(DV.last())
                AC.hold(AC.last())
                DV.lag = AC.lag = 1
                col_of = lambda h: sm[:, 4 * (h % NB):4 * (h % NB) + 4]
                for h in pair(g):
                    slope = 2.0 ** (-8.0 * (h + 1) / AH)
                    bank_free[h % 4] = stt(E[h % NB], dist, -slope, banks[h % 4][:, 0:3 * P], ALU.mult, ALU.add,
                                           s_tok[h], e_free[h % NB])
                m_tok = {}
                for t, s in enumerate(parts_):
                    for h in pair(g):
                        m_tok[h] = DV.add(lambda e, h=h, t=t, s=s: e.tensor_reduce(
                            col_of(h)[:, t:t + 1], E[h % NB][:, s], AX.X, ALU.max, negate=True))
                x_tok = {}
                for t, s in enumerate(parts_):
                    for h in pair(g):
                        c = col_of(h)
                        x_tok[h] = act(E[h % NB][:, s], E[h % NB][:, s], ACT.Exp, m_tok[h], bias=c[:, t:t + 1],
                                       acc=c[:, 2 + t:3 + t])
                for h in pair(g):
                    DV.add(lambda e, h=h: e.reciprocal(col_of(h)[:, 2:4], col_of(h)[:, 2:4]), x_tok[h])
                for t, s in enumerate(parts_):
                    for h in pair(g):
                        p_tok[h] = ts(E[h % NB][:, s], E[h % NB][:, s], col_of(h)[:, 2 + t:3 + t], None, ALU.mult)
                DV.lag = AC.lag = 0

            def turn_p(g):
                for h in pair(g):
                    i, b = h % NB, rot()
                    e_free[i] = transposes(b, [(n * P, E[i][:, n * P:(n + 1) * P]) for n in range(3)], p_tok[h])
                    bank_free[b] = et_tok[h] = copy(ET[i], banks[b][:, 0:3 * P], e_free[i], et_free[i], on="A")

            def values(g):
                b = rot()
                for h in pair(g):
                    et_free[h % NB] = attend(b, h, v_, ET[h % NB], et_tok[h])
                bank_free[b] = split_out(o[:, g, :], banks[b][:, 0:T], 1.0, et_free[h % NB])

            scores(0)
            scores(1)
            for g in range(AH // 2):
                ada_more()
                soft(g)
                if g + 2 < AH // 2:
                    scores(g + 2)
                turn_p(g)
                if g:
                    values(g - 1)
            values(AH // 2 - 1)
            out_product(A["b_wo"], o, DV.last())
            return residual(2, A["ln_g"][1, 0], A["ln_b"][1, 0])

        def attend(b, h, v_, PT, tok):
            p0 = AD * (h % 2)
            o = banks[b][p0:p0 + AD, :]
            vh = [v_[:, s, h * AD:(h + 1) * AD] for s in range(TT)]
            mm(o[:, 0:P], vh[0], PT[:, 0:P], 0, 1, tok, bank_free[b])
            mm(o[:, P:T], vh[0], PT[:, P:T], 0, 2)
            return mm(o[:, P:T], vh[1], PT[:, T:3 * P], 1, 2, signal=True)

        def normed(gain, layer, x_done, dst):
            xn = arena(TT, D)
            row_ready = small(ROWG[:, :], row(A[gain][layer]), rowg_read[0])
            toks = rms(X, xn, row_ready, x_done)
            rowg_read[0] = toks[-1]

            def move(ks, cs, o, tok):
                if isinstance(dst, Split):
                    return split_out(dst[:, ks, cs], o, 1.0, tok)
                return copy(dst[:, ks, cs], o, tok)

            return lambda: (channels(xn, move, toks), [AC.last(), DV.last()])[1]

        def pool_mixer(layer, j, x_done):
            fence()
            arena_at[0] = 4 * D
            HT = arena(KD, T)
            early_keys(layer, 0)
            move = normed("mix_norm_g_2", layer, x_done, HT)
            early_keys(layer, 1)
            h_ready = move()
            pt = arena(KD, T)
            buf = [arena(2, T, at=14 * D + i * 2 * T) for i in range(2)]
            DV.hold(h_ready)
            early_keys(layer, 2, 3)
            for g, win in enumerate(WINDOWS):
                src = cur = HT[:, 2 * g:2 * g + 2, :]
                sh, i = 1, 0
                while sh < win:
                    nxt = buf[i % 2]
                    DV.add(lambda e, nxt=nxt, cur=cur, sh=sh: e.tensor_copy(nxt[:, :, 0:sh], cur[:, :, 0:sh]))
                    tt(nxt[:, :, sh:T], cur[:, :, sh:T], cur[:, :, 0:T - sh], ALU.add)
                    cur, sh, i = nxt, 2 * sh, i + 1
                inv = const("count")[:, g * T:(g + 1) * T].unsqueeze(1).broadcast_to([P, 2, T])
                tt(cur, cur, inv, ALU.mult)
                tok = tt(pt[:, 2 * g:2 * g + 2, :], cur, src, ALU.subtract)
            scale = small(ROWG[:, :], row(A["pool_scale_2"][j]), rowg_read[0])
            n, w, arrived = take(A["pool_w_2"][j].rearrange("g (k p) n -> p (g k) n", p=P), split=False)
            for t in range(TT):
                for g in range(4):
                    b = 2 * t + g // 2
                    for k in range(2):
                        ready = mm(banks[b][:, (g % 2) * T:(g % 2 + 1) * T], pt[:, 2 * g + k, t * P:(t + 1) * P],
                                   w[:, 2 * g + k, :], k, 2, arrived, tok, bank_free[b], signal=(k == 1))
            give(n, ready)
            for t in range(TT):
                for h in range(2):
                    s = slice(h * 512, (h + 1) * 512)
                    b = 2 * t + h
                    bank_free[b] = tt(RT[:, s], banks[b][:, :], ROWG[:, s], ALU.mult, ready, scale)
                    rowg_read[0] = bank_free[b]
                    tok = tt(X[:, t, s], X[:, t, s], RT[:, s], ALU.add)
            return [tok, tok]

        def stick_breaking(layer, x_done):
            fence()
            HT = arena2(KD, T)
            h_ready = normed("mix_norm_g_2", layer, x_done, HT)()
            q, k_, v_, o = arena(KD, T), arena(KD, T), arena(TT, D), arena2(KD, T)
            w = A["sb_w_qkv_2"][0]
            ready = project_heads(q, w, 0, AD ** -0.5, HT, h_ready)
            ready += project_heads(k_, w, D, 1.0, HT, h_ready)
            ready += project_values(v_, w, 2 * D, HT, h_ready)
            NB = 4
            DV.hold(PE.last())
            AC.hold(PE.last())
            SPL, MIN, LS, AT = ([arena(3 * P, at=3 * P * (NB * j + i)) for i in range(NB)] for j in range(4))
            past = CONST[:, CONST_AT["past0"]:CONST_AT["past0"] + 3 * P]
            later, negone = const("later"), const("negone")
            s_tok, r_tok, m_tok, a_tok, l_free, a_free = {}, {}, {}, {}, [None] * NB, [None] * NB

            def pair(g):
                return (2 * g, 2 * g + 1)

            def scores(g):
                for h in pair(g):
                    b, p0 = h % 4, AD * (h % 2)
                    qh, kh = q[p0:p0 + AD, h // 2, :], k_[p0:p0 + AD, h // 2, :]
                    mm(banks[b][:, 0:T], kh[:, 0:P], qh, 0, 1, ready, bank_free[b])
                    s_tok[h] = mm(banks[b][:, T:3 * P], kh[:, P:T], qh[:, P:T], 0, 1, signal=True)

            def alternate(on):
                if on:
                    DV.hold(DV.last())
                    AC.hold(AC.last())
                DV.lag = AC.lag = int(on)

            def step(g):
                alternate(True)
                now, before = (pair(g) if g < AH // 2 else ()), (pair(g - 1) if g else ())
                z = lambda h: banks[h % 4][:, 0:3 * P]
                t1, t2, t3 = {}, {}, {}
                for h in now:
                    act(SPL[h % NB], z(h), ACT.Abs, s_tok[h])
                for h in now:
                    act(SPL[h % NB], SPL[h % NB], ACT.Exp, scale=-1.0)
                for h in now:
                    t1[h] = act(SPL[h % NB], SPL[h % NB], ACT.Ln, bias=1.0)
                for h in before:
                    i, b = h % NB, rot()
                    mm(banks[b][:, 0:P], later, LS[i][:, 0:P], 0, 1, r_tok[h], bank_free[b])
                    mm(banks[b][:, P:T], later, LS[i][:, P:T], 0, 2)
                    mm(banks[b][:, P:T], negone, LS[i][:, T:3 * P], 1, 2)
                    l_free[i] = mm(banks[b][:, T:3 * P], later, LS[i][:, T:3 * P], 0, 1, signal=True)
                    t2[h] = bank_free[b] = tt(AT[i], MIN[i], banks[b][:, 0:3 * P], ALU.add, l_free[i], m_tok[h],
                                              a_free[i])
                for h in before:
                    t3[h] = act(AT[h % NB], AT[h % NB], ACT.Exp, t2[h])
                for h in now:
                    stt(LS[h % NB], z(h), 0.0, SPL[h % NB], ALU.max, ALU.add, t1[h], l_free[h % NB])
                for h in now:
                    r_tok[h] = tt(LS[h % NB], LS[h % NB], past, ALU.mult)
                for h in now:
                    m_tok[h] = bank_free[h % 4] = stt(MIN[h % NB], z(h), 0.0, SPL[h % NB], ALU.min, ALU.subtract)
                for h in before:
                    a_tok[h] = tt(AT[h % NB], AT[h % NB], past, ALU.mult, t3[h])
                alternate(False)

            def values(g):
                b = rot()
                for h in pair(g):
                    a_free[h % NB] = attend(b, h, v_, AT[h % NB], a_tok[h])
                bank_free[b] = split_out(o[:, g, :], banks[b][:, 0:T], 1.0, a_free[h % NB])

            scores(0)
            scores(1)
            for g in range(AH // 2 + 1):
                step(g)
                if g > 1:
                    values(g - 2)
                if g + 2 < AH // 2:
                    scores(g + 2)
            values(AH // 2 - 1)
            out_product(A["sb_w_o_2"][0], o, DV.last())
            return add_acc()

        def s5(layer, x_done):
            now = fence()
            HT = arena(KD, T)
            arena_at[0] = 2 * KD * T
            par = arena(3, NT5)
            br, bi, cr, ci = (arena(NT5, 2 * SC) for _ in range(4))
            got = [small(par, A["s5_par"], now), small(br, A["s5_b_re"], now), small(bi, A["s5_b_im"], now),
                   small(cr, A["s5_c_re"], now), small(ci, A["s5_c_im"], now)]
            tm = [arena(NT5) for _ in range(16)]
            rest_at, arena_at[0] = arena_at[0], KD * T
            h_ready = normed("mix_norm_g_2", layer, x_done, HT)()
            arena_at[0] = rest_at
            norm_read = PE.last()
            PE.hold(h_ready)
            are, aim, ldt = par[:, 0, :], par[:, 1, :], par[:, 2, :]
            dt, x, th, r, cs, sn, er, em, sh, nr, ni, rd, cor, coi, u1, u2 = tm
            AC.hold(got)
            DV.hold(got)
            tok = act(dt, ldt, ACT.Exp)
            tt(x, are, dt, ALU.mult, tok)
            tt(th, aim, dt, ALU.mult)
            ts(u1, th, 1.0 / (2.0 * float(np.pi)), ROUND_MAGIC, ALU.mult, ALU.add)
            ts(u1, u1, -ROUND_MAGIC, None, ALU.add)
            stt(r, u1, -TWO_PI_HI, th, ALU.mult, ALU.add)
            stt(r, u1, -TWO_PI_LO, r, ALU.mult, ALU.add)
            ts(r, r, 3.1415925, -3.1415925, ALU.min, ALU.max)
            stt(u2, r, -1.0, r, ALU.mult, ALU.max)
            tok = ts(u2, u2, -1.0, float(np.pi) / 2, ALU.mult, ALU.add)
            act(er, x, ACT.Exp, tok)
            act(em, x, ACT.Tanh, scale=0.5)
            act(sn, r, ACT.Sin)
            act(sh, r, ACT.Sin, scale=0.5)
            tok = act(cs, u2, ACT.Sin)
            ts(u1, em, -1.0, 1.0, ALU.mult, ALU.add, tok)
            DV.add(lambda e: e.reciprocal(u1, u1))
            stt(em, em, 2.0, u1, ALU.mult, ALU.mult)
            tt(nr, em, cs, ALU.mult)
            tt(sh, sh, sh, ALU.mult)
            stt(nr, sh, -2.0, nr, ALU.mult, ALU.add)
            tt(ni, er, sn, ALU.mult)
            tt(u1, are, are, ALU.mult)
            tt(rd, aim, aim, ALU.mult)
            tt(rd, rd, u1, ALU.add)
            DV.add(lambda e: e.reciprocal(rd, rd))
            tt(cor, nr, are, ALU.mult)
            tt(u1, ni, aim, ALU.mult)
            tt(cor, cor, u1, ALU.add)
            tt(cor, cor, rd, ALU.mult)
            tt(coi, ni, are, ALU.mult)
            tt(u1, nr, aim, ALU.mult)
            tt(coi, coi, u1, ALU.subtract)
            tt(coi, coi, rd, ALU.mult)
            G5 = 4
            ncr = arena(NT5, 2 * SC)
            tables = [(arena(G5, T), arena(G5, T)) for _ in range(2)]
            W1, W2 = arena(G5, P), arena(G5, P)
            m0 = len(split_no)
            spare = [parts32[(m0 + n) % NSPLIT] for n in (1, 2)]
            xm, xk = (spare[0][:, n, :].rearrange("p (a b) -> p a b", a=KD) for n in range(2))
            xv = spare[1][:, 0, :].rearrange("p (a b) -> p a b", a=TT)
            for k in range(KD):
                xm_ready = act(xm[:, k, :], MEMN[:, k, :], ACT.Identity, scale=col("mem_norm_g_2", 8 * layer + k))
            w_kv = A["xa_wkv_2"][layer]
            early_work = [lambda s=s: project_heads(xk, w_kv, 0, 1.0, xm, xm_ready, "A", [s], False)
                          for s in range(4)]
            early_work += [lambda s=s: project_values(xv, w_kv, D, xm, xm_ready, "A", [s], False)
                           for s in range(2)]
            DV.hold(norm_read)
            V = [arena(4, T, at=KD * T + 4 * T * n) for n in range(2)]
            wide = lambda v: v.unsqueeze(2).broadcast_to([P, NT5, 2 * SC])
            b1, b2 = (v.rearrange("p a b -> p (a b)").rearrange("p (a b) -> p a b", a=NT5) for v in V)
            tt(b1, br, wide(coi), ALU.mult)
            tt(b2, bi, wide(coi), ALU.mult)
            tt(br, br, wide(cor), ALU.mult)
            tt(br, br, b2, ALU.subtract)
            tt(bi, bi, wide(cor), ALU.mult)
            tt(bi, bi, b1, ALU.add)
            ts(ncr, cr, -1.0, None, ALU.mult)
            bar_ready = ts(ci, ci, -1.0, None, ALU.mult)

            NS = 32
            third = parts32[m0 % NSPLIT]
            shc, shs = (third[:, 0, n * NT5 * NS:(n + 1) * NT5 * NS].rearrange("p (a b) -> p a b", a=NT5)
                        for n in range(2))
            ws = [third[:, 1, n * 512:(n + 1) * 512].rearrange("p (a b) -> p a b", a=NT5) for n in range(2)]
            wp = [third[:, 1, 1024 + n * 256:1280 + n * 256].rearrange("p (a b) -> p a b", a=G5) for n in range(2)]
            t_ready, t_free = {}, {}

            def powers(C, S, w, add, n, top, *first):
                while n < top:
                    shape = [P, C.shape[1], n]
                    cn, sn_ = (v[:, :, n - 1:n].broadcast_to(shape) for v in (C, S))
                    lo, hi = slice(0, n), slice(n, 2 * n)
                    for o, a, b, op in ((w[0][:, :, lo], S[:, :, lo], sn_, ALU.mult),
                                        (w[1][:, :, lo], S[:, :, lo], cn, ALU.mult),
                                        (S[:, :, hi], C[:, :, lo], sn_, ALU.mult),
                                        (C[:, :, hi], C[:, :, lo], cn, ALU.mult),
                                        (C[:, :, hi], C[:, :, hi], w[0][:, :, lo], ALU.subtract),
                                        (S[:, :, hi], S[:, :, hi], w[1][:, :, lo], ALU.add)):
                        tok = add(lambda e, o=o, a=a, b=b, op=op: e.tensor_tensor(o, a, b, op), *first)
                        first = ()
                    n *= 2
                return tok

            DV.add(lambda e: e.tensor_copy(shc[:, :, 0:1], cs.unsqueeze(2)))
            DV.add(lambda e: e.tensor_copy(shs[:, :, 0:1], sn.unsqueeze(2)))
            sh_ready = powers(shc, shs, ws, DV.add, 1, NS)

            def make_table(g):
                C, S = tables[g % 2]
                for dst, src in ((C, shc), (S, shs)):
                    tok = AC.add(lambda e, dst=dst, src=src: e.copy(dst[:, :, 0:NS], src[:, g * G5:(g + 1) * G5, :]),
                                 sh_ready, t_free.get(g - 2))
                t_ready[g] = powers(C, S, wp, lambda f, *w: ML.add(f, ML.last(), *w), NS, P, tok)

            def finish_table(g):
                t_ready[g] = powers(*tables[g % 2], (W1, W2), DV.add, P, T, t_ready[g])

            make_table(0)
            BT = [arena(KD, P) for _ in range(2)]
            for src, dst in ((br, BT[0]), (bi, BT[1])):
                for k in range(0, KD, 4):
                    b = rot()
                    tok = transposes(b, [(j * P, src[:, 4 * (k + j):4 * (k + j) + 4, :].rearrange("p a b -> p (a b)"))
                                         for j in range(4)], bar_ready)
                    bank_free[b] = bt_ready = copy(dst[:, k:k + 4, :], banks[b][:, :].rearrange(
                        "p (a b) -> p a b", a=4), tok, on="D")
            flat = lambda v: v.rearrange("p a b -> p (a b)").rearrange("p (a b) -> p a b", a=4)
            PR = [flat(br), flat(bi)]
            pr_free, p_tok, u_tok, u_bank = [bt_ready, bt_ready], {}, {}, {}
            two = lambda v: v.unsqueeze(1).broadcast_to([P, 2, T])

            def inputs_of(i):
                kt, p0 = i // 4, 32 * (i % 4)
                b = u_bank[i] = rot()
                for j in range(2):
                    u_tok[i] = mm(bank2(b)[:, j, :], BT[j][p0:p0 + 32, kt, :], HT[p0:p0 + 32, kt, :], 0, 1,
                                  bt_ready, bank_free[b], signal=(j == 1))

            def recur(i):
                both = (i, i + 1)
                g = i // G5
                ct, st = ([tables[g % 2][m][:, x % G5, :] for x in both] for m in range(2))
                DV.hold(DV.last())
                DV.lag = 1
                for n, x in enumerate(both):
                    tt(V[n][:, 0:2, :], bank2(u_bank[x]), two(ct[n]), ALU.mult, u_tok[x], t_ready[g])
                for n, x in enumerate(both):
                    bank_free[u_bank[x]] = tt(V[n][:, 2:4, :], bank2(u_bank[x]), two(st[n]), ALU.mult, v_free[n])
                for n in range(2):
                    tt(V[n][:, 0, :], V[n][:, 0, :], V[n][:, 3, :], ALU.add)
                for n in range(2):
                    tt(V[n][:, 1, :], V[n][:, 1, :], V[n][:, 2, :], ALU.subtract)
                for j in range(2):
                    for n, x in enumerate(both):
                        tok = DV.add(lambda e, j=j, n=n, x=x: e.tensor_tensor_scan(
                            V[n][:, 2 + j, :], er[:, x:x + 1].broadcast_to([P, T]), V[n][:, j, :], 0.0,
                            ALU.mult, ALU.add))
                for n, x in enumerate(both):
                    p_tok[x] = [tt(PR[n][:, 0:2, :], V[n][:, 2:4, :], two(ct[n]), ALU.mult, pr_free[n])]
                DV.lag = 0
                for n, x in enumerate(both):
                    v_free[n] = ML.add(lambda e, n=n: e.tensor_tensor(PR[n][:, 2:4, :], V[n][:, 2:4, :], two(st[n]),
                                                                      ALU.mult), tok, pr_free[n])
                    p_tok[x].append(v_free[n])
                t_free[g] = [v_free[1], p_tok[i + 1][0]]

            v_free = [None, None]

            def outputs_of(i):
                kt, p0, yb = i // 4, 32 * (i % 4), (i // 4) % 2
                o = banks[yb][p0:p0 + 32, 0:T]
                pr = PR[i % 2]
                mm(o, cr[:, i, :], pr[:, 0, :], 0, 4, p_tok[i], bank_free[yb])
                mm(o, ci[:, i, :], pr[:, 1, :], 1, 4)
                mm(o, ci[:, i, :], pr[:, 2, :], 2, 4)
                pr_free[i % 2] = mm(o, ncr[:, i, :], pr[:, 3, :], 3, 4, signal=True)

            def finish_outputs(kt, *waits):
                g, yb = MEMG[:, kt, :], kt % 2
                bank_free[yb] = stt(g, HT[:, kt, :], col("s5_d_2", kt), banks[yb][:, 0:T], ALU.mult, ALU.add,
                                    *waits)
                return act(g, g, ACT.Gelu_apprx_tanh, bank_free[yb])

            DV.hold(h_ready)
            inputs_of(0)
            inputs_of(1)
            for i in range(0, NT5, 2):
                if i % G5 == 0:
                    finish_table(i // G5)
                recur(i)
                if i % G5 == 0:
                    if i // G5 + 1 < NT5 // G5:
                        make_table(i // G5 + 1)
                    if i:
                        finish_outputs(i // 4 - 1, y_done)
                if i + 2 < NT5:
                    inputs_of(i + 2)
                    inputs_of(i + 3)
                outputs_of(i)
                outputs_of(i + 1)
                y_done = PE.last()
                if i >= 4 and i % 4 == 0 and early_work:
                    early_work.pop(0)()
            gtok = finish_outputs(KD - 1, y_done)
            AC.hold(PE.last(), ML.last())
            AC.add(lambda e: e.copy(XK, xk))
            tok = AC.add(lambda e: e.copy(XV, xv))
            early[layer] = {"source": None, "keys": [tok], "values": [tok]}
            part_free[m0 + 1 - NSPLIT] = part_free[m0 + 2 - NSPLIT] = tok
            part_free[m0 - NSPLIT] = ML.last()
            for h in range(4):
                bs = [rot(), rot()]
                for m, c0 in enumerate((0, D)):
                    n, w, arrived = take(cols_of(A["s5_w_glu_2"][0], c0 + h * 256, 256), split=False)
                    for t in range(TT):
                        for k in range(KD):
                            tok = mm(bank2(bs[m])[:, t, :], MEMG[:, k, t * P:(t + 1) * P], w[:, k, :], k, KD,
                                     arrived, gtok, bank_free[bs[m]], signal=(k == KD - 1))
                    give(n, tok)
                rt = RT[:, 512 * (h % 2):512 * (h % 2) + 512].rearrange("p (t n) -> p t n", t=TT)
                bank_free[bs[1]] = act(rt, bank2(bs[1]), ACT.Sigmoid, tok, DV.last())
                bank_free[bs[0]] = tt(rt, rt, bank2(bs[0]), ALU.mult, bank_free[bs[1]])
                s = slice(h * 256, (h + 1) * 256)
                x_done = tt(X[:, :, s], X[:, :, s], rt, ALU.add)
            return [x_done, x_done]

        def cross(layer, x_done):
            fence()
            arena_at[0] = 4 * D
            HT, q = arena2(KD, T), arena(KD, T)
            o = MG
            k_, v_ = XK, XV
            arena_at[0] = 14 * D
            if layer in early:
                move = normed("xa_norm_g_2", layer, x_done, HT)
                rest = MG is early[layer]["source"]
                if rest:
                    early_values(layer, 0)
                h_ready = move()
                if rest:
                    early_values(layer, 1)
                ready, vready = early[layer]["keys"], early[layer]["values"]
            else:
                move = normed("xa_norm_g_2", layer, x_done, HT)
                for k in range(KD):
                    m_ready = split_out(MG[:, k, :], MEMN[:, k, :], col("mem_norm_g_2", 8 * layer + k))
                ready = project_heads(k_, A["xa_wkv_2"][layer], 0, 1.0, MG, m_ready)
                vready = project_values(v_, A["xa_wkv_2"][layer], D, MG, m_ready)
                h_ready = move()
            ready += project_heads(q, A["xa_wq_2"][layer], 0, XD ** -0.5, HT, h_ready)
            DV.hold(PE.last())
            AC.hold(PE.last())
            E, ET = arena(XH, TT, T, at=4 * D), [arena(2, T, at=6 * D + 2 * T * i) for i in range(2)]
            sm = arena(4 * XH, at=7 * D)
            s_tok, p_tok, et_free = {}, {}, [None, None]
            for h in range(XH):
                for t in range(TT):
                    for c in range(2):
                        s_tok[h] = mm(banks[h][:, t * T:(t + 1) * T], q[:, 2 * h + c, t * P:(t + 1) * P],
                                      k_[:, 2 * h + c, :], c, 2, ready, bank_free[h], signal=(c == 1))
            m_tok = {}
            cs = [sm[:, 4 * h:4 * h + 4] for h in range(XH)]
            for h in range(XH):
                m_tok[h] = DV.add(lambda e, h=h: e.tensor_reduce(cs[h][:, 0:2], bank2(h), AX.X, ALU.max,
                                                                 negate=True), s_tok[h])
            for h in range(XH):
                for t in range(TT):
                    t2 = act(E[:, h, t, :], bank2(h)[:, t, :], ACT.Exp, m_tok[h], bias=cs[h][:, t:t + 1],
                             acc=cs[h][:, 2 + t:3 + t])
                bank_free[h] = t2
                DV.add(lambda e, h=h: e.reciprocal(cs[h][:, 2:4], cs[h][:, 2:4]), t2)
                p_tok[h] = tt(E[:, h, :, :], E[:, h, :, :], cs[h][:, 2:4].unsqueeze(2).broadcast_to([P, TT, T]),
                              ALU.mult)
            et_tok = {}

            def turn_p(h):
                b = rot()
                tok = transposes(b, [((m * 2 + t) * P, E[:, h, t, m * P:(m + 1) * P])
                                     for m in range(2) for t in range(TT)], p_tok[h])
                bank_free[b] = et_tok[h] = copy(ET[h % 2], bank2(b), tok, et_free[h % 2], on="A")

            turn_p(0)
            for h in range(XH):
                if h + 1 < XH:
                    turn_p(h + 1)
                b = rot()
                for d in range(2):
                    for m in range(2):
                        t2 = mm(bank2(b)[:, d, :], v_[:, m, h * XD + d * P:h * XD + (d + 1) * P], ET[h % 2][:, m, :],
                                m, 2, et_tok[h], vready, bank_free[b], signal=(m == 1))
                et_free[h % 2] = t2
                bank_free[b] = split_out(o[:, 2 * h:2 * h + 2, :], bank2(b), 1.0, t2)
            out_product(A["xa_wo_2"][layer], o, DV.last())
            return add_acc()

        def ffn(layer, x_done):
            fence()
            HT = arena2(KD, T)
            h_ready = normed("ffn_norm_g_2", layer, x_done, HT)()
            hids = [arena2(4, T) for _ in range(3)]
            raw = [arena(2, T) for _ in range(2)]
            hid_free = [None] * 3
            U = [arena(2, 2 + T) for _ in range(4)]
            CV = [arena(2, T) for _ in range(2)]
            for u in U:
                DV.add(lambda e, u=u: e.memset(u[:, :, 0:2], 0.0))
            w_up, w_dn = A["ffn_w_up_2"][layer], A["ffn_w_down_2"][layer]
            u_free, cv_free, hid_tok = [None] * 4, [None] * 2, {}

            def conv(dst, u, c0, *waits):
                w = lambda j, n: col("ffn_conv_w_2", (layer * 3 + j) * 2 * KF + c0 + n)
                DV.lag = 1
                for n in range(2):
                    ts(dst[:, n, :], u[:, n, 2:2 + T], w(2, n), col("ffn_conv_b_2", layer * 2 * KF + c0 + n),
                       ALU.mult, ALU.add, *waits)
                for j in (1, 0):
                    for n in range(2):
                        tok = stt(dst[:, n, :], u[:, n, j:j + T], w(j, n), dst[:, n, :], ALU.mult, ALU.add)
                DV.lag = 0
                return tok

            def up(s):
                i, turn_ = s % 2, (s // 2) % 3
                hid = hids[turn_][:, 2 * i:2 * i + 2, :]

                def evac(u, dst, c0, cv):
                    def f(_, b, tok):
                        t1 = copy(U[u][:, :, 2:2 + T], bank2(b), tok, u_free[u], on="A")
                        u_free[u] = conv(dst, U[u], c0, t1, cv)
                        return t1
                    return f

                n, wg, arrived = take(cols_of(w_up, FF + s * 256, 256))
                give(n, to_channels(wg, HT, KD, 2, evac(2 * i + 1, CV[i], KF + 2 * s, None), [arrived, h_ready]))
                t3 = act(CV[i], CV[i], ACT.Silu, u_free[2 * i + 1])
                n, wv, arrived = take(cols_of(w_up, s * 256, 256))
                give(n, to_channels(wv, HT, KD, 2, evac(2 * i, raw[i], 2 * s, None), [arrived]))
                tok = tt(raw[i], raw[i], CV[i], ALU.mult, t3)
                hid_tok[s] = split_out(hid, raw[i], 1.0, tok, hid_free[turn_])

            def down(s):
                turn_ = (s // 2) % 3
                n, w, arrived = take(rows_of(w_dn, 2 * s, 2))
                hid_free[turn_] = to_tokens(w, hids[turn_], 2, s == 0, s == KF // 2 - 1, [arrived, hid_tok[s]],
                                            k0=2 * (s % 2))
                give(n, hid_free[turn_])

            for s in range(KF // 2):
                up(s)
                if s >= 2:
                    down(s - 2)
            if (layer + 1) % 3 == 0 and layer + 1 < DEPTH2:
                memory_parts(layer + 1)
            down(KF // 2 - 2)
            down(KF // 2 - 1)
            return add_acc()

        fence()
        x_done = mlstm()
        x_done = moe(0, x_done)
        x_done = moba(x_done)
        x_done = moe(1, x_done)
        rowg_read[0] = DV.last()
        for layer in range(DEPTH2):
            if layer % 3 == 0:
                x_done = pool_mixer(layer, layer // 3, x_done)
            elif layer % 3 == 1:
                x_done = stick_breaking(layer, x_done)
            else:
                x_done = s5(layer, x_done)
            x_done = cross(layer, x_done)
            x_done = ffn(layer, x_done)
        g_ready = small(ROWG[:, :], row(A["final_norm_g_2"]), rowg_read[0])
        x_done = rms(X, X, g_ready, x_done)
        done = small(out.rearrange("(t p) n -> p t n", p=P), X[:, :, :], DV.last())
        ML.hold(done)
        if plan is None:
            return units

        block = ctx.enter_context(nc.Block())

        @block.sync
        def _(eng):
            LD.run(eng)

        @block.gpsimd
        def _(eng):
            ML.run(eng)

        @block.tensor
        def _(eng):
            PE.run(eng)

        @block.vector
        def _(eng):
            DV.run(eng)

        @block.scalar
        def _(eng):
            AC.run(eng)


def host_layout(inputs, np):
    f = lambda name: np.asarray(inputs[name])
    cols = np.zeros((P, NCOLS), np.float32)
    for name, n in COLS:
        if name in ("bi", "bf"):
            b = f("a_b_if")[0]
            cols[0:MH, COL_AT[name]] = b[0:MH] if name == "bi" else b[MH:]
        else:
            cols[:, COL_AT[name]:COL_AT[name] + n] = f(name).reshape(n, P).T
    states = lambda a: a.reshape(NT5, 2, SP).transpose(1, 2, 0).reshape(P, NT5)

    def blocks(a):
        o = np.zeros((2, SP, NT5, 2, SC), np.float32)
        for g in range(2):
            o[g, :, :, g, :] = a[g::2].transpose(1, 0, 2)
        return o.reshape(P, NT5, 2 * SC)

    out = {
        "consts": constants(), "cols": cols,
        "x": f("x")[0], "xT": f("x")[0].T, "mem_2": f("mem_2")[0],
        "s5_par": np.stack([states(f("s5_a_re_2")[0]), states(f("s5_a_im_2")[0]),
                            states(np.broadcast_to(f("s5_log_dt_2")[0][:, None], (SG, SP)))], axis=1),
        "s5_b_re": blocks(f("s5_b_re_2")[0]), "s5_b_im": blocks(f("s5_b_im_2")[0]),
        "s5_c_re": blocks(f("s5_c_re_2")[0].transpose(0, 2, 1)),
        "s5_c_im": blocks(f("s5_c_im_2")[0].transpose(0, 2, 1)),
        "a_w_in": f("a_w_in")[0], "a_wq": f("a_wq")[0], "a_wk": f("a_wk")[0], "a_wv": f("a_wv")[0],
        "a_w_if": f("a_w_if")[0], "a_w_out": f("a_w_out")[0], "b_wq": f("b_wq")[0], "b_wo": f("b_wo")[0],
    }
    for name in ("w_ada", "b_ada", "ln_g", "ln_b", "b_w_kv", "moe_w_router", "moe_b_router", "moe_w_gate",
                 "moe_w_up", "moe_w_down", "pool_w_2", "pool_scale_2", "sb_w_qkv_2", "sb_w_o_2", "s5_w_glu_2",
                 "xa_wq_2", "xa_wkv_2", "xa_wo_2", "ffn_w_up_2", "ffn_w_down_2", "final_norm_g_2",
                 "mix_norm_g_2", "xa_norm_g_2", "ffn_norm_g_2"):
        out[name] = f(name)
    return out


def kernel(**inputs):
    import concourse.bacc as bacc
    from concourse.bass_utils import run_bass_kernel_spmd

    arrays = {f"in_{name}": np.ascontiguousarray(a) for name, a in host_layout(inputs, np).items()}

    def program(plan):
        nc = bacc.Bacc("TRN2", target_bir_lowering=False, num_devices=1)
        args = {name[3:]: nc.dram_tensor(name, a.shape, mybir.dt.from_np(a.dtype), kind="ExternalInput").ap()
                for name, a in arrays.items()}
        out = nc.dram_tensor("out_0", (T, D), F32, kind="ExternalOutput").ap()
        return nc, build(nc, args, out, plan)

    _, units = program(None)
    nc, _ = program(units)
    r = run_bass_kernel_spmd(nc, [arrays], core_ids=[0])
    return r.results[0]["out_0"].reshape(1, T, D)
```
